# Optimizing a Trainium2 kernel written in Bass

```python
import jax, jax.numpy as jnp
from jax import lax
import numpy as np

D_MODEL = 1024
BATCH = 1
SEQ = 256
DEPTH = 1

CHUNK = 64

D_POOL = D_MODEL // 2
POOL_WINDOWS = (2, 4, 8, 16)
POOL_GROUPS = len(POOL_WINDOWS)
POOL_GROUP_DIM = D_POOL // POOL_GROUPS

D_CONV = D_MODEL // 2
CONV_WIDTH = 3

D_IN = D_POOL + 3 * D_CONV + 2 * D_MODEL

N_KEYS = 128
N_EXPERTS = N_KEYS * N_KEYS
PEER_HEADS = 8
PEER_QUERY_DIM = 256
PEER_HALF = PEER_QUERY_DIM // 2
PEER_TOPK = 16
PEER_TOKEN_BLOCK = 128

RMS_EPS = 1e-6


def rmsnorm(x, g):
    xf = x.astype(jnp.float32)
    y = xf * lax.rsqrt(jnp.mean(xf * xf, axis=-1, keepdims=True) + RMS_EPS)
    return (y * g.astype(jnp.float32)).astype(x.dtype)

def pool_mixer(u, group_w, scale):
    S_ = u.shape[1]
    uf = u.astype(jnp.float32)
    csum = jnp.cumsum(uf, axis=1)
    pos = jnp.arange(S_)
    outs = []
    for g, w in enumerate(POOL_WINDOWS):
        sl = slice(g * POOL_GROUP_DIM, (g + 1) * POOL_GROUP_DIM)
        c = csum[:, :, sl]
        c_shift = jnp.pad(c[:, :S_ - w, :], ((0, 0), (w, 0), (0, 0)))
        cnt = jnp.minimum(pos + 1, w).astype(jnp.float32)[None, :, None]
        outs.append((c - c_shift) / cnt - uf[:, :, sl])
    p = jnp.stack(outs, axis=2).astype(u.dtype)
    p = jnp.einsum('bsgc,gcd->bsgd', p, group_w)
    return p.reshape(u.shape) * scale

def short_conv_mixer(c_gate, b_gate, v, conv_w):
    S_ = v.shape[1]
    u = c_gate * v
    up = jnp.pad(u, ((0, 0), (CONV_WIDTH - 1, 0), (0, 0)))
    y = up[:, 0:S_, :] * conv_w[0]
    for k in range(1, CONV_WIDTH):
        y = y + up[:, k:k + S_, :] * conv_w[k]
    return b_gate * y

def peer_ffn(h, w_q, sub_keys, expert_u, expert_v):
    B_, S_, D_ = h.shape
    hb_all = h.reshape(B_ * S_ // PEER_TOKEN_BLOCK, PEER_TOKEN_BLOCK, D_)

    def block(hb):
        q = (hb @ w_q).reshape(PEER_TOKEN_BLOCK, PEER_HEADS, 2, PEER_HALF)
        s = jnp.einsum('thpc,hpkc->thpk', q, sub_keys).astype(jnp.float32)
        top_s, top_i = lax.top_k(s, PEER_TOPK)
        cand_s = top_s[:, :, 0, :, None] + top_s[:, :, 1, None, :]
        cand_i = top_i[:, :, 0, :, None] * N_KEYS + top_i[:, :, 1, None, :]
        cand_s = cand_s.reshape(PEER_TOKEN_BLOCK, PEER_HEADS, PEER_TOPK * PEER_TOPK)
        cand_i = cand_i.reshape(PEER_TOKEN_BLOCK, PEER_HEADS, PEER_TOPK * PEER_TOPK)
        fin_s, fin_pos = lax.top_k(cand_s, PEER_TOPK)
        idx = jnp.take_along_axis(cand_i, fin_pos, axis=-1)
        gates = jax.nn.softmax(fin_s, axis=-1)
        u = expert_u[idx]
        act = jax.nn.gelu(jnp.einsum('thkd,td->thk', u, hb).astype(jnp.float32), approximate=False)
        wts = (gates * act).astype(hb.dtype)
        return jnp.einsum('thk,thkd->td', wts, expert_v[idx])

    out = lax.map(block, hb_all)
    return out.reshape(B_, S_, D_)

def first_inputs(seed: int = 0) -> dict:
    key = jax.random.key(seed)
    ks = jax.random.split(key, 16)
    f32 = jnp.float32
    nrm = lambda k, shape, s: jax.random.normal(k, shape, f32) * s
    L = DEPTH
    return {
        "x": nrm(ks[0], (BATCH, SEQ, D_MODEL), 1.0),
        "g_mix": 1.0 + nrm(ks[1], (L, D_MODEL), 0.02),
        "w_in": nrm(ks[2], (L, D_MODEL, D_IN), D_MODEL ** -0.5),
        "pool_group_w": nrm(ks[3], (L, POOL_GROUPS, POOL_GROUP_DIM, POOL_GROUP_DIM), POOL_GROUP_DIM ** -0.5),
        "pool_scale": 1.0 + nrm(ks[4], (L, D_POOL), 0.02),
        "conv_w": nrm(ks[5], (L, CONV_WIDTH, D_CONV), CONV_WIDTH ** -0.5),
        "w_branch_pool": nrm(ks[6], (L, D_POOL, D_MODEL), D_POOL ** -0.5),
        "w_branch_conv": nrm(ks[7], (L, D_CONV, D_MODEL), D_CONV ** -0.5),
        "w_out": nrm(ks[8], (L, D_MODEL, D_MODEL), D_MODEL ** -0.5),
        "g_ffn": 1.0 + nrm(ks[9], (L, D_MODEL), 0.02),
        "w_q": nrm(ks[10], (L, D_MODEL, PEER_HEADS * PEER_QUERY_DIM), D_MODEL ** -0.5),
        "sub_keys": nrm(ks[11], (L, PEER_HEADS, 2, N_KEYS, PEER_HALF), PEER_HALF ** -0.5),
        "expert_u": nrm(ks[12], (L, N_EXPERTS, D_MODEL), D_MODEL ** -0.5),
        "expert_v": nrm(ks[13], (L, N_EXPERTS, D_MODEL), PEER_HEADS ** -0.5),
        "g_final": 1.0 + nrm(ks[14], (D_MODEL,), 0.02),
    }

def first_block(x, g_mix, w_in, pool_group_w, pool_scale, conv_w, w_branch_pool, w_branch_conv,
              w_out, g_ffn, w_q, sub_keys, expert_u, expert_v, g_final):
    for l in range(DEPTH):
        h = rmsnorm(x, g_mix[l])
        z = h @ w_in[l]
        o1 = D_POOL
        o2 = o1 + D_CONV
        o3 = o2 + D_CONV
        o4 = o3 + D_CONV
        o5 = o4 + D_MODEL
        z_pool, z_c, z_b, z_v = z[..., :o1], z[..., o1:o2], z[..., o2:o3], z[..., o3:o4]
        gate_a, gate_b = z[..., o4:o5], z[..., o5:]
        a = pool_mixer(z_pool, pool_group_w[l], pool_scale[l]) @ w_branch_pool[l]
        b = short_conv_mixer(z_c, z_b, z_v, conv_w[l]) @ w_branch_conv[l]
        m = jax.nn.sigmoid(gate_a) * a + jax.nn.sigmoid(gate_b) * b
        x = x + m @ w_out[l]
        h2 = rmsnorm(x, g_ffn[l])
        x = x + peer_ffn(h2, w_q[l], sub_keys[l], expert_u[l], expert_v[l])
    return rmsnorm(x, g_final)


HEAD_DIM = 64
MIX_WIDTH = D_MODEL
RWKV_WIDTH = MIX_WIDTH // 2
MOBA_WIDTH = MIX_WIDTH - RWKV_WIDTH
RWKV_HEADS = RWKV_WIDTH // HEAD_DIM
MOBA_HEADS = MOBA_WIDTH // HEAD_DIM
DECAY_LORA = max(32, int(round(1.8 * D_MODEL ** 0.5 / 32)) * 32)
AAA_LORA = max(32, int(round(1.8 * D_MODEL ** 0.5 / 32)) * 32)
GATE_LORA = max(32, int(round(0.6 * D_MODEL ** 0.8 / 32)) * 32)
RWKV_LN_EPS = 64e-5
RWKV_PROJ = 3 * RWKV_WIDTH + DECAY_LORA + AAA_LORA + GATE_LORA
MOBA_PROJ = 3 * MOBA_WIDTH
IN_COLS = RWKV_PROJ + MOBA_PROJ
MOBA_BLOCK = 256
MOBA_TOPK = 3
MOBA_QUERY_CHUNK = 16
N_EXPERTS_2 = 32
TOP_K = 4
D_FF = D_MODEL
SWIGLU_LIMIT = 7.0
SWIGLU_ALPHA = 1.702
EXPERT_ROWS = 128
NORM_EPS = 1e-6


def rms_norm(x, g):
    xf = x.astype(jnp.float32)
    y = xf * lax.rsqrt(jnp.mean(xf * xf, axis=-1, keepdims=True) + NORM_EPS)
    return (y * g.astype(jnp.float32)).astype(x.dtype)

def token_shift(p):
    return jnp.pad(p, ((0, 0), (1, 0), (0, 0)))[:, :-1]

def rwkv7_time_mix(p, mu, w0, w_up, a0, a_up, g_up, k_k, k_a, r_k, ln_g, ln_b):
    B, S, _ = p.shape
    H, N, W = RWKV_HEADS, HEAD_DIM, RWKV_WIDTH
    f32 = jnp.float32
    p = p + (token_shift(p) - p) * mu
    r, k, v, xw, xa, xg = jnp.split(
        p, [W, 2 * W, 3 * W, 3 * W + DECAY_LORA, 3 * W + DECAY_LORA + AAA_LORA], axis=-1)
    w_log = -jax.nn.softplus(-(w0 + jnp.tanh(xw) @ w_up)) - 0.5
    decay = jnp.exp(-jnp.exp(w_log.astype(f32)))
    a = jax.nn.sigmoid(a0 + xa @ a_up)
    g = jax.nn.sigmoid(xg) @ g_up
    heads = lambda t: t.reshape(B, S, H, N).astype(f32)
    kk = heads(k * k_k)
    kk = kk / jnp.maximum(jnp.linalg.norm(kk, axis=-1, keepdims=True), 1e-12)
    k = k * (1.0 + (a - 1.0) * k_a)
    r_h, k_h, v_h, w_h, a_h = heads(r), heads(k), heads(v), heads(decay), heads(a)

    def step(state, inp):
        r_t, w_t, k_t, v_t, kk_t, a_t = inp
        sa = jnp.einsum('bhij,bhj->bhi', state, -kk_t)
        state = (state * w_t[:, :, None, :]
                 + sa[..., None] * (kk_t * a_t)[:, :, None, :]
                 + v_t[..., None] * k_t[:, :, None, :])
        y_t = jnp.einsum('bhij,bhj->bhi', state, r_t)
        return state, y_t

    sf = lambda t: jnp.moveaxis(t, 1, 0)
    state0 = jnp.zeros((B, H, N, N), f32)
    _, y = lax.scan(step, state0, (sf(r_h), sf(w_h), sf(k_h), sf(v_h), sf(kk), sf(a_h)))
    y = jnp.moveaxis(y, 0, 1)
    mean = jnp.mean(y, axis=-1, keepdims=True)
    var = jnp.mean(jnp.square(y - mean), axis=-1, keepdims=True)
    y = ((y - mean) * lax.rsqrt(var + RWKV_LN_EPS)).reshape(B, S, W) * ln_g + ln_b
    bonus = jnp.sum(r_h * k_h * r_k, axis=-1, keepdims=True) * v_h
    y = (y + bonus.reshape(B, S, W)) * g
    return y.astype(p.dtype)

def moba_attention(p, q_norm_g, k_norm_g):
    B, S, _ = p.shape
    H, N, BLK, QC = MOBA_HEADS, HEAD_DIM, MOBA_BLOCK, MOBA_QUERY_CHUNK
    f32 = jnp.float32
    to_heads = lambda t: t.reshape(B, S, H, N).transpose(0, 2, 1, 3)
    q, k, v = [to_heads(t) for t in jnp.split(p, 3, axis=-1)]
    q = rms_norm(q, q_norm_g)
    k = rms_norm(k, k_norm_g)
    NB = -(-S // BLK)
    n_sel = min(MOBA_TOPK, NB)
    pad = NB * BLK - S
    kb = jnp.pad(k, ((0, 0), (0, 0), (0, pad), (0, 0))).reshape(B, H, NB, BLK, N)
    vb = jnp.pad(v, ((0, 0), (0, 0), (0, pad), (0, 0))).reshape(B, H, NB, BLK, N)
    kmean = jnp.mean(kb.astype(f32), axis=3)
    slopes = jnp.exp2(-8.0 * (jnp.arange(H, dtype=f32) + 1.0) / H)
    scale = HEAD_DIM ** -0.5
    bi = jnp.arange(B)[:, None, None, None]
    hi = jnp.arange(H)[None, :, None, None]
    n_chunks = S // QC
    q_chunks = jnp.moveaxis(q.reshape(B, H, n_chunks, QC, N), 2, 0)

    def attend_chunk(args):
        qi, ci = args
        t0 = ci * QC
        j = t0 // BLK
        tq = t0 + jnp.arange(QC)
        gate = jnp.einsum('bhqd,bhnd->bhqn', qi.astype(f32), kmean)
        gate = jnp.where(jnp.arange(NB) < j, gate, -jnp.inf)
        _, sel = lax.top_k(gate, n_sel)
        ksel = kb[bi, hi, sel]
        vsel = vb[bi, hi, sel]
        kpos_sel = sel[..., None] * BLK + jnp.arange(BLK)
        s_sel = (jnp.einsum('bhqd,bhqmkd->bhqmk', qi, ksel).astype(f32) * scale
                 - slopes[:, None, None, None] * (tq[:, None, None] - kpos_sel))
        s_sel = jnp.where((jnp.arange(n_sel) < j)[:, None], s_sel, -jnp.inf)
        k_own = lax.dynamic_index_in_dim(kb, j, axis=2, keepdims=False)
        v_own = lax.dynamic_index_in_dim(vb, j, axis=2, keepdims=False)
        kpos_own = j * BLK + jnp.arange(BLK)
        s_own = (jnp.einsum('bhqd,bhkd->bhqk', qi, k_own).astype(f32) * scale
                 - slopes[:, None, None] * (tq[:, None] - kpos_own[None, :]))
        s_own = jnp.where(kpos_own[None, :] <= tq[:, None], s_own, -jnp.inf)
        s = jnp.concatenate([s_sel.reshape(B, H, QC, n_sel * BLK), s_own], axis=-1)
        prob = jax.nn.softmax(s, axis=-1)
        p_sel = prob[..., :n_sel * BLK].reshape(B, H, QC, n_sel, BLK)
        p_own = prob[..., n_sel * BLK:]
        out = (jnp.einsum('bhqmk,bhqmkd->bhqd', p_sel, vsel)
               + jnp.einsum('bhqk,bhkd->bhqd', p_own, v_own))
        return out.astype(qi.dtype)

    out = lax.map(attend_chunk, (q_chunks, jnp.arange(n_chunks, dtype=jnp.int32)))
    out = jnp.moveaxis(out, 0, 2).reshape(B, H, S, N)
    return out.transpose(0, 2, 1, 3).reshape(B, S, MOBA_WIDTH)

def moe_ffn(h, w_router, b_router, w_gate_up, b_gate_up, w_down, b_down):
    T, D = h.shape
    logits = (h @ w_router + b_router).astype(jnp.float32)
    top_val, top_idx = lax.top_k(logits, TOP_K)
    weights = jax.nn.softmax(top_val, axis=-1)
    M = T * TOP_K
    slot_expert = top_idx.reshape(M)
    slot_token = jnp.arange(M, dtype=jnp.int32) // TOP_K
    slot_weight = weights.reshape(M)
    order = jnp.argsort(slot_expert)
    e_sorted = slot_expert[order]
    counts = jnp.bincount(slot_expert, length=N_EXPERTS_2)
    padded = (counts + EXPERT_ROWS - 1) // EXPERT_ROWS * EXPERT_ROWS
    pad_end = jnp.cumsum(padded)
    pad_start = pad_end - padded
    start = jnp.cumsum(counts) - counts
    dest = pad_start[e_sorted] + jnp.arange(M) - start[e_sorted]
    P = M + N_EXPERTS_2 * EXPERT_ROWS
    n_blocks = P // EXPERT_ROWS
    buf_token = jnp.zeros((P,), jnp.int32).at[dest].set(slot_token[order])
    buf_weight = jnp.zeros((P,), jnp.float32).at[dest].set(slot_weight[order])
    blk_expert = jnp.minimum(
        jnp.searchsorted(pad_end, jnp.arange(n_blocks) * EXPERT_ROWS, side='right'), N_EXPERTS_2 - 1)

    def expert_block(args):
        tok, e = args
        xb = h[tok]
        gu = xb @ w_gate_up[e] + b_gate_up[e]
        gate = jnp.minimum(gu[:, :D_FF], SWIGLU_LIMIT)
        up = jnp.clip(gu[:, D_FF:], -SWIGLU_LIMIT, SWIGLU_LIMIT)
        act = (up + 1.0) * gate * jax.nn.sigmoid(SWIGLU_ALPHA * gate)
        return act @ w_down[e] + b_down[e]

    y = lax.map(expert_block, (buf_token.reshape(n_blocks, EXPERT_ROWS), blk_expert)).reshape(P, D)
    return jax.ops.segment_sum(y * buf_weight[:, None], buf_token, num_segments=T)

def hybrid_layer(x, c, w_ada, b_ada, norm1_g, w_in, rwkv_mu, rwkv_w0, rwkv_w_up, rwkv_a0,
                 rwkv_a_up, rwkv_g_up, rwkv_k_k, rwkv_k_a, rwkv_r_k, rwkv_ln_g, rwkv_ln_b,
                 q_norm_g, k_norm_g, w_out, norm2_g, w_router, b_router, w_gate_up,
                 b_gate_up, w_down, b_down):
    B, S, D = x.shape
    mods = jax.nn.silu(c) @ w_ada + b_ada
    shift1, scale1, gate1, shift2, scale2, gate2 = jnp.split(mods[:, None, :], 6, axis=-1)
    h = rms_norm(x, norm1_g) * (1.0 + scale1) + shift1
    proj = h @ w_in
    y_rwkv = rwkv7_time_mix(proj[..., :RWKV_PROJ], rwkv_mu, rwkv_w0, rwkv_w_up, rwkv_a0,
                            rwkv_a_up, rwkv_g_up, rwkv_k_k, rwkv_k_a, rwkv_r_k,
                            rwkv_ln_g, rwkv_ln_b)
    y_moba = moba_attention(proj[..., RWKV_PROJ:], q_norm_g, k_norm_g)
    x = x + gate1 * (jnp.concatenate([y_rwkv, y_moba], axis=-1) @ w_out)
    h = rms_norm(x, norm2_g) * (1.0 + scale2) + shift2
    y = moe_ffn(h.reshape(B * S, D), w_router, b_router, w_gate_up, b_gate_up, w_down, b_down)
    return x + gate2 * y.reshape(B, S, D).astype(x.dtype)

def second_inputs(seed: int = 0) -> dict:
    key = jax.random.key(seed)
    ks = jax.random.split(key, 27)
    nrm = lambda k, shape, s: jax.random.normal(k, shape, jnp.float32) * s
    L = DEPTH
    return {
        'x': nrm(ks[0], (BATCH, SEQ, D_MODEL), 1.0),
        'c': nrm(ks[1], (BATCH, D_MODEL), 1.0),
        'w_ada': nrm(ks[2], (L, D_MODEL, 6 * D_MODEL), 0.5 * D_MODEL ** -0.5),
        'b_ada': nrm(ks[3], (L, 6 * D_MODEL), 0.02),
        'norm1_g': 1.0 + nrm(ks[4], (L, D_MODEL), 0.05),
        'w_in': nrm(ks[5], (L, D_MODEL, IN_COLS), D_MODEL ** -0.5),
        'rwkv_mu': jax.random.uniform(ks[6], (L, RWKV_PROJ), jnp.float32),
        'rwkv_w0': jax.random.uniform(ks[7], (L, RWKV_WIDTH), jnp.float32, minval=-6.0, maxval=0.0),
        'rwkv_w_up': nrm(ks[8], (L, DECAY_LORA, RWKV_WIDTH), 0.3 * DECAY_LORA ** -0.5),
        'rwkv_a0': nrm(ks[9], (L, RWKV_WIDTH), 0.5),
        'rwkv_a_up': nrm(ks[10], (L, AAA_LORA, RWKV_WIDTH), 0.5 * AAA_LORA ** -0.5),
        'rwkv_g_up': nrm(ks[11], (L, GATE_LORA, RWKV_WIDTH), GATE_LORA ** -0.5),
        'rwkv_k_k': 0.85 + nrm(ks[12], (L, RWKV_WIDTH), 0.05),
        'rwkv_k_a': 1.0 + nrm(ks[13], (L, RWKV_WIDTH), 0.05),
        'rwkv_r_k': nrm(ks[14], (L, RWKV_HEADS, HEAD_DIM), 0.1),
        'rwkv_ln_g': 1.0 + nrm(ks[15], (L, RWKV_WIDTH), 0.05),
        'rwkv_ln_b': nrm(ks[16], (L, RWKV_WIDTH), 0.02),
        'q_norm_g': 1.0 + nrm(ks[17], (L, HEAD_DIM), 0.05),
        'k_norm_g': 1.0 + nrm(ks[18], (L, HEAD_DIM), 0.05),
        'w_out': nrm(ks[19], (L, MIX_WIDTH, D_MODEL), MIX_WIDTH ** -0.5),
        'norm2_g': 1.0 + nrm(ks[20], (L, D_MODEL), 0.05),
        'w_router': nrm(ks[21], (L, D_MODEL, N_EXPERTS_2), D_MODEL ** -0.5),
        'b_router': nrm(ks[22], (L, N_EXPERTS_2), 0.01),
        'w_gate_up': nrm(ks[23], (L, N_EXPERTS_2, D_MODEL, 2 * D_FF), D_MODEL ** -0.5),
        'b_gate_up': nrm(ks[24], (L, N_EXPERTS_2, 2 * D_FF), 0.01),
        'w_down': nrm(ks[25], (L, N_EXPERTS_2, D_FF, D_MODEL), D_FF ** -0.5),
        'b_down': nrm(ks[26], (L, N_EXPERTS_2, D_MODEL), 0.01),
    }

def second_block(x, c, w_ada, b_ada, norm1_g, w_in, rwkv_mu, rwkv_w0, rwkv_w_up, rwkv_a0,
              rwkv_a_up, rwkv_g_up, rwkv_k_k, rwkv_k_a, rwkv_r_k, rwkv_ln_g, rwkv_ln_b,
              q_norm_g, k_norm_g, w_out, norm2_g, w_router, b_router, w_gate_up,
              b_gate_up, w_down, b_down):
    for l in range(DEPTH):
        x = hybrid_layer(x, c, w_ada[l], b_ada[l], norm1_g[l], w_in[l], rwkv_mu[l], rwkv_w0[l],
                         rwkv_w_up[l], rwkv_a0[l], rwkv_a_up[l], rwkv_g_up[l], rwkv_k_k[l],
                         rwkv_k_a[l], rwkv_r_k[l], rwkv_ln_g[l], rwkv_ln_b[l], q_norm_g[l],
                         k_norm_g[l], w_out[l], norm2_g[l], w_router[l], b_router[l],
                         w_gate_up[l], b_gate_up[l], w_down[l], b_down[l])
    return x


def setup_inputs(seed=0):
    out = dict(first_inputs(seed))
    for name, value in second_inputs(seed + 1).items():
        if name != "x":
            out[name + "_2"] = value
    return out


def reference(
    x, g_mix, w_in, pool_group_w, pool_scale, conv_w, w_branch_pool, w_branch_conv, w_out,
    g_ffn, w_q, sub_keys, expert_u, expert_v, g_final, c_2, w_ada_2, b_ada_2, norm1_g_2, w_in_2,
    rwkv_mu_2, rwkv_w0_2, rwkv_w_up_2, rwkv_a0_2, rwkv_a_up_2, rwkv_g_up_2, rwkv_k_k_2,
    rwkv_k_a_2, rwkv_r_k_2, rwkv_ln_g_2, rwkv_ln_b_2, q_norm_g_2, k_norm_g_2, w_out_2,
    norm2_g_2, w_router_2, b_router_2, w_gate_up_2, b_gate_up_2, w_down_2, b_down_2,
):
    x = first_block(
        x, g_mix, w_in, pool_group_w, pool_scale, conv_w, w_branch_pool, w_branch_conv, w_out,
        g_ffn, w_q, sub_keys, expert_u, expert_v, g_final,
    )
    return second_block(
        x, c_2, w_ada_2, b_ada_2, norm1_g_2, w_in_2, rwkv_mu_2, rwkv_w0_2, rwkv_w_up_2,
        rwkv_a0_2, rwkv_a_up_2, rwkv_g_up_2, rwkv_k_k_2, rwkv_k_a_2, rwkv_r_k_2, rwkv_ln_g_2,
        rwkv_ln_b_2, q_norm_g_2, k_norm_g_2, w_out_2, norm2_g_2, w_router_2, b_router_2,
        w_gate_up_2, b_gate_up_2, w_down_2, b_down_2,
    )


_drawn_inputs = setup_inputs


def setup_inputs(seed=0):
    import zlib

    import numpy as np

    out = dict(_drawn_inputs(seed))
    spreads = {}
    factors = {'pool_scale': 2.718,
     'norm1_g_2': 3.817,
     'rwkv_w_up_2': 8.0,
     'rwkv_k_k_2': 36.216,
     'rwkv_k_a_2': 3.604,
     'rwkv_ln_g_2': 38.848,
     'rwkv_ln_b_2': 64.0,
     'q_norm_g_2': 6.982,
     'k_norm_g_2': 7.706,
     'b_router_2': 45.304,
     'b_gate_up_2': 64.0,
     'b_down_2': 190.288,
     'norm2_g_2': 8.0}
    for name, (base, spread) in spreads.items():
        noise = np.random.default_rng([zlib.crc32(name.encode()), seed]).standard_normal(out[name].shape)
        drawn = base * np.exp(spread * noise) if base else spread * noise
        out[name] = __import__('jax').numpy.asarray(drawn.astype(out[name].dtype))
    for name, factor in factors.items():
        out[name] = (out[name] * factor).astype(out[name].dtype)
    return out
```

```python
from contextlib import ExitStack

import numpy as np

import concourse.bass as bass
from concourse import mybir

F32 = mybir.dt.float32
U32 = mybir.dt.uint32
I32 = mybir.dt.int32
ALU = mybir.AluOpType
ACT = mybir.ActivationFunctionType
AX_X = mybir.AxisListType.X

P = 128
D = 1024
T = 256
TT = T // P
KD = D // P
CW = 256
CHUNK = KD * CW
SLOTS = 12

D_IN = 4096
POOL_G = 4
HEADS = 8
HP = 2 * HEADS
NK = 128
TOPK = 16
HK = HEADS * TOPK
NEXP_PEER = NK * NK
EPS = 1e-6
GATHER_SLOTS = 4

W2 = 512
RW = 1824
MB = 1536
RWP = 2048
NH = 8
HD = 64
CL = 32
NC = T // CL
LN_EPS = 64e-5
NE = 32
TOPE = 4
CAP = 64
PASSES = T // CAP
FF = 1024
LIMIT = 7.0
ALPHA = 1.702
NEG = -1.0e30
LOWEST = -3.0e38

N_Z = D_IN // CW
N_BR = 4
N_O1 = D // CW
N_Q = 2048 // CW
N_KEYS = 1
N_ADA = 6 * D // CW
N_MB = MB // CW
N_RW = RWP // CW
N_O2 = D // CW
C_Z = 0
C_BR = C_Z + N_Z
C_O1 = C_BR + N_BR
C_Q = C_O1 + N_O1
C_KEYS = C_Q + N_Q
C_ADA = C_KEYS + N_KEYS
C_MB = C_ADA + N_ADA
C_RW = C_MB + N_MB
C_O2 = C_RW + N_RW
C_MOE = C_O2 + N_O2
GU_CHUNKS = KD
DN_CHUNKS = 4
E_CHUNKS = GU_CHUNKS + DN_CHUNKS
assert E_CHUNKS == SLOTS

COLS = {}
_at = 0
for _name, _n in (("g_mix", 8), ("pool_scale", 4), ("conv_w", 12), ("norm1_g", 8), ("mu", 16), ("w0", 4),
                  ("a0", 4), ("k_k", 4), ("k_a", 4), ("r_k", 4), ("ln_g", 4), ("ln_b", 4), ("q_g", 1),
                  ("k_g", 1), ("norm2_g", 8), ("c", 8)):
    COLS[_name] = (_at, _n)
    _at += _n
N_COLS = _at
M_GROUP, M_LORA, M_GUP, M_ROUTER = 0, 512, 1024, 2048
N_MATS = M_ROUTER + KD * NE


def build(nc, xd, stream, colsd, matsd, rowsd, badad, expert_u, expert_v, w_gate_up, w_down, bias_moe, out, dbg=None):
    with ExitStack() as ctx:
        def sb(name, shape, dt=F32):
            return ctx.enter_context(nc.sbuf_tensor(name, shape, dt))

        def sem(name):
            return ctx.enter_context(nc.semaphore(name))

        ring = sb("ring", [P, SLOTS, CHUNK])
        xres = sb("xres", [P, TT, D])
        gates = sb("gates", [P, 2, D])
        mats = sb("mats", [P, N_MATS])
        cols = sb("cols", [P, N_COLS])
        modcols = sb("modcols", [P, 4, KD])
        evcols = sb("evcols", [P, 2, KD])
        ident = sb("ident", [P, P])
        ones = sb("ones", [P, P])
        headblk = sb("headblk", [P, P])
        mask_st = sb("mask_st", [P, 2, P])
        mask_ts = sb("mask_ts", [P, P])
        before = sb("before", [P, P])
        iota16 = sb("iota16", [P, TOPK])
        iota_slot = sb("iota_slot", [P, 2 * CAP])
        iota_e = sb("iota_e", [P, NE])
        iota_e2 = sb("iota_e2", [P, NE + 1])
        half_e = sb("half_e", [P, P])
        brow_r = sb("brow_r", [P, NE])
        stat = sb("stat", [P, 8])
        AR = 20480
        arena = sb("arena", [P, AR])
        psum = ctx.enter_context(nc.psum_tensor("psum", [P, 8, 512], F32))

        def area(at, *dims, parts=P):
            n = int(np.prod(dims))
            assert at + n <= AR, (at, dims)
            v = arena[0:parts, at:at + n]
            if len(dims) == 2:
                v = v.rearrange("p (a b) -> p a b", a=dims[0])
            if len(dims) == 3:
                v = v.rearrange("p (a b c) -> p a b c", a=dims[0], b=dims[1])
            return v

        def col(name, i=0):
            at, n = COLS[name]
            assert i < n
            return cols[:, at + i:at + i + 1]

        xn = area(0, TT, D)
        hT = area(2048, KD, T)
        zT = area(4096, 28, T)
        PADW = 16 + T
        u_pad = area(11264, POOL_G, PADW)
        q_a = area(12352, POOL_G, PADW)
        q_b = area(13440, POOL_G, PADW)
        cnt = area(14528, POOL_G, T)
        pT = area(15552, POOL_G, T)
        aT = area(16576, POOL_G, T)
        cv = area(17600, 4, 2 + T)
        cT = area(18632, 4, T)
        mT = area(11264, KD, T)
        gffn = area(14528, D)
        h2 = area(0, TT, D)
        h2T = area(2048, KD, T)
        xn2 = area(4096, TT, D)
        qT = area(8192, HP, T)
        S = area(4096, TT, HP, NK)
        gat = area(8192, GATHER_SLOTS, D)
        cand = area(12288, HEADS, TOPK * TOPK)
        eq = area(2048, HK, TOPK)
        brow = area(15552, 6 * CW)
        cb = area(17088, KD, P)
        mrow = area(18112, 2, CW)
        gfin = area(12288, D)
        sm = 18624
        top_s = area(sm, HEADS, 2, TOPK)
        top_i = area(sm + 256, HEADS, 2, TOPK).bitcast(U32)
        top_f = area(sm + 512, HEADS, 2, TOPK)
        fin_s = area(sm + 768, HEADS, TOPK)
        fin_p = area(sm + 896, HEADS, TOPK).bitcast(U32)
        pos_u = area(sm + 1024, 2, HK).bitcast(U32)
        pos_f = area(14336, 2, HK)
        sel_f = area(14592, 2, HK)
        stat_c = sb("stat_c", [P, KD])
        gsm = sb("gsm", [P, 4, HEADS])
        peer_g = sb("peer_g", [P, TT, HK])
        peer_i = area(14848, TT, HK).bitcast(U32)
        peer_h = area(15104, TT, HK)
        st_i = sb("st_i", [P, TOPK], U32)
        st_h = sb("st_h", [P, TOPK])

        xn3 = area(2048, TT, D)
        hT3 = area(0, KD, T)
        mqk = area(4096, 2 * 4, T)
        mv = area(6144, TT, W2)
        msq = area(7168, 2 * 4, T)
        mrs = area(9216, 2 * 4, T)
        dist0 = area(11264, P)
        dist1 = area(11392, T)
        sc0 = area(11776, NH, P)
        sc1 = area(12800, NH, T)
        prT = area(7168, NH, TT, P)
        ymT = area(2048, 4, T)
        PT1 = T + 1
        pt = area(16624, 15, PT1)
        ps = area(4096, 15, T)
        r_, k_, v_ = ps[:, 0:4, :], ps[:, 4:8, :], ps[:, 8:12, :]
        wd = area(7936, 4, T)
        aa = area(8960, 4, T)
        gg = area(9984, 4, T)
        kk = area(11008, 4, T)
        t1 = area(12032, 4, T)
        t2 = area(13056, 4, T)
        pc = area(14080, 4, T)
        ar = area(15104, 4, 2, T)
        bt = area(17152, 4, T)
        kt_ = area(18176, 4, T)
        bon = area(19200, 4, T)
        nak = area(0, NH, 2, P)
        pw_s = area(3072, NH, P)
        pw_t = area(4096, NH, P)
        inv = area(5120, NH, P)
        phi = area(3072, P // CL, 4, P)
        gam = area(5120, P // CL, 4, HD)
        tok = area(7168, 4, W2)
        rbk = area(11008, NH, 2, P)
        nts = area(13056, NH, P)
        qt = area(13056, 4, P)
        yT = area(14080, 4, T)
        states = [area(9216 + 256 * i, 4, HD) for i in range(3)]
        states += [mats[:, 256 * i:256 * i + 256].rearrange("p (a b) -> p a b", a=4) for i in range(2)]
        z2 = area(3072, NH, HD)
        dn = area(0, 4, T)
        dsq = area(11008, 4, T)
        drs = area(12032, 4, T)
        ga_t = area(3072, TT, CW)
        xn4 = area(0, TT, D)
        hT4 = area(2048, KD, T)
        acc = area(4096, TT, D)
        xs = area(6144, W2)
        xT = area(6656, 4, P)
        ag = area(7168, 512)
        au = area(7680, 512)
        sg = area(8192, 512)
        act_t = area(8704, 4, P)
        ye = area(9216, 512)
        sct = area(9728, TT, P)
        oh = area(9984, TT, CAP)
        ohw = area(10112, TT, 2 * CAP)
        sel_e = area(10368, P)
        bmoe = area(10496, 3, 512)
        m0 = 12032
        lg = area(m0, TT, NE)
        eqe = area(m0 + 64, TT, NE)
        picks = area(m0 + 128, TT, NE)
        wts = area(m0 + 192, TT, NE)
        rank = area(m0 + 256, TT, NE + 1)
        top8 = area(m0 + 392, TT, 8)
        top8i = area(m0 + 408, TT, 8).bitcast(U32)
        top8f = area(m0 + 424, TT, 8)
        w4 = area(m0 + 440, TT, TOPE)
        wsum = area(m0 + 448, 2, TT)
        most = area(m0 + 452, 1)
        most_i = area(m0 + 453, 1).bitcast(I32)
        mx = gsm[:, 0:2, :]
        pl = peer_g[:, 0, 0:4 * NC].rearrange("p (a b) -> p a b", a=4)

        loaded_x = sem("loaded_x")
        loaded_p = sem("loaded_p")
        loaded_rows = sem("loaded_rows")
        loaded_fin = sem("loaded_fin")
        consts = sem("consts")
        const_step = sem("const_step")
        landed = [sem(f"landed{i}") for i in range(SLOTS)]
        chunk_done = sem("chunk_done")
        vec_step = sem("vec_step")
        ms_ready = sem("ms_ready")
        std_ready = sem("std_ready")
        xn_ready = [sem(f"xn_ready{i}") for i in range(4)]
        turned = [sem(f"turned{i}") for i in range(4)]
        hT_ready = [sem(f"hT_ready{i}") for i in range(4)]
        z_out = sem("z_out")
        p_ready = sem("p_ready")
        group_mm = sem("group_mm")
        a_ready = sem("a_ready")
        c_ready = sem("c_ready")
        br_mm = sem("br_mm")
        m_ready = sem("m_ready")
        x_mid = sem("x_mid")
        q_out = sem("q_out")
        s_mm = sem("s_mm")
        s_out = sem("s_out")
        exp_in = sem("exp_in")
        exp_out = sem("exp_out")
        idx_ready = sem("idx_ready")
        staged = sem("staged")
        free_seen = sem("free_seen")
        row_in = [sem(f"row_in{i}") for i in range(GATHER_SLOTS)]
        row_used = sem("row_used")
        head_kept = sem("head_kept")
        dots_done = sem("dots_done")
        gelu_done = sem("gelu_done")
        cb_sig = sem("cb_sig")
        cb_ready = sem("cb_ready")
        ada_out = sem("ada_out")
        mcol_mm = sem("mcol_mm")
        mcol_out = sem("mcol_out")
        ev_ready = sem("ev_ready")
        stored = sem("stored")
        mb_out = sem("mb_out")
        rw_out = sem("rw_out")
        bias_made = sem("bias_made")
        msq_ready = sem("msq_ready")
        msum_mm = sem("msum_mm")
        mms_ready = sem("mms_ready")
        mstd_ready = sem("mstd_ready")
        mqk_ready = sem("mqk_ready")
        sc_mm = sem("sc_mm")
        sc_read = sem("sc_read")
        mexp_in = sem("mexp_in")
        mexp_out = sem("mexp_out")
        prob_ready = sem("prob_ready")
        pr_mm = sem("pr_mm")
        prT_ready = sem("prT_ready")
        pv_mm = sem("pv_mm")
        ym_ready = sem("ym_ready")
        ps_ready = sem("ps_ready")
        lora_in = sem("lora_in")
        lora_mm = sem("lora_mm")
        sig_out = sem("sig_out")
        dec_out = sem("dec_out")
        ksq_ready = sem("ksq_ready")
        ksum_mm = sem("ksum_mm")
        knorm_out = sem("knorm_out")
        rkk_ready = sem("rkk_ready")
        bon_mm = sem("bon_mm")
        tilde = sem("tilde")
        tok_mm = sem("tok_mm")
        tok_ready = sem("tok_ready")
        gram_mm = sem("gram_mm")
        gram_out = sem("gram_out")
        nt_mm = sem("nt_mm")
        nt_out = sem("nt_out")
        ps_mm = sem("ps_mm")
        ps_out = sem("ps_out")
        pt_mm = sem("pt_mm")
        pt_out = sem("pt_out")
        ix_mm = sem("ix_mm")
        ix_out = sem("ix_out")
        wu_mm = sem("wu_mm")
        wu_out = sem("wu_out")
        q2_mm = sem("q2_mm")
        q2_out = sem("q2_out")
        yp_mm = sem("yp_mm")
        yp_out = sem("yp_out")
        fg_mm = sem("fg_mm")
        fg_out = sem("fg_out")
        st_mm = sem("st_mm")
        st_out = sem("st_out")
        ys_mm = sem("ys_mm")
        ys_out = sem("ys_out")
        ln_mm = sem("ln_mm")
        ln_sq = sem("ln_sq")
        ln_ms = sem("ln_ms")
        ln_std = sem("ln_std")
        y_done = sem("y_done")
        lg_mm = sem("lg_mm")
        wexp_in = sem("wexp_in")
        wexp_out = sem("wexp_out")
        picks_ready = sem("picks_ready")
        rank_mm = sem("rank_mm")
        count_ready = sem("count_ready")
        loaded_b = sem("loaded_b")
        oh_ready = sem("oh_ready")
        ohw_ready = sem("ohw_ready")
        sel_ready = sem("sel_ready")
        g_mm = sem("g_mm")
        xs_ready = sem("xs_ready")
        xt_mm = sem("xt_mm")
        xT_ready = sem("xT_ready")
        gu_mm = sem("gu_mm")
        xt_scaled = sem("xt_scaled")
        up_ready = sem("up_ready")
        rk_made = sem("rk_made")
        gate_ready = sem("gate_ready")
        gu_read = sem("gu_read")
        sg_ready = sem("sg_ready")
        act_ready = sem("act_ready")
        at_mm = sem("at_mm")
        actT_ready = sem("actT_ready")
        y_mm = sem("y_mm")
        ye_ready = sem("ye_ready")
        sct_mm = sem("sct_mm")
        sct_ready = sem("sct_ready")
        sum_mm = sem("sum_mm")
        acc_done = sem("acc_done")
        out_ready = sem("out_ready")

        def uses(n):
            return 16 * (n // SLOTS + 1)

        def slot(n):
            return ring[:, n % SLOTS, :]

        def wide(n):
            return slot(n).rearrange("p (k c) -> p k c", k=KD)

        def further_passes(eng, work):
            eng.wait_ge(count_ready, 1)
            count = eng.value_load(most_i[0:1, 0:1], min_val=0, max_val=T)
            with eng.Fori(1, PASSES) as p:
                with eng.If(count > p * CAP):
                    work(p)

        block = ctx.enter_context(nc.Block())

        @block.sync
        def _(sp):
            sp.dma_start(xres[:], xd.rearrange("(a p) d -> p a d", p=P)).then_inc(loaded_x, 16)
            for j in range(SLOTS):
                sp.dma_start(ring[:, j, :], stream[j]).then_inc(landed[j], 16)
            whole = C_MOE // SLOTS
            with sp.Fori(1, whole) as i:
                for j in range(SLOTS):
                    sp.wait_ge(chunk_done, i * SLOTS + (j - SLOTS + 1))
                    sp.dma_start(ring[:, j, :], stream[i * SLOTS + j]).then_inc(landed[j], 16)
            for n in range(whole * SLOTS, C_MOE):
                sp.wait_ge(chunk_done, n - SLOTS + 1)
                sp.dma_start(slot(n), stream[n]).then_inc(landed[n % SLOTS], 16)

            def experts(p):
                with sp.Fori(0, NE) as e:
                    for j in range(E_CHUNKS):
                        n = C_MOE + j
                        sp.wait_ge(chunk_done, e * E_CHUNKS + (p * (NE * E_CHUNKS) + (n - SLOTS + 1)))
                        if j < GU_CHUNKS:
                            src = w_gate_up[e, j * P:(j + 1) * P, :]
                            dst = slot(n)
                        else:
                            q = j - GU_CHUNKS
                            src = w_down[e, q * 2 * P:(q + 1) * 2 * P, :].rearrange("(k p) c -> p k c", p=P)
                            dst = slot(n).rearrange("p (k c) -> p k c", k=2)
                        sp.dma_start(dst, src).then_inc(landed[n % SLOTS], 16)

            experts(0)
            further_passes(sp, experts)
            sp.wait_ge(out_ready, TT)
            sp.dma_start(out.rearrange("(a p) d -> p a d", p=P), xres[:]).then_inc(stored, 16)
            sp.wait_ge(stored, 16)

        @block.gpsimd
        def _(pool):
            made = [0]

            def make(ins):
                made[0] += 1
                ins.then_inc(const_step, 1)
                pool.wait_ge(const_step, made[0])

            def number(out, pattern, base=0, by_row=0):
                return pool.iota(out, pattern, base=base, channel_multiplier=by_row,
                                 allow_small_or_imprecise_dtypes=True)

            def keep(m, src, pattern, op, base=0, by_row=0):
                return pool.affine_select(out=m, in_=src, compare_op=op, fill=0.0, base=base, pattern=pattern,
                                          channel_multiplier=by_row)

            make(pool.memset(ident[:], 0.0))
            make(pool.memset(ones[:], 1.0))
            make(pool.affine_select(out=ident[:], in_=ident[:], compare_op=ALU.not_equal, fill=1.0, base=0,
                                    pattern=[[-1, P]], channel_multiplier=1))
            make(number(cnt, [[0, POOL_G], [1, T]], base=1))
            make(number(iota16[:], [[1, TOPK]]))
            make(number(iota_slot[:], [[0, 2], [1, CAP]]))
            make(number(iota_e[:], [[1, NE]]))
            make(number(iota_e2[:], [[2, NE + 1]]))
            make(number(half_e[0:2 * NE, :], [[-1, 2], [0, CAP]], by_row=1))
            hb = headblk[:].rearrange("p (b c) -> p b c", b=2)
            make(keep(hb, ones[:].rearrange("p (b c) -> p b c", b=2), [[-HD, 2], [0, HD]], ALU.is_ge, by_row=1))
            make(keep(hb, hb, [[HD, 2], [0, HD]], ALU.is_ge, base=HD - 1, by_row=-1))
            make(keep(before[:], ones[:], [[1, P]], ALU.is_gt, by_row=-1))
            in_chunks = [[-CL, P // CL], [0, CL]]
            for m, op in ((0, ALU.is_gt), (1, ALU.is_ge)):
                mm = mask_st[:, m, :]
                make(keep(mm, ones[:], [[1, P]], op, by_row=-1))
                mm = mm.rearrange("p (b c) -> p b c", c=CL)
                make(keep(mm, mm, in_chunks, ALU.is_ge, by_row=1))
            mm = mask_ts[:]
            make(keep(mm, ones[:], [[-1, P]], ALU.is_gt, by_row=1))
            mm = mm.rearrange("p (b c) -> p b c", c=CL)
            make(keep(mm, mm, [[CL, P // CL], [0, CL]], ALU.is_ge, base=CL - 1, by_row=-1))
            pool.sem_inc(consts, 1)

            def gather(table, tt, first):
                with pool.Fori(0, HEADS) as i:
                    for q in range(TOPK // GATHER_SLOTS):
                        at = q * GATHER_SLOTS
                        pool.tensor_copy(st_i[:, at:at + GATHER_SLOTS],
                                         peer_i[:, tt, bass.ds(i * TOPK + at, GATHER_SLOTS)]).then_inc(staged, 1)
                        pool.wait_ge(staged, i * 4 + (first // GATHER_SLOTS + q + 1))
                        for k in range(GATHER_SLOTS):
                            pool.wait_ge(row_used, i * TOPK + (first + at + k + 1))
                            pool.sem_inc(free_seen, 1)
                            pool.indirect_dma_start(gat[:, k, :], None, table,
                                                    bass.IndirectOffsetOnAxis(st_i[:, at + k:at + k + 1], 0)
                                                    ).then_inc(row_in[k], 16)

            for n, (table, tt) in enumerate(((expert_u, 0), (expert_u, 1), (expert_v, 0), (expert_v, 1))):
                if n < 2:
                    pool.wait_ge(idx_ready, n + 1)
                gather(table, tt, n * HK)
            pool.wait_ge(xn_ready[2], TT)
            at = made[0]
            for tt, m in ((0, dist0), (1, dist1)):
                n = m.shape[-1]
                make(number(m, [[1, n]], base=-tt * P, by_row=-1))
                make(pool.affine_select(out=m, in_=m, compare_op=ALU.is_ge, fill=NEG, base=tt * P,
                                        pattern=[[-1, n]], channel_multiplier=1))
            for sc, m in ((sc0, dist0), (sc1, dist1)):
                for par in range(2):
                    for c in range(4):
                        pool.tensor_scalar(sc[:, 4 * par + c, :], m, 2.0 ** -(2 * c + par + 1), None,
                                           ALU.mult).then_inc(bias_made, 1)

        @block.scalar
        def _(act):
            act.dma_start(cols[:], colsd).then_inc(loaded_p, 16)
            act.dma_start(mats[:], matsd).then_inc(loaded_p, 16)
            act.dma_start(brow_r[:], rowsd[:, 2 * D:2 * D + NE].to_broadcast([P, NE])).then_inc(loaded_p, 16)

            def deviation(n):
                act.wait_ge(ms_ready, 2 * (n + 1))
                act.activation(stat[:, 2:4], stat[:, 0:2], ACT.Sqrt).then_inc(std_ready, 1)

            def turn_out(n, dst, scale=None, bias=None):
                for k in range(KD):
                    act.wait_ge(turned[n], k + 1)
                    src = psum[:, k % 4, 0:T]
                    if scale is None:
                        act.copy(dst[:, k, :], src).then_inc(hT_ready[n], 1)
                    elif bias is None:
                        act.activation(dst[:, k, :], src, ACT.Copy, scale=scale(k)).then_inc(hT_ready[n], 1)
                    else:
                        act.activation(dst[:, k, :], src, ACT.Identity, scale=scale(k),
                                       bias=bias(k)).then_inc(hT_ready[n], 1)

            act.sem_inc(ye_ready, 1)
            act.sem_inc(sct_ready, 1)
            act.wait_ge(loaded_p, 48)
            deviation(0)
            turn_out(0, hT, lambda k: col("g_mix", k))
            for n in range(N_Z):
                act.wait_ge(chunk_done, C_Z + n + 1)
                src = psum[:, 2 + n % 4, :].rearrange("p (a t) -> p a t", a=2)
                if n < 2:
                    act.copy(u_pad[:, 2 * n:2 * n + 2, 16:16 + T], src).then_inc(z_out, 1)
                elif n < 8:
                    act.copy(zT[:, 2 * n - 4:2 * n - 2, :], src).then_inc(z_out, 1)
                else:
                    act.activation(zT[:, 2 * n - 4:2 * n - 2, :], src, ACT.Sigmoid).then_inc(z_out, 1)
            act.wait_ge(group_mm, 1)
            for g in range(POOL_G):
                act.activation(aT[:, g, :], psum[:, 6 + g // 2, (g % 2) * T:(g % 2) * T + T], ACT.Copy,
                               scale=col("pool_scale", g)).then_inc(a_ready, 1)
            act.wait_ge(m_ready, KD)
            act.activation(modcols[:, 0, :], cols[:, COLS["c"][0]:COLS["c"][0] + KD], ACT.Sigmoid).then_inc(cb_sig, 1)
            act.dma_start(gffn, rowsd[:, 0:D].to_broadcast([P, D])).then_inc(loaded_rows, 16)
            act.dma_start(brow[0:97:32, :], badad).then_inc(loaded_rows, 16)
            deviation(1)
            turn_out(1, h2T)
            for n in range(N_Q):
                act.wait_ge(chunk_done, C_Q + n + 1)
                act.copy(qT[:, 2 * n:2 * n + 2, :],
                         psum[:, 2 + n % 4, :].rearrange("p (a t) -> p a t", a=2)).then_inc(q_out, 1)
            for n in range(TT * HP // 4):
                act.wait_ge(s_mm, n + 1)
                act.copy(S[:, n // 4, 4 * (n % 4):4 * (n % 4) + 4, :],
                         psum[:, n % 4, :].rearrange("p (a c) -> p a c", a=4)).then_inc(s_out, 1)

            def mod_chunk(n):
                act.wait_ge(chunk_done, C_ADA + n + 1)
                part, at = n // 4, (n % 4) * CW
                src = psum[:, 4 + n % 2, 0:CW]
                if part in (2, 5):
                    act.copy(gates[:, part // 3, at:at + CW], src).then_inc(ada_out, 1)
                else:
                    w = part if part < 2 else part - 1
                    act.copy(mrow[0:1, n % 2, :], src[0:1]).then_inc(ada_out, 1)
                    m = sum(1 for x in range(n) if x // 4 not in (2, 5))
                    act.wait_ge(mcol_mm, m + 1)
                    act.copy(modcols[:, w, 2 * (n % 4):2 * (n % 4) + 2], psum[:, 6, 0:2]).then_inc(mcol_out, 1)

            act.wait_ge(cb_ready, KD)
            for n in range(2):
                mod_chunk(n)
            for tt in range(TT):
                act.wait_ge(exp_in, tt + 1)
                act.activation(peer_g[:, tt, :], peer_g[:, tt, :], ACT.Exp).then_inc(exp_out, 1)
                for n in range(2 + 11 * tt, 13 + 11 * tt):
                    mod_chunk(n)
            for tt in range(TT):
                act.wait_ge(dots_done, tt + 1)
                act.activation(peer_h[:, tt, :], peer_h[:, tt, :], ACT.Gelu).then_inc(gelu_done, 1)
            act.wait_ge(idx_ready, 2)
            act.dma_start(gfin, rowsd[:, D:2 * D].to_broadcast([P, D])).then_inc(loaded_fin, 16)
            deviation(2)
            deviation(3)
            act.wait_ge(ev_ready, 2)
            turn_out(2, hT3, lambda k: evcols[:, 0, k:k + 1], lambda k: modcols[:, 0, k:k + 1])
            for n in range(N_MB):
                act.wait_ge(chunk_done, C_MB + n + 1)
                src = psum[:, 2 + n % 4, :].rearrange("p (a t) -> p a t", a=2)
                dst = mqk[:, 2 * n:2 * n + 2, :] if n < 4 else mv[:, :, (n - 4) * CW:(n - 3) * CW]
                act.copy(dst, src).then_inc(mb_out, 1)
            for n in range(N_RW):
                act.wait_ge(chunk_done, C_RW + n + 1)
                src = psum[:, 2 + (N_MB + n) % 4, :].rearrange("p (a t) -> p a t", a=2)
                if n < N_RW - 1:
                    act.copy(pt[:, 2 * n:2 * n + 2, 1:], src).then_inc(rw_out, 1)
                else:
                    act.copy(pt[0:32, 14, 1:], src[0:32, 0, :]).then_inc(rw_out, 1)
            act.wait_ge(mms_ready, 4)
            act.activation(mrs, mrs, ACT.Sqrt).then_inc(mstd_ready, 1)
            for tt, sc in ((0, sc0), (1, sc1)):
                act.wait_ge(mexp_in, tt + 1)
                act.activation(sc, sc, ACT.Exp).then_inc(mexp_out, 1)
                for b in range(2 * (tt + 1)):
                    act.wait_ge(pr_mm, 2 * tt + b + 1)
                    src = psum[:, (0, 1, 4, 5, 6, 7)[2 * tt + b], :]
                    if tt == 0:
                        act.copy(prT[:, 4 * b:4 * b + 4, 0, :], src.rearrange("p (a t) -> p a t", a=4)).then_inc(prT_ready, 1)
                    else:
                        act.copy(prT[:, 2 * b:2 * b + 2, :, :],
                                 src.rearrange("p (a b t) -> p a b t", a=2, b=2)).then_inc(prT_ready, 1)
                act.wait_ge(pv_mm, tt + 1)
                act.copy(ymT[:, :, tt * P:(tt + 1) * P],
                         psum[:, 2 + tt, :].rearrange("p (a t) -> p a t", a=4)).then_inc(ym_ready, 1)
            act.wait_ge(ps_ready, 1)
            act.activation(ps[0:64, 12, :], ps[0:64, 12, :], ACT.Tanh).then_inc(lora_in, 1)
            act.activation(ps[:, 13, :], ps[:, 13, :], ACT.Sigmoid).then_inc(lora_in, 1)
            act.activation(ps[0:32, 14, :], ps[0:32, 14, :], ACT.Sigmoid).then_inc(lora_in, 1)
            act.wait_ge(lora_mm, 3)
            for c in range(4):
                src = psum[:, c // 2, (c % 2) * T:(c % 2) * T + T]
                act.activation(wd[:, c, :], src, ACT.Sigmoid, bias=col("w0", c)).then_inc(sig_out, 1)
            for c in range(4):
                src = psum[:, 2 + c // 2, (c % 2) * T:(c % 2) * T + T]
                act.activation(aa[:, c, :], src, ACT.Sigmoid, bias=col("a0", c)).then_inc(sig_out, 1)
            for b in range(2):
                act.copy(gg[:, 2 * b:2 * b + 2, :],
                         psum[:, 4 + b, :].rearrange("p (a t) -> p a t", a=2)).then_inc(sig_out, 1)
            act.wait_ge(ksum_mm, 1)
            for b in range(2):
                act.activation(t1[:, 2 * b:2 * b + 2, :], psum[:, 6 + b, :].rearrange("p (a t) -> p a t", a=2),
                               ACT.Sqrt).then_inc(knorm_out, 1)
            act.wait_ge(sig_out, 4)
            act.activation(wd, wd, ACT.Exp, scale=-float(np.exp(-0.5))).then_inc(dec_out, 1)
            for tt in range(TT):
                for i in range(0, 4, 2):
                    act.wait_ge(tok_mm, 4 * tt + i + 1)
                    act.copy(tok[:, i, :], psum[:, i, :]).then_inc(tok_ready, 1)
                for lv in range(1, 5):
                    dst = (nts, pw_t)[lv % 2]
                    for q in range(2):
                        act.wait_ge(pt_mm, 8 * tt + 2 * (lv - 1) + q + 1)
                        act.copy(dst[:, 4 * q:4 * q + 4, :],
                                 psum[:, 2 + q, :].rearrange("p (a t) -> p a t", a=4)).then_inc(pt_out, 1)
                act.wait_ge(yp_mm, tt + 1)
                act.copy(yT[:, :, tt * P:(tt + 1) * P],
                         psum[:, 1, :].rearrange("p (a t) -> p a t", a=4)).then_inc(yp_out, 1)
            act.wait_ge(ln_ms, 1)
            act.activation(drs, drs, ACT.Sqrt).then_inc(ln_std, 1)
            deviation(4)
            turn_out(3, hT4, lambda k: evcols[:, 1, k:k + 1], lambda k: modcols[:, 2, k:k + 1])
            act.dma_start(bmoe[0:2 * NE], bias_moe.rearrange("r (a c) -> r a c", a=3)).then_inc(loaded_b, 16)
            act.wait_ge(wexp_in, 1)
            act.activation(w4, w4, ACT.Exp).then_inc(wexp_out, 1)

            def front(f):
                act.wait_ge(g_mm, f + 2)
                act.copy(xs, psum[:, 2, :]).then_inc(xs_ready, 1)

            def experts(p):
                front(p * (NE + 1))
                with act.Fori(0, NE) as e:
                    it = p * NE + e
                    f = p * (NE + 1) + e
                    act.wait_ge(gate_ready, it + 1)
                    act.activation(sg, ag, ACT.Sigmoid, scale=ALPHA).then_inc(sg_ready, 1)
                    front(f + 1)
                    act.wait_ge(at_mm, it + 1)
                    act.copy(act_t, psum[:, 4, :].rearrange("p (a t) -> p a t", a=4)).then_inc(actT_ready, 1)
                    act.wait_ge(y_mm, it + 1)
                    act.copy(ye, psum[:, 5, :]).then_inc(ye_ready, 1)
                    act.wait_ge(sct_mm, it + 2)
                    act.copy(sct, psum[:, 2, 0:2 * P].rearrange("p (a t) -> p a t", a=2)).then_inc(sct_ready, 1)

            experts(0)
            further_passes(act, experts)

        @block.vector
        def _(dve):
            steps = [0]

            def ordered(ins):
                steps[0] += 1
                ins.then_inc(vec_step, 1)
                dve.wait_ge(vec_step, steps[0])

            def norm(n, dst, src):
                for tt in range(TT):
                    dve.tensor_tensor_reduce(dst[:, tt, :], src[:, tt, :], src[:, tt, :], 1.0 / D, EPS,
                                             ALU.mult, ALU.add, stat[:, tt:tt + 1]).then_inc(ms_ready, 1)
                dve.wait_ge(std_ready, n + 1)
                ordered(dve.reciprocal(stat[:, 4:6], stat[:, 2:4]))
                dve.wait_ge(ms_ready, 2 * (n + 1))

            dve.sem_inc(row_used, GATHER_SLOTS)
            dve.sem_inc(gu_read, 1)
            dve.sem_inc(acc_done, 1)
            dve.memset(u_pad[:, :, 0:16], 0.0)
            dve.memset(q_a[:, :, 0:16], 0.0)
            dve.memset(q_b[:, :, 0:16], 0.0)
            ordered(dve.memset(cv[:, :, 0:2], 0.0))
            dve.wait_ge(loaded_x, 16)
            norm(0, xn, xres)
            for tt in range(TT):
                dve.tensor_scalar(xn[:, tt, :], xres[:, tt, :], stat[:, 4 + tt:5 + tt], None,
                                  ALU.mult).then_inc(xn_ready[0], 1)
            dve.wait_ge(consts, 1)
            for g in range(POOL_G):
                dve.tensor_scalar(cnt[:, g, :], cnt[:, g, :], float(2 << g), None, ALU.min).then_inc(vec_step, 1)
            steps[0] += POOL_G
            dve.wait_ge(vec_step, steps[0])
            ordered(dve.reciprocal(cnt, cnt))
            dve.wait_ge(z_out, 2)
            ordered(dve.tensor_tensor(q_a[:, :, 16:], u_pad[:, :, 16:], u_pad[:, :, 15:15 + T], ALU.add))
            ordered(dve.tensor_tensor(q_b[:, 1:, 16:], q_a[:, 1:, 16:], q_a[:, 1:, 14:14 + T], ALU.add))
            ordered(dve.tensor_tensor(q_a[:, 2:, 16:], q_b[:, 2:, 16:], q_b[:, 2:, 12:12 + T], ALU.add))
            ordered(dve.tensor_tensor(q_b[:, 3:, 16:], q_a[:, 3:, 16:], q_a[:, 3:, 8:8 + T], ALU.add))
            dve.tensor_tensor(pT[:, 0:4:2, :], q_a[:, 0:4:2, 16:], cnt[:, 0:4:2, :], ALU.mult).then_inc(vec_step, 1)
            steps[0] += 1
            ordered(dve.tensor_tensor(pT[:, 1:4:2, :], q_b[:, 1:4:2, 16:], cnt[:, 1:4:2, :], ALU.mult))
            dve.tensor_tensor(pT, pT, u_pad[:, :, 16:], ALU.subtract).then_inc(p_ready, 1)
            dve.wait_ge(z_out, 8)
            ordered(dve.tensor_tensor(cv[:, :, 2:], zT[:, 0:4, :], zT[:, 8:12, :], ALU.mult))
            for t in range(4):
                dve.tensor_scalar(cT[:, t, :], cv[:, t, 0:T], col("conv_w", t), None, ALU.mult).then_inc(vec_step, 1)
            steps[0] += 4
            dve.wait_ge(vec_step, steps[0])
            for w in (1, 2):
                for t in range(4):
                    dve.scalar_tensor_tensor(cT[:, t, :], cv[:, t, w:w + T], col("conv_w", 4 * w + t), cT[:, t, :],
                                             ALU.mult, ALU.add).then_inc(vec_step, 1)
                steps[0] += 4
                dve.wait_ge(vec_step, steps[0])
            dve.tensor_tensor(cT, cT, zT[:, 4:8, :], ALU.mult).then_inc(c_ready, 1)
            dve.wait_ge(z_out, N_Z)
            dve.wait_ge(p_ready, 1)
            for k in range(KD):
                dve.wait_ge(br_mm, k + 1)
                ab = psum[:, 2 + k % 4, :].rearrange("p (a t) -> p a t", a=2)
                ga = zT[:, 12 + k, :]
                gb = zT[:, 20 + k, :]
                dve.tensor_tensor(ga, ab[:, 0, :], ga, ALU.mult).then_inc(vec_step, 1)
                steps[0] += 1
                ordered(dve.tensor_tensor(gb, ab[:, 1, :], gb, ALU.mult))
                dve.tensor_tensor(mT[:, k, :], ga, gb, ALU.add).then_inc(m_ready, 1)
            for n in range(N_O1):
                dve.wait_ge(chunk_done, C_O1 + n + 1)
                dve.tensor_tensor(xres[:, :, n * CW:(n + 1) * CW],
                                  psum[:, 2 + n % 4, :].rearrange("p (a c) -> p a c", a=TT),
                                  xres[:, :, n * CW:(n + 1) * CW], ALU.add).then_inc(x_mid, 1)
            dve.wait_ge(x_mid, N_O1)
            norm(1, xn2, xres)
            dve.wait_ge(loaded_rows, 32)
            for tt in range(TT):
                ordered(dve.tensor_scalar(xn2[:, tt, :], xres[:, tt, :], stat[:, 4 + tt:5 + tt], None, ALU.mult))
                dve.tensor_tensor(h2[:, tt, :], xn2[:, tt, :], gffn, ALU.mult).then_inc(xn_ready[1], 1)
            dve.wait_ge(cb_sig, 1)
            at = COLS["c"][0]
            ordered(dve.tensor_tensor(stat_c[:], cols[:, at:at + KD], modcols[:, 0, :], ALU.mult))
            for k in range(KD):
                dve.tensor_scalar(cb[:, k, :], ones[:], stat_c[:, k:k + 1], None, ALU.mult).then_inc(cb_ready, 1)

            dve.wait_ge(s_out, TT * HP // 4)
            for tt in range(TT):
                def top16(n, val, ind, of):
                    for r in range(2):
                        for i in range(n):
                            dve.max(val(i, r), of(i)).then_inc(vec_step, 1)
                        steps[0] += n
                        dve.wait_ge(vec_step, steps[0])
                        for i in range(n):
                            dve.max_index(ind(i, r), val(i, r), of(i)).then_inc(vec_step, 1)
                        steps[0] += n
                        dve.wait_ge(vec_step, steps[0])
                        if r == 0:
                            for i in range(n):
                                dve.match_replace(of(i), val(i, r), of(i), LOWEST).then_inc(vec_step, 1)
                            steps[0] += n
                            dve.wait_ge(vec_step, steps[0])

                top16(HP, lambda i, r: top_s[:, i // 2, i % 2, 8 * r:8 * r + 8],
                      lambda i, r: top_i[:, i // 2, i % 2, 8 * r:8 * r + 8], lambda i: S[:, tt, i, :])
                c4 = cand.rearrange("p h (a b) -> p h a b", a=TOPK)
                shape = [P, HEADS, TOPK, TOPK]
                ordered(dve.tensor_tensor(c4, top_s[:, :, 0, :].unsqueeze(3).to_broadcast(shape),
                                          top_s[:, :, 1, :].unsqueeze(2).to_broadcast(shape), ALU.add))
                top16(HEADS, lambda i, r: fin_s[:, i, 8 * r:8 * r + 8], lambda i, r: fin_p[:, i, 8 * r:8 * r + 8],
                      lambda i: cand[:, i, :])
                dve.tensor_tensor(peer_g[:, tt, :].rearrange("p (h k) -> p h k", h=HEADS), fin_s,
                                  fin_s[:, :, 0:1].to_broadcast([P, HEADS, TOPK]), ALU.subtract).then_inc(exp_in, 1)
                flat_p = fin_p.rearrange("p h k -> p (h k)")
                ordered(dve.tensor_copy(top_f, top_i))
                ordered(dve.tensor_scalar(pos_u[:, 0, :], flat_p, 4, None, ALU.logical_shift_right))
                ordered(dve.tensor_scalar(pos_u[:, 1, :], flat_p, 15, None, ALU.bitwise_and))
                ordered(dve.tensor_copy(pos_f, pos_u))
                sh = [P, HK, TOPK]
                for half in range(2):
                    ordered(dve.tensor_tensor(eq, pos_f[:, half, :].unsqueeze(2).to_broadcast(sh),
                                              iota16[:].unsqueeze(1).to_broadcast(sh), ALU.is_equal))
                    e4 = eq.rearrange("p (h k) a -> p h k a", h=HEADS)
                    ordered(dve.tensor_tensor(e4, e4, top_f[:, :, half, :].unsqueeze(2).to_broadcast(shape), ALU.mult))
                    ordered(dve.tensor_reduce(sel_f[:, half, :], eq, AX_X, ALU.add))
                ordered(dve.scalar_tensor_tensor(sel_f[:, 0, :], sel_f[:, 0, :], float(NK), sel_f[:, 1, :],
                                                 ALU.mult, ALU.add))
                dve.tensor_copy(peer_i[:, tt, :], sel_f[:, 0, :]).then_inc(idx_ready, 1)
                dve.wait_ge(exp_out, tt + 1)
                g3 = peer_g[:, tt, :].rearrange("p (h k) -> p h k", h=HEADS)
                ordered(dve.tensor_reduce(gsm[:, 0, :], g3, AX_X, ALU.add))
                ordered(dve.reciprocal(gsm[:, 1, :], gsm[:, 0, :]))
                ordered(dve.tensor_tensor(g3, g3, gsm[:, 1, :].unsqueeze(2).to_broadcast([P, HEADS, TOPK]), ALU.mult))

            def arrivals(i, first, k):
                return i * (16 * TOPK // GATHER_SLOTS) + 16 * ((first + k) // GATHER_SLOTS + 1)

            for tt in range(TT):
                first = tt * HK
                with dve.Fori(0, HEADS) as i:
                    for k in range(TOPK):
                        dve.wait_ge(row_in[k % GATHER_SLOTS], arrivals(i, first, k))
                        g = gat[:, k % GATHER_SLOTS, :]
                        dve.tensor_tensor_reduce(g, g, h2[:, tt, :], 1.0, 0.0, ALU.mult, ALU.add,
                                                 st_h[:, k:k + 1]).then_inc(row_used, 1)
                    dve.wait_ge(row_used, i * TOPK + (first + TOPK + GATHER_SLOTS))
                    dve.tensor_copy(peer_h[:, tt, bass.ds(i * TOPK, TOPK)], st_h[:]).then_inc(head_kept, 1)
                    dve.wait_ge(head_kept, i + (tt * HEADS + 1))
                dve.sem_inc(dots_done, 1)
            for tt in range(TT):
                dve.wait_ge(gelu_done, tt + 1)
                ordered(dve.tensor_tensor(peer_h[:, tt, :], peer_h[:, tt, :], peer_g[:, tt, :], ALU.mult))
                first = (TT + tt) * HK
                with dve.Fori(0, HEADS) as i:
                    dve.tensor_copy(st_h[:], peer_h[:, tt, bass.ds(i * TOPK, TOPK)]).then_inc(head_kept, 1)
                    dve.wait_ge(head_kept, i + ((TT + tt) * HEADS + 1))
                    for k in range(TOPK):
                        dve.wait_ge(row_in[k % GATHER_SLOTS], arrivals(i, first, k))
                        dve.scalar_tensor_tensor(xres[:, tt, :], gat[:, k % GATHER_SLOTS, :], st_h[:, k:k + 1],
                                                 xres[:, tt, :], ALU.mult, ALU.add).then_inc(row_used, 1)
                        dve.wait_ge(row_used, i * TOPK + (first + k + 1 + GATHER_SLOTS))
            norm(2, h2, xres)
            dve.wait_ge(loaded_fin, 16)
            for tt in range(TT):
                ordered(dve.tensor_scalar(xres[:, tt, :], xres[:, tt, :], stat[:, 4 + tt:5 + tt], None, ALU.mult))
                ordered(dve.tensor_tensor(xres[:, tt, :], xres[:, tt, :], gfin, ALU.mult))
            dve.wait_ge(mcol_out, 16)
            for i, name in ((0, "norm1_g"), (1, "norm2_g")):
                at, n = COLS[name]
                dve.scalar_tensor_tensor(evcols[:, i, :], modcols[:, 2 * i + 1, :], 1.0, cols[:, at:at + n],
                                         ALU.add, ALU.mult).then_inc(ev_ready, 1)
            norm(3, xn3, xres)
            for tt in range(TT):
                dve.tensor_scalar(xn3[:, tt, :], xres[:, tt, :], stat[:, 4 + tt:5 + tt], None,
                                  ALU.mult).then_inc(xn_ready[2], 1)
            ordered(dve.memset(pt[:, :, 0:1], 0.0))
            dve.wait_ge(mb_out, 4)
            dve.tensor_tensor(msq, mqk, mqk, ALU.mult).then_inc(msq_ready, 1)
            for b in range(4):
                dve.wait_ge(msum_mm, b + 1)
                dve.tensor_scalar(mrs[:, 2 * b:2 * b + 2, :], psum[:, (6, 7, 0, 1)[b], :].rearrange("p (a t) -> p a t", a=2),
                                  1.0 / HD, EPS, ALU.mult, ALU.add).then_inc(mms_ready, 1)
            dve.wait_ge(mstd_ready, 1)
            ordered(dve.reciprocal(mrs, mrs))
            for i, name in ((0, "q_g"), (1, "k_g")):
                dve.scalar_tensor_tensor(mqk[:, 4 * i:4 * i + 4, :], mqk[:, 4 * i:4 * i + 4, :], col(name),
                                         mrs[:, 4 * i:4 * i + 4, :], ALU.mult, ALU.mult).then_inc(mqk_ready, 1)
            dve.wait_ge(bias_made, 2 * NH)
            for tt, sc in ((0, sc0), (1, sc1)):
                nk = (tt + 1) * P
                hb = 4 // (tt + 1)
                for b in range(2 * (tt + 1)):
                    dve.wait_ge(sc_mm, 2 * tt + b + 1)
                    s3 = sc[:, hb * b:hb * b + hb, :]
                    src = psum[:, (6, 7, 0, 1, 2, 3)[2 * tt + b], :].rearrange("p (a t) -> p a t", a=hb)
                    dve.scalar_tensor_tensor(s3, src, float(HD) ** -0.5, s3, ALU.mult, ALU.add).then_inc(sc_read, 1)
                dve.wait_ge(sc_read, 2 * tt + 2 * (tt + 1))
                shape = [P, NH, nk]
                ordered(dve.tensor_reduce(mx[:, 0, :], sc, AX_X, ALU.max))
                dve.tensor_tensor(sc, sc, mx[:, 0, :].unsqueeze(2).to_broadcast(shape), ALU.subtract).then_inc(mexp_in, 1)
                dve.wait_ge(mexp_out, tt + 1)
                ordered(dve.tensor_reduce(mx[:, 0, :], sc, AX_X, ALU.add))
                ordered(dve.reciprocal(mx[:, 1, :], mx[:, 0, :]))
                dve.tensor_tensor(sc, sc, mx[:, 1, :].unsqueeze(2).to_broadcast(shape), ALU.mult).then_inc(prob_ready, 1)
            dve.wait_ge(ym_ready, TT)
            dve.wait_ge(rw_out, N_RW)
            dve.tensor_tensor(ps[:, 0:14, :], pt[:, 0:14, 0:T], pt[:, 0:14, 1:], ALU.subtract).then_inc(vec_step, 1)
            steps[0] += 1
            ordered(dve.tensor_tensor(ps[0:32, 14, :], pt[0:32, 14, 0:T], pt[0:32, 14, 1:], ALU.subtract))
            for t in (12, 13, 14, 4, 5, 6, 7, 0, 1, 2, 3, 8, 9, 10, 11):
                n = P if t < 14 else 32
                at = COLS["mu"][0] + t
                ins = dve.scalar_tensor_tensor(ps[0:n, t, :], ps[0:n, t, :], cols[0:n, at:at + 1], pt[0:n, t, 1:],
                                               ALU.mult, ALU.add)
                if t == 14:
                    ins.then_inc(ps_ready, 1)
            ordered(ins)
            for c in range(4):
                dve.tensor_scalar(kk[:, c, :], k_[:, c, :], col("k_k", c), None, ALU.mult).then_inc(vec_step, 1)
            steps[0] += 4
            dve.wait_ge(vec_step, steps[0])
            dve.tensor_tensor(t1, kk, kk, ALU.mult).then_inc(ksq_ready, 1)
            dve.wait_ge(sig_out, 10)
            for c in range(4):
                dve.tensor_scalar(t2[:, c, :], aa[:, c, :], -1.0, col("k_a", c), ALU.add, ALU.mult).then_inc(vec_step, 1)
            steps[0] += 4
            dve.wait_ge(vec_step, steps[0])
            ordered(dve.scalar_tensor_tensor(k_, t2, 1.0, k_, ALU.add, ALU.mult))
            for c in range(4):
                dve.scalar_tensor_tensor(t2[:, c, :], r_[:, c, :], col("r_k", c), k_[:, c, :],
                                         ALU.mult, ALU.mult).then_inc(rkk_ready, 1)
            dve.wait_ge(knorm_out, 2)
            ordered(dve.tensor_scalar(t1, t1, 1e-12, None, ALU.max))
            ordered(dve.reciprocal(t1, t1))
            ordered(dve.tensor_tensor(kk, kk, t1, ALU.mult))
            for b in range(2):
                dve.wait_ge(bon_mm, 1)
                dve.tensor_tensor(bon[:, 2 * b:2 * b + 2, :], psum[:, b, :].rearrange("p (a t) -> p a t", a=2),
                                  v_[:, 2 * b:2 * b + 2, :], ALU.mult).then_inc(vec_step, 1)
            steps[0] += 2
            dve.wait_ge(dec_out, 1)
            dve.wait_ge(vec_step, steps[0])
            ordered(dve.memset(t1, 0.0))
            ordered(dve.tensor_copy(t1[:, :, 0:T:CL], wd[:, :, 0:T:CL]))
            ordered(dve.memset(wd[:, :, 0:T:CL], 0.0))
            for c in range(4):
                dve.tensor_tensor_scan(pc[:, c, :], wd[:, c, :], t1[:, c, :], 0.0, ALU.mult, ALU.add).then_inc(vec_step, 1)
            steps[0] += 4
            dve.wait_ge(vec_step, steps[0])
            dve.tensor_copy(pl[:], pc[:, :, CL - 1:T:CL]).then_inc(vec_step, 1)
            pm = wd.rearrange("p a (c l) -> p a c l", l=CL)
            pcc = pc.rearrange("p a (c l) -> p a c l", l=CL)
            dve.memset(pm[:, :, :, 0:1], 1.0).then_inc(vec_step, 1)
            steps[0] += 2
            for c in range(4):
                dve.tensor_copy(pm[:, c, :, 1:], pcc[:, c, :, 0:CL - 1]).then_inc(vec_step, 1)
            steps[0] += 4
            dve.wait_ge(vec_step, steps[0])
            dve.wait_ge(bon_mm, 1)
            ordered(dve.reciprocal(t2, pc))
            ordered(dve.tensor_tensor(kt_, k_, t2, ALU.mult))
            ordered(dve.tensor_tensor(bt, kk, aa, ALU.mult))
            ordered(dve.tensor_tensor(bt, bt, t2, ALU.mult))
            ordered(dve.scalar_tensor_tensor(ar[:, :, 0, :], kk, -1.0, wd, ALU.mult, ALU.mult))
            dve.tensor_tensor(ar[:, :, 1, :], r_, pc, ALU.mult).then_inc(tilde, 1)
            dve.wait_ge(tilde, 1)
            ordered(dve.memset(states[0], 0.0))

            def pair4(bank):
                return psum[:, bank, :].rearrange("p (a t) -> p a t", a=4)

            for tt in range(TT):
                for i in range(1, 4, 2):
                    dve.wait_ge(tok_mm, 4 * tt + i + 1)
                    dve.tensor_copy(tok[:, i, :], psum[:, i, :]).then_inc(tok_ready, 1)
                for c in range(4):
                    for par in range(2):
                        h = 2 * c + par
                        dve.wait_ge(gram_mm, 8 * tt + h + 1)
                        g = psum[:, 4 + 2 * (c % 2) + par, :].rearrange("p (a b t) -> p b a t", a=2, b=2)
                        m = [P, 2, P]
                        dve.tensor_tensor(nak[:, h, :, :], g[:, 0, :, :], mask_st[:, 0:1, :].to_broadcast(m),
                                          ALU.mult).then_inc(vec_step, 1)
                        steps[0] += 1
                        dve.tensor_tensor(rbk[:, h, :, :], g[:, 1, :, :], mask_st[:, 1:2, :].to_broadcast(m),
                                          ALU.mult).then_inc(gram_out, 1)
                dve.wait_ge(nt_mm, tt + 1)
                for par in range(2):
                    dve.tensor_tensor(nts[:, par:NH:2, :], pair4(2 + par), mask_ts[:].unsqueeze(1).to_broadcast([P, 4, P]),
                                      ALU.mult).then_inc(nt_out, 1)
                dve.wait_ge(vec_step, steps[0])
                dve.tensor_tensor(inv, nak[:, :, 0, :], ident[:].unsqueeze(1).to_broadcast([P, NH, P]),
                                  ALU.add).then_inc(nt_out, 1)
                for lv in range(1, 5):
                    for q in range(2):
                        if lv < 4:
                            dve.wait_ge(ps_mm, 6 * tt + 2 * (lv - 1) + q + 1)
                            dst = pw_s[:, 4 * q:4 * q + 4, :] if lv % 2 else nak[:, 4 * q:4 * q + 4, 0, :]
                            dve.tensor_copy(dst, pair4(q)).then_inc(ps_out, 1)
                    for q in range(2):
                        dve.wait_ge(ix_mm, 8 * tt + 2 * (lv - 1) + q + 1)
                        iv = inv[:, 4 * q:4 * q + 4, :]
                        dve.tensor_tensor(iv, iv, pair4(4 + q), ALU.add).then_inc(ix_out, 1)
                dve.wait_ge(wu_mm, 3 * tt + 1)
                dve.tensor_copy(z2, psum[:, 6, :].rearrange("p (h c) -> p h c", h=NH)).then_inc(wu_out, 1)
                for q in range(2):
                    dve.wait_ge(wu_mm, 3 * tt + q + 2)
                    dve.tensor_copy(nak[:, 4 * q:4 * q + 4, 1, :], pair4((7, 0)[q])).then_inc(wu_out, 1)
                dve.wait_ge(q2_mm, tt + 1)
                dve.tensor_tensor(qt, pair4(0), ar[:, :, 1, tt * P:(tt + 1) * P], ALU.add).then_inc(q2_out, 1)
                ordered(dve.memset(phi, 0.0))
                for c in range(P // CL):
                    dve.wait_ge(fg_mm, 4 * tt + c + 1)
                    f4 = psum[:, 2 + c, 0:T].rearrange("p (a j) -> p a j", a=4)
                    for par in range(2):
                        a, b = HD * par, HD * par + HD
                        dve.tensor_tensor(phi[a:b, c, :, a:b], f4[a:b], ident[a:b, a:b].unsqueeze(1).to_broadcast([HD, 4, HD]),
                                          ALU.add).then_inc(vec_step, 1)
                        steps[0] += 1
                    dve.tensor_copy(gam[:, c, :, :],
                                    psum[:, 2 + c, T:2 * T].rearrange("p (a j) -> p a j", a=4)).then_inc(fg_out, 1)
                for c in range(P // CL):
                    g = tt * (P // CL) + c
                    if g == NC - 1:
                        break
                    nx = states[(g + 1) % 5]
                    dve.wait_ge(st_mm, g + 1)
                    dve.wait_ge(fg_out, 4 * tt + 4)
                    ordered(dve.tensor_tensor(nx, psum[:, 6 + g % 2, 0:T].rearrange("p (a i) -> p a i", a=4),
                                              gam[:, c, :, :], ALU.add))
                    dve.tensor_tensor(nx, nx, pl[:, :, g:g + 1].to_broadcast([P, 4, HD]), ALU.mult).then_inc(st_out, 1)
                dve.wait_ge(yp_out, tt + 1)
                for par in range(2):
                    dve.wait_ge(ys_mm, 2 * tt + par + 1)
                    a, b = HD * par, HD * par + HD
                    yv = yT[a:b, :, tt * P:(tt + 1) * P]
                    dve.tensor_tensor(yv, yv, pair4(4 + par)[a:b], ALU.add).then_inc(ys_out, 1)
            dve.wait_ge(ys_out, 4)
            for b in range(2):
                dve.wait_ge(ln_mm, b + 1)
                s2 = slice(2 * b, 2 * b + 2)
                dve.scalar_tensor_tensor(dn[:, s2, :], psum[:, b, :].rearrange("p (a t) -> p a t", a=2), -1.0 / HD,
                                         yT[:, s2, :], ALU.mult, ALU.add).then_inc(vec_step, 1)
            steps[0] += 2
            dve.wait_ge(vec_step, steps[0])
            dve.tensor_tensor(dsq, dn, dn, ALU.mult).then_inc(ln_sq, 1)
            for b in range(2):
                dve.wait_ge(ln_mm, 3 + b)
                ins = dve.tensor_scalar(drs[:, 2 * b:2 * b + 2, :], psum[:, 2 + b, :].rearrange("p (a t) -> p a t", a=2),
                                        1.0 / HD, LN_EPS, ALU.mult, ALU.add)
            ins.then_inc(ln_ms, 1)
            dve.wait_ge(ln_std, 1)
            ordered(dve.reciprocal(drs, drs))
            ordered(dve.tensor_tensor(dn, dn, drs, ALU.mult))
            for c in range(4):
                dve.tensor_scalar(dn[:, c, :], dn[:, c, :], col("ln_g", c), col("ln_b", c), ALU.mult,
                                  ALU.add).then_inc(vec_step, 1)
            steps[0] += 4
            dve.wait_ge(vec_step, steps[0])
            ordered(dve.tensor_tensor(dn, dn, bon, ALU.add))
            dve.tensor_tensor(yT, dn, gg, ALU.mult).then_inc(y_done, 1)
            for n in range(N_O2):
                dve.wait_ge(chunk_done, C_O2 + n + 1)
                cs = slice(n * CW, (n + 1) * CW)
                ordered(dve.tensor_tensor(ga_t, psum[:, 2 + n % 4, :].rearrange("p (a c) -> p a c", a=TT),
                                          gates[:, 0:1, cs].to_broadcast([P, TT, CW]), ALU.mult))
                ordered(dve.tensor_tensor(xres[:, :, cs], xres[:, :, cs], ga_t, ALU.add))
            norm(4, xn4, xres)
            for tt in range(TT):
                dve.tensor_scalar(xn4[:, tt, :], xres[:, tt, :], stat[:, 4 + tt:5 + tt], None,
                                  ALU.mult).then_inc(xn_ready[3], 1)
            dve.wait_ge(lg_mm, 1)
            sh = [P, TT, NE]
            ordered(dve.tensor_tensor(lg, psum[:, 5, 0:TT * NE].rearrange("p (a e) -> p a e", a=TT),
                                      brow_r[:].unsqueeze(1).to_broadcast(sh), ALU.add))
            for tt in range(TT):
                ordered(dve.max(top8[:, tt, :], lg[:, tt, :]))
                ordered(dve.max_index(top8i[:, tt, :], top8[:, tt, :], lg[:, tt, :]))
            ordered(dve.tensor_copy(top8f, top8i))
            dve.tensor_tensor(w4, top8[:, :, 0:TOPE], top8[:, :, 0:1].to_broadcast([P, TT, TOPE]),
                              ALU.subtract).then_inc(wexp_in, 1)
            ordered(dve.memset(picks, 0.0))
            dve.wait_ge(wexp_out, 1)
            ordered(dve.tensor_reduce(wsum[:, 0, :], w4, AX_X, ALU.add))
            ordered(dve.reciprocal(wsum[:, 1, :], wsum[:, 0, :]))
            ordered(dve.tensor_tensor(w4, w4, wsum[:, 1, :].unsqueeze(2).to_broadcast([P, TT, TOPE]), ALU.mult))
            ordered(dve.memset(wts, 0.0))
            for k in range(TOPE):
                ordered(dve.tensor_tensor(eqe, top8f[:, :, k:k + 1].to_broadcast(sh),
                                          iota_e[:].unsqueeze(1).to_broadcast(sh), ALU.is_equal))
                ordered(dve.tensor_tensor(picks, picks, eqe, ALU.add))
                ordered(dve.tensor_tensor(eqe, eqe, w4[:, :, k:k + 1].to_broadcast(sh), ALU.mult))
                ordered(dve.tensor_tensor(wts, wts, eqe, ALU.add))
            dve.memset(acc, 0.0).then_inc(picks_ready, 1)
            dve.wait_ge(rank_mm, 1)
            ordered(dve.memset(rank, -1.0))
            ordered(dve.scalar_tensor_tensor(rank[:, :, 0:NE], psum[:, 6, 0:TT * NE].rearrange("p (a e) -> p a e", a=TT),
                                             1.0, picks, ALU.add, ALU.mult))
            dve.tensor_scalar(rank[:, :, 0:NE], rank[:, :, 0:NE], -1.0, None, ALU.add).then_inc(rk_made, 1)
            ordered(dve.tensor_reduce(most, psum[:, 6, TT * NE:TT * NE + NE], AX_X, ALU.max))
            dve.tensor_copy(most_i, most).then_inc(count_ready, 1)

            def front_in(f, e):
                dve.wait_ge(g_mm, f + 1)
                for tt in range(TT):
                    ins = dve.tensor_scalar(oh[:, tt, :], iota_slot[:, 0:CAP], rank[:, tt, bass.ds(e, 1)], None, ALU.is_equal)
                ins.then_inc(oh_ready, 1)

            def bias_rows(e):
                dve.tensor_scalar(sel_e[0:2 * NE], half_e[0:2 * NE, :], iota_e2[0:2 * NE, bass.ds(e, 1)], None,
                                  ALU.is_equal).then_inc(sel_ready, 1)

            def front_out(f):
                dve.wait_ge(xt_mm, f + 1)
                sh4 = [P, 4, 2, CAP]
                x4 = xT.rearrange("p j (h s) -> p j h s", h=2)
                src = psum[:, 3, :].rearrange("p (j h s) -> p j h s", j=4, h=2)
                sc_ = evcols[:, 1, :].rearrange("p (h j) -> p j h", h=2).unsqueeze(3).to_broadcast(sh4)
                sf_ = modcols[:, 2, :].rearrange("p (h j) -> p j h", h=2).unsqueeze(3).to_broadcast(sh4)
                dve.tensor_tensor(x4, src, sc_, ALU.mult).then_inc(xt_scaled, 1)
                dve.wait_ge(xt_scaled, f + 1)
                dve.tensor_tensor(x4, x4, sf_, ALU.add).then_inc(xT_ready, 1)

            def experts(p):
                dve.wait_ge(rk_made, p + 1)
                f0 = p * (NE + 1)
                front_in(f0, 0)
                bias_rows(0)
                front_out(f0)
                with dve.Fori(0, NE) as e:
                    it = p * NE + e
                    f = p * (NE + 1) + e
                    front_in(f + 1, e + 1)
                    dve.wait_ge(sct_mm, it + 1)
                    for tt in range(TT):
                        ins = dve.tensor_scalar(ohw[:, tt, :], iota_slot[:], rank[:, tt, bass.ds(e, 1)],
                                                wts[:, tt, bass.ds(e, 1)], ALU.is_equal, ALU.mult)
                    ins.then_inc(ohw_ready, 1)
                    dve.wait_ge(gu_mm, it + 1)
                    dve.tensor_scalar(ag, psum[:, 0, :], LIMIT, None, ALU.min).then_inc(gate_ready, 1)
                    dve.tensor_scalar(au, psum[:, 1, :], LIMIT, -LIMIT, ALU.min, ALU.max).then_inc(gu_read, 1)
                    bias_rows(e + 1)
                    dve.wait_ge(gu_read, it + 2)
                    dve.scalar_tensor_tensor(au, au, 1.0, ag, ALU.add, ALU.mult).then_inc(up_ready, 1)
                    dve.wait_ge(up_ready, it + 1)
                    dve.wait_ge(sg_ready, it + 1)
                    dve.tensor_tensor(ag, au, sg, ALU.mult).then_inc(act_ready, 1)
                    front_out(f + 1)
                    for tt in range(TT):
                        dve.wait_ge(sum_mm, it * TT + (tt + 1))
                        dve.tensor_tensor(acc[:, tt, :], acc[:, tt, :],
                                          psum[:, (6, 3)[tt]:(8, 5)[tt], :].rearrange("p a c -> p (a c)"),
                                          ALU.add).then_inc(acc_done, 1)
                dve.wait_ge(acc_done, (p + 1) * (NE * TT) + 1)
                dve.tensor_scalar(rank, rank, -float(CAP), None, ALU.add).then_inc(rk_made, 1)

            experts(0)
            further_passes(dve, experts)
            for tt in range(TT):
                ordered(dve.tensor_tensor(acc[:, tt, :], acc[:, tt, :], gates[:, 1, :], ALU.mult))
                dve.tensor_tensor(xres[:, tt, :], xres[:, tt, :], acc[:, tt, :], ALU.add).then_inc(out_ready, 1)

        @block.tensor
        def _(pe):
            def turn(n, src):
                pe.wait_ge(xn_ready[n], TT)
                for k in range(KD):
                    if k >= 4:
                        pe.wait_ge(hT_ready[n], k - 3)
                    for tt in range(TT):
                        last = pe.transpose(psum[:, k % 4, tt * P:(tt + 1) * P], src[:, tt, k * P:(k + 1) * P], ident[:])
                    last.then_inc(turned[n], 1)

            def chunk(n):
                pe.wait_ge(landed[n % SLOTS], uses(n))

            def channels(n, acts, bank, width=2):
                chunk(n)
                for c in range(width):
                    for k in range(KD):
                        last = pe.matmul(psum[:, bank, c * T:(c + 1) * T], wide(n)[:, k, c * P:(c + 1) * P],
                                         acts[:, k, :], start=(k == 0), stop=(k == KD - 1))
                return last

            def tokens(n, acts, bank, owed=False):
                chunk(n)
                for tt in range(TT):
                    for k in range(KD):
                        last = pe.matmul(psum[:, bank, tt * CW:(tt + 1) * CW], acts[:, k, tt * P:(tt + 1) * P],
                                         wide(n)[:, k, :], start=(k == 0), stop=(k == KD - 1))
                        if owed and tt == 0 and k == 0:
                            last.then_inc(chunk_done, 1)
                return last

            pe.sem_inc(g_mm, 1)
            pe.sem_inc(sct_mm, 1)
            pe.wait_ge(consts, 1)
            turn(0, xn)
            pe.wait_ge(hT_ready[0], KD)
            for n in range(N_Z):
                if n >= 4:
                    pe.wait_ge(z_out, n - 3)
                channels(C_Z + n, hT, 2 + n % 4).then_inc(chunk_done, 1)
            pe.wait_ge(p_ready, 1)
            pe.wait_ge(loaded_p, 48)
            for g in range(POOL_G):
                last = pe.matmul(psum[:, 6 + g // 2, (g % 2) * T:(g % 2) * T + T],
                                 mats[:, M_GROUP + g * P:M_GROUP + (g + 1) * P], pT[:, g, :], start=True, stop=True)
            last.then_inc(group_mm, 1)
            pe.wait_ge(a_ready, POOL_G)
            pe.wait_ge(c_ready, 1)
            for k in range(KD):
                pair = k // 4
                if k % 4 == 0:
                    chunk(C_BR + 2 * pair)
                    chunk(C_BR + 2 * pair + 1)
                if k >= 4:
                    pe.wait_ge(m_ready, k - 3)
                elif k == 0:
                    pe.wait_ge(z_out, N_Z)
                for b, act_in in ((0, aT), (1, cT)):
                    w = slot(C_BR + 2 * pair + b).rearrange("p (k c) -> p k c", k=4)
                    for q in range(4):
                        last = pe.matmul(psum[:, 2 + k % 4, b * T:(b + 1) * T], w[:, q, (k % 4) * P:(k % 4 + 1) * P],
                                         act_in[:, q, :], start=(q == 0), stop=(q == 3))
                        if k == 4 and b == 0 and q == 0:
                            last.then_inc(chunk_done, 1)
                    if k % 4 == 3 and b == 0:
                        last.then_inc(chunk_done, 1)
                last.then_inc(br_mm, 1)
            pe.wait_ge(m_ready, KD)
            for n in range(N_O1):
                tokens(C_O1 + n, mT, 2 + n % 4, owed=(n == 0)).then_inc(chunk_done, 1)
            turn(1, h2)
            pe.wait_ge(hT_ready[1], KD)
            pe.wait_ge(x_mid, N_O1)
            for n in range(N_Q):
                if n >= 4:
                    pe.wait_ge(q_out, n - 3)
                channels(C_Q + n, h2T, 2 + n % 4).then_inc(chunk_done, 1)
            chunk(C_KEYS)
            pe.wait_ge(q_out, N_Q)
            for n in range(TT * HP // 4):
                if n >= 4:
                    pe.wait_ge(s_out, n - 3)
                tt = n // 4
                for i in range(4):
                    hp = 4 * (n % 4) + i
                    last = pe.matmul(psum[:, n % 4, i * NK:(i + 1) * NK], qT[:, hp, tt * P:(tt + 1) * P],
                                     slot(C_KEYS)[:, hp * NK:(hp + 1) * NK], start=True, stop=True)
                last.then_inc(s_mm, 1)
            pe.wait_ge(cb_ready, KD)
            pe.wait_ge(loaded_rows, 32)
            pe.wait_ge(s_out, TT * HP // 4)
            m = 0
            for n in range(N_ADA):
                chunk(C_ADA + n)
                if n >= 2:
                    pe.wait_ge(ada_out, n - 1)
                for k in range(KD):
                    first = pe.matmul(psum[:, 4 + n % 2, 0:CW], cb[:, k, :], wide(C_ADA + n)[:, k, :],
                                      start=(k == 0), stop=False)
                    if n == 0 and k == 0:
                        first.then_inc(chunk_done, 1)
                r = 32 * (n // 6)
                last = pe.matmul(psum[:, 4 + n % 2, 0:CW], ones[r:r + 1, :], brow[r:r + 1, (n % 6) * CW:(n % 6 + 1) * CW],
                                 start=False, stop=True)
                last.then_inc(chunk_done, 1)
                if n // 4 not in (2, 5):
                    pe.wait_ge(ada_out, n + 1)
                    if m:
                        pe.wait_ge(mcol_out, m)
                    for i in range(2):
                        last = pe.matmul(psum[:, 6, i:i + 1], mrow[0:1, n % 2, i * P:(i + 1) * P], ones[0:1, 0:1],
                                         start=True, stop=True)
                    last.then_inc(mcol_mm, 1)
                    m += 1
            turn(2, xn3)
            pe.wait_ge(hT_ready[2], KD)
            for n in range(N_MB):
                if n >= 4:
                    pe.wait_ge(mb_out, n - 3)
                ins = channels(C_MB + n, hT3, 2 + n % 4) if n < 4 else tokens(C_MB + n, hT3, 2 + n % 4)
                ins.then_inc(chunk_done, 1)
            pe.wait_ge(msq_ready, 1)
            for b in range(4):
                pe.matmul(psum[:, (6, 7, 0, 1)[b], :], headblk[:], msq[:, 2 * b:2 * b + 2, :].rearrange("p a t -> p (a t)"),
                          start=True, stop=True).then_inc(msum_mm, 1)
            for n in range(N_RW):
                k = N_MB + n
                pe.wait_ge(mb_out, min(k - 3, N_MB))
                if k - 3 > N_MB:
                    pe.wait_ge(rw_out, k - 3 - N_MB)
                if n < N_RW - 1:
                    channels(C_RW + n, hT3, 2 + k % 4).then_inc(chunk_done, 1)
                else:
                    chunk(C_RW + n)
                    for q in range(KD):
                        last = pe.matmul(psum[0:32, 2 + k % 4, 0:T], wide(C_RW + n)[:, q, 0:32], hT3[:, q, :],
                                         start=(q == 0), stop=(q == KD - 1))
                    last.then_inc(chunk_done, 1)
            pe.wait_ge(mqk_ready, 2)
            pe.wait_ge(mms_ready, 4)
            pe.wait_ge(rw_out, N_RW)
            for tt in range(TT):
                nk = (tt + 1) * P
                for b in range(2 * (tt + 1)):
                    par = b // (tt + 1)
                    rows = slice(HD * par, HD * par + HD)
                    hb = 4 // (tt + 1)
                    for i in range(hb):
                        c = (hb * b + i) % 4
                        last = pe.matmul(psum[:, (6, 7, 0, 1, 2, 3)[2 * tt + b], i * nk:(i + 1) * nk],
                                         mqk[rows, c, tt * P:(tt + 1) * P], mqk[rows, 4 + c, 0:nk], start=True, stop=True)
                    last.then_inc(sc_mm, 1)
            for tt, sc in ((0, sc0), (1, sc1)):
                pe.wait_ge(prob_ready, tt + 1)
                if tt == 1:
                    pe.wait_ge(pv_mm, 1)
                    pe.wait_ge(ym_ready, 1)
                pe.wait_ge(sc_read, 6)
                for b in range(2 * (tt + 1)):
                    hb = 4 // (tt + 1)
                    for i in range(hb):
                        for kt in range(tt + 1):
                            at = (i * (tt + 1) + kt) * P
                            last = pe.transpose(psum[:, (0, 1, 4, 5, 6, 7)[2 * tt + b], at:at + P],
                                                sc[:, hb * b + i, kt * P:(kt + 1) * P], ident[:])
                    last.then_inc(pr_mm, 1)
                pe.wait_ge(prT_ready, (2, 6)[tt])
                for par in range(2):
                    for c in range(4):
                        for kt in range(tt + 1):
                            h = 2 * c + par
                            last = pe.matmul(psum[HD * par:HD * par + HD, 2 + tt, c * P:(c + 1) * P],
                                             mv[:, kt, h * HD:(h + 1) * HD], prT[:, 4 * par + c, kt, :],
                                             start=(kt == 0), stop=(kt == tt))
                last.then_inc(pv_mm, 1)
            pe.wait_ge(lora_in, 3)
            pe.wait_ge(ym_ready, TT)
            for i, rows in ((0, slice(0, 64)), (1, slice(64, 128))):
                for c in range(4):
                    last = pe.matmul(psum[:, 2 * i + c // 2, (c % 2) * T:(c % 2) * T + T],
                                     mats[rows, M_LORA + c * P:M_LORA + (c + 1) * P], ps[rows, 12, :],
                                     start=True, stop=True)
                last.then_inc(lora_mm, 1)
            for c in range(4):
                o = psum[:, 4 + c // 2, (c % 2) * T:(c % 2) * T + T]
                pe.matmul(o, mats[:, M_GUP + c * P:M_GUP + (c + 1) * P], ps[:, 13, :], start=True, stop=False)
                last = pe.matmul(o, mats[0:32, M_GUP + W2 + c * P:M_GUP + W2 + (c + 1) * P], ps[0:32, 14, :],
                                 start=False, stop=True)
            last.then_inc(lora_mm, 1)
            pe.wait_ge(ksq_ready, 1)
            for b in range(2):
                last = pe.matmul(psum[:, 6 + b, :], headblk[:], t1[:, 2 * b:2 * b + 2, :].rearrange("p a t -> p (a t)"),
                                 start=True, stop=True)
            last.then_inc(ksum_mm, 1)
            pe.wait_ge(rkk_ready, 4)
            pe.wait_ge(sig_out, 10)
            for b in range(2):
                last = pe.matmul(psum[:, b, :], headblk[:], t2[:, 2 * b:2 * b + 2, :].rearrange("p a t -> p (a t)"),
                                 start=True, stop=True)
            last.then_inc(bon_mm, 1)
            pe.wait_ge(tilde, 1)
            for tt in range(TT):
                ts = slice(tt * P, (tt + 1) * P)
                if tt:
                    pe.wait_ge(ys_out, 2)
                for i, src in enumerate((ar[:, :, 0, :], bt, kt_, v_)):
                    for c in range(4):
                        last = pe.transpose(psum[:, i, c * P:(c + 1) * P], src[:, c, ts], ident[:])
                    last.then_inc(tok_mm, 1)
                for c in range(4):
                    for par in range(2):
                        h = 2 * c + par
                        rows = slice(HD * par, HD * par + HD)
                        if c >= 2:
                            pe.wait_ge(gram_out, 8 * tt + h - 3)
                        for i, src in enumerate((bt, kt_)):
                            last = pe.matmul(psum[:, 4 + 2 * (c % 2) + par, i * 2 * P:(i + 1) * 2 * P], src[rows, c, ts],
                                             ar[rows, c, :, ts], start=True, stop=True)
                        last.then_inc(gram_mm, 1)
                pe.wait_ge(tok_ready, 4 * tt + 4)
                for par in range(2):
                    rows = slice(HD * par, HD * par + HD)
                    for c in range(4):
                        last = pe.matmul(psum[:, 2 + par, c * P:(c + 1) * P], ar[rows, c, 0, ts], bt[rows, c, ts],
                                         start=True, stop=True)
                last.then_inc(nt_mm, 1)
                pe.wait_ge(nt_out, 3 * tt + 3)
                for lv in range(1, 5):
                    s_src = (lambda h: nak[:, h, 0, :]) if lv % 2 else (lambda h: pw_s[:, h, :])
                    t_src, t_dst = (nts, pw_t) if lv % 2 else (pw_t, nts)
                    if lv > 1:
                        pe.wait_ge(ps_out, 6 * tt + 2 * (lv - 1))
                        pe.wait_ge(pt_out, 8 * tt + 2 * (lv - 1))
                    for q in range(2):
                        hs = range(4 * q, 4 * q + 4)
                        for h in hs:
                            last = pe.matmul(psum[:, 2 + q, (h % 4) * P:(h % 4 + 1) * P], s_src(h), t_src[:, h, :],
                                             start=True, stop=True)
                        last.then_inc(pt_mm, 1)
                        if lv < 4:
                            for h in hs:
                                last = pe.matmul(psum[:, q, (h % 4) * P:(h % 4 + 1) * P], t_src[:, h, :], s_src(h),
                                                 start=True, stop=True)
                            last.then_inc(ps_mm, 1)
                    for q in range(2):
                        pe.wait_ge(pt_out, 8 * tt + 2 * (lv - 1) + q + 1)
                        if lv > 1:
                            pe.wait_ge(ix_out, 8 * tt + 2 * (lv - 2) + q + 1)
                        for h in range(4 * q, 4 * q + 4):
                            last = pe.matmul(psum[:, 4 + q, (h % 4) * P:(h % 4 + 1) * P], t_dst[:, h, :], inv[:, h, :],
                                             start=True, stop=True)
                        last.then_inc(ix_mm, 1)
                for h in range(NH):
                    last = pe.matmul(psum[:, 6, h * HD:(h + 1) * HD], nak[:, h, 1, :], tok[:, 3, h * HD:(h + 1) * HD],
                                     start=True, stop=True)
                last.then_inc(wu_mm, 1)
                pe.wait_ge(ix_out, 8 * tt + 8)
                pe.wait_ge(wu_out, 3 * tt + 1)
                for h in range(NH):
                    b = (7, 0)[h // 4]
                    at = (h % 4) * P
                    pe.matmul(psum[:, b, at:at + HD], inv[:, h, :], tok[:, 0, h * HD:(h + 1) * HD], start=True, stop=True)
                    last = pe.matmul(psum[:, b, at + HD:at + P], inv[:, h, :], z2[:, h, :], start=True, stop=True)
                    if h % 4 == 3:
                        last.then_inc(wu_mm, 1)
                pe.wait_ge(wu_out, 3 * tt + 3)
                for par in range(2):
                    for c in range(4):
                        h = 2 * c + par
                        last = pe.matmul(psum[HD * par:HD * par + HD, 0, c * P:(c + 1) * P], nak[:, h, 1, 0:HD],
                                         rbk[:, h, 0, :], start=True, stop=True)
                last.then_inc(q2_mm, 1)
                for par in range(2):
                    for c in range(4):
                        h = 2 * c + par
                        o = psum[HD * par:HD * par + HD, 1, c * P:(c + 1) * P]
                        pe.matmul(o, tok[:, 3, h * HD:(h + 1) * HD], rbk[:, h, 1, :], start=True, stop=False)
                        last = pe.matmul(o, nak[:, h, 1, HD:P], rbk[:, h, 0, :], start=False, stop=True)
                last.then_inc(yp_mm, 1)
                for ch in range(P // CL):
                    rows = slice(CL * ch, CL * ch + CL)
                    for par in range(2):
                        for c in range(4):
                            h = 2 * c + par
                            hs = slice(h * HD, (h + 1) * HD)
                            orow = slice(HD * par, HD * par + HD)
                            pe.matmul(psum[orow, 2 + ch, c * HD:(c + 1) * HD], nak[rows, h, 1, 0:HD], tok[rows, 1, hs],
                                      start=True, stop=True)
                            o = psum[orow, 2 + ch, T + c * HD:T + (c + 1) * HD]
                            pe.matmul(o, tok[rows, 1, hs], nak[rows, h, 1, HD:P], start=True, stop=False)
                            last = pe.matmul(o, tok[rows, 2, hs], tok[rows, 3, hs], start=False, stop=True)
                    last.then_inc(fg_mm, 1)
                for ch in range(P // CL):
                    g = tt * (P // CL) + ch
                    if g == NC - 1:
                        break
                    pe.wait_ge(fg_out, 4 * tt + ch + 1)
                    if g:
                        pe.wait_ge(st_out, g)
                    for c in range(4):
                        last = pe.matmul(psum[:, 6 + g % 2, c * HD:(c + 1) * HD], phi[:, ch, c, :], states[g % 5][:, c, :],
                                         start=True, stop=True)
                    last.then_inc(st_mm, 1)
                pe.wait_ge(q2_out, tt + 1)
                pe.wait_ge(fg_out, 4 * tt + 4)
                if tt:
                    pe.wait_ge(st_out, NC - 1)
                else:
                    pe.wait_ge(st_out, P // CL - 1)
                for par in range(2):
                    rows = slice(HD * par, HD * par + HD)
                    for c in range(4):
                        for ch in range(P // CL):
                            g = tt * (P // CL) + ch
                            at = c * P + ch * CL
                            last = pe.matmul(psum[rows, 4 + par, at:at + CL], states[g % 5][rows, c, :],
                                             qt[rows, c, ch * CL:(ch + 1) * CL], start=True, stop=True)
                    last.then_inc(ys_mm, 1)
            pe.wait_ge(ys_out, 4)
            for i, src in ((0, yT), (1, dsq)):
                if i:
                    pe.wait_ge(ln_sq, 1)
                for b in range(2):
                    pe.matmul(psum[:, 2 * i + b, :], headblk[:], src[:, 2 * b:2 * b + 2, :].rearrange("p a t -> p (a t)"),
                              start=True, stop=True).then_inc(ln_mm, 1)
            pe.wait_ge(y_done, 1)
            for n in range(N_O2):
                chunk(C_O2 + n)
                for tt in range(TT):
                    for k in range(KD):
                        y = yT if k < 4 else ymT
                        last = pe.matmul(psum[:, 2 + n % 4, tt * CW:(tt + 1) * CW], y[:, k % 4, tt * P:(tt + 1) * P],
                                         wide(C_O2 + n)[:, k, :], start=(k == 0), stop=(k == KD - 1))
                last.then_inc(chunk_done, 1)
            turn(3, xn4)
            pe.wait_ge(hT_ready[3], KD)
            for tt in range(TT):
                for k in range(KD):
                    last = pe.matmul(psum[:, 5, tt * NE:(tt + 1) * NE], hT4[:, k, tt * P:(tt + 1) * P],
                                     mats[:, M_ROUTER + k * NE:M_ROUTER + (k + 1) * NE],
                                     start=(k == 0), stop=(k == KD - 1))
            last.then_inc(lg_mm, 1)
            pe.wait_ge(picks_ready, 1)
            pe.matmul(psum[:, 6, 0:NE], before[:], picks[:, 0, :], start=True, stop=True)
            pe.matmul(psum[:, 6, NE:2 * NE], ones[:], picks[:, 0, :], start=True, stop=False)
            pe.matmul(psum[:, 6, NE:2 * NE], before[:], picks[:, 1, :], start=False, stop=True)
            pe.matmul(psum[:, 6, 2 * NE:3 * NE], ones[:], picks[:, 0, :], start=True, stop=False)
            pe.matmul(psum[:, 6, 2 * NE:3 * NE], ones[:], picks[:, 1, :], start=False, stop=True).then_inc(rank_mm, 1)
            pe.wait_ge(loaded_b, 16)
            pe.wait_ge(count_ready, 1)

            def front_gather(f):
                pe.wait_ge(oh_ready, f + 1)
                for tt in range(TT):
                    for h in range(2):
                        last = pe.matmul(psum[CAP * h:CAP * h + CAP, 2, :], oh[:, tt, :], xn4[:, tt, h * 512:(h + 1) * 512],
                                         start=(tt == 0), stop=(tt == TT - 1))
                last.then_inc(g_mm, 1)

            def front_turn(f):
                pe.wait_ge(xs_ready, f + 1)
                for j in range(4):
                    last = pe.transpose(psum[:, 3, j * P:(j + 1) * P], xs[:, j * P:(j + 1) * P], ident[:])
                last.then_inc(xt_mm, 1)

            def experts(p):
                f0 = p * (NE + 1)
                front_gather(f0)
                front_turn(f0)
                with pe.Fori(0, NE) as e:
                    it = p * NE + e
                    f = p * (NE + 1) + e

                    def moe_chunk(j):
                        n = C_MOE + j
                        pe.wait_ge(landed[n % SLOTS], it * 16 + uses(n))
                        return slot(n)

                    pe.wait_ge(xT_ready, f + 1)
                    pe.wait_ge(gu_read, it + 1)
                    for kt in range(GU_CHUNKS):
                        w = moe_chunk(kt)
                        x = xT[:, kt % 4, CAP * (kt // 4):CAP * (kt // 4) + CAP]
                        for gu in range(2):
                            for h in range(2):
                                at = gu * FF + h * 512
                                last = pe.matmul(psum[CAP * h:CAP * h + CAP, gu, :], x, w[:, at:at + 512],
                                                 start=(kt == 0), stop=False, skip_group_check=True)
                        last.then_inc(chunk_done, 1)
                    pe.wait_ge(sel_ready, f + 1)
                    for gu in range(2):
                        last = pe.matmul(psum[:, gu, :], sel_e[0:2 * NE], bmoe[0:2 * NE, gu, :], start=False, stop=True,
                                         skip_group_check=True)
                    pe.wait_ge(ye_ready, it + 1)
                    last = pe.matmul(psum[:, 5, :], sel_e[0:2 * NE], bmoe[0:2 * NE, 2, :], start=True, stop=False,
                                     skip_group_check=True)
                    last.then_inc(gu_mm, 1)
                    pe.wait_ge(sct_ready, it + 1)
                    front_gather(f + 1)
                    pe.wait_ge(act_ready, it + 1)
                    pe.wait_ge(acc_done, it * TT + 1)
                    for j in range(4):
                        last = pe.transpose(psum[:, 4, j * P:(j + 1) * P], ag[:, j * P:(j + 1) * P], ident[:])
                    last.then_inc(at_mm, 1)
                    front_turn(f + 1)
                    pe.wait_ge(actT_ready, it + 1)
                    for q in range(DN_CHUNKS):
                        w = moe_chunk(GU_CHUNKS + q)
                        for i in range(2):
                            kt = 2 * q + i
                            a_in = act_t[:, kt % 4, CAP * (kt // 4):CAP * (kt // 4) + CAP]
                            for h in range(2):
                                last = pe.matmul(psum[CAP * h:CAP * h + CAP, 5, :], a_in,
                                                 w[:, i * D + h * 512:i * D + h * 512 + 512],
                                                 start=False, stop=(kt == KD - 1), skip_group_check=True)
                        if q < DN_CHUNKS - 1:
                            last.then_inc(chunk_done, 1)
                    last.then_inc(y_mm, 1)
                    pe.wait_ge(ohw_ready, it + 1)
                    for tt in range(TT):
                        last = pe.transpose(psum[:, 2, tt * P:(tt + 1) * P], ohw[:, tt, :], ident[:])
                        if tt == 0:
                            last.then_inc(chunk_done, 1)
                    last.then_inc(sct_mm, 1)
                    pe.wait_ge(sct_ready, it + 2)
                    pe.wait_ge(ye_ready, it + 2)
                    pe.wait_ge(xT_ready, f + 2)
                    for tt in range(TT):
                        for h in range(2):
                            rows = slice(CAP * h, CAP * h + CAP)
                            last = pe.matmul(psum[:, (6, 3)[tt] + h, :], sct[rows, tt, :], ye[rows, :],
                                             start=True, stop=True)
                        last.then_inc(sum_mm, 1)

            experts(0)
            further_passes(pe, experts)


def kernel(**inputs):
    from concourse import bacc
    from concourse.bass_utils import run_bass_kernel_spmd

    a = {n: np.asarray(v) for n, v in inputs.items()}
    f = np.float32

    def chunks(w):
        n = w.shape[1] // CW
        return w.reshape(KD, P, n, CW).transpose(2, 1, 0, 3).reshape(n, P, CHUNK)

    def branch(w):
        return w.reshape(4, P, 2, 512).transpose(2, 1, 0, 3).reshape(2, P, CHUNK)

    pool_b, conv_b = branch(a["w_branch_pool"][0]), branch(a["w_branch_conv"][0])
    keys = a["sub_keys"][0].reshape(HP, NK, P).transpose(2, 0, 1).reshape(1, P, CHUNK)
    w2 = a["w_in_2"][0]
    w2 = np.concatenate([w2[:, RW:], w2[:, :RW], np.zeros((D, RWP - RW), f)], axis=1)
    stream = np.concatenate([
        chunks(a["w_in"][0]), pool_b[0:1], conv_b[0:1], pool_b[1:2], conv_b[1:2], chunks(a["w_out"][0]),
        chunks(a["w_q"][0]), keys, chunks(a["w_ada_2"][0]), chunks(w2), chunks(a["w_out_2"][0])])

    def column(v, n):
        v = v.reshape(-1)
        return np.concatenate([v, np.zeros(n * P - v.size, f)]).reshape(n, P).T

    vectors = {
        "g_mix": a["g_mix"], "pool_scale": a["pool_scale"], "conv_w": a["conv_w"], "norm1_g": a["norm1_g_2"],
        "mu": a["rwkv_mu_2"], "w0": a["rwkv_w0_2"], "a0": a["rwkv_a0_2"], "k_k": a["rwkv_k_k_2"],
        "k_a": a["rwkv_k_a_2"], "r_k": a["rwkv_r_k_2"], "ln_g": a["rwkv_ln_g_2"], "ln_b": a["rwkv_ln_b_2"],
        "q_g": np.tile(a["q_norm_g_2"].reshape(-1), 2), "k_g": np.tile(a["k_norm_g_2"].reshape(-1), 2),
        "norm2_g": a["norm2_g_2"], "c": a["c_2"]}
    cols = np.concatenate([column(vectors[n], COLS[n][1]) for n in COLS], axis=1)
    group = a["pool_group_w"][0].transpose(1, 0, 2).reshape(P, 512)
    lora = np.concatenate([a["rwkv_w_up_2"][0], a["rwkv_a_up_2"][0]], axis=0)
    gup = np.concatenate([a["rwkv_g_up_2"][0], np.zeros((2 * P - 160, W2), f)]).reshape(2, P, W2)
    gup = gup.transpose(1, 0, 2).reshape(P, 2 * W2)
    router = a["w_router_2"][0].reshape(KD, P, NE).transpose(1, 0, 2).reshape(P, KD * NE)
    mats = np.concatenate([group, lora, gup, router], axis=1)
    rows = np.concatenate([a["g_ffn"].reshape(-1), a["g_final"].reshape(-1), a["b_router_2"].reshape(-1)])[None]
    bada = a["b_ada_2"].reshape(4, 6 * CW)
    bg = a["b_gate_up_2"][0].reshape(NE, 2, 2, 512).transpose(0, 2, 1, 3).reshape(2 * NE, D)
    bias_moe = np.concatenate([bg, a["b_down_2"][0].reshape(2 * NE, 512)], axis=1)
    arrays = {
        "x": a["x"][0], "stream": stream, "cols": cols, "mats": mats, "rows": rows, "bada": bada,
        "expert_u": a["expert_u"][0], "expert_v": a["expert_v"][0], "w_gate_up": a["w_gate_up_2"][0],
        "w_down": a["w_down_2"][0], "bias_moe": bias_moe}
    arrays = {n: np.ascontiguousarray(v) for n, v in arrays.items()}
    nc = bacc.Bacc("TRN2", target_bir_lowering=False, num_devices=1)
    args = [nc.dram_tensor("in_" + n, v.shape, mybir.dt.from_np(v.dtype), kind="ExternalInput").ap()
            for n, v in arrays.items()]
    out = nc.dram_tensor("out", (T, D), F32, kind="ExternalOutput").ap()
    build(nc, *args, out)
    r = run_bass_kernel_spmd(nc, [{"in_" + n: v for n, v in arrays.items()}], core_ids=[0])
    return r.results[0]["out"].reshape(1, T, D)
```

```python
from contextlib import ExitStack

import numpy as np

import concourse.bass as bass
from concourse import mybir

F32 = mybir.dt.float32
U32 = mybir.dt.uint32
I32 = mybir.dt.int32
ALU = mybir.AluOpType
ACT = mybir.ActivationFunctionType
AX_X = mybir.AxisListType.X

P = 128
D = 1024
T = 256
TT = T // P
KD = D // P
CW = 256
CHUNK = KD * CW
SLOTS = 12

D_IN = 4096
POOL_G = 4
HEADS = 8
HP = 2 * HEADS
NK = 128
TOPK = 16
HK = HEADS * TOPK
NEXP_PEER = NK * NK
EPS = 1e-6
GATHER_SLOTS = 8
PAIR = 2

W2 = 512
RW = 1824
MB = 1536
RWP = 2048
NH = 8
HD = 64
CL = 32
NC = T // CL
LN_EPS = 64e-5
NE = 32
TOPE = 4
CAP = 64
PASSES = T // CAP
FF = 1024
LIMIT = 7.0
ALPHA = 1.702
NEG = -1.0e30
LOWEST = -3.0e38

S_BANK = (0, 1, 6, 7)

SC_BANK = (6, 7, 0, 1, 6, 7)
PR_BANK = (0, 1, 7, 0, 1, 7)

N_Z = D_IN // CW
N_BR = 4
N_O1 = D // CW
N_Q = 2048 // CW
N_KEYS = 1
N_ADA = 6 * D // CW
N_MB = MB // CW
N_RW = RWP // CW
N_O2 = D // CW
C_Z = 0
C_BR = C_Z + N_Z
C_O1 = C_BR + N_BR
C_Q = C_O1 + N_O1
C_KEYS = C_Q + N_Q
C_ADA = C_KEYS + N_KEYS
C_MB = C_ADA + N_ADA
C_RW = C_MB + N_MB
C_O2 = C_RW + N_RW
C_MOE = C_O2 + N_O2
GU_CHUNKS = KD
DN_CHUNKS = 4
E_CHUNKS = GU_CHUNKS + DN_CHUNKS
assert E_CHUNKS == SLOTS

COLS = {}
_at = 0
for _name, _n in (("g_mix", 8), ("pool_scale", 4), ("conv_w", 12), ("norm1_g", 8), ("mu", 16), ("w0", 4),
                  ("a0", 4), ("k_k", 4), ("k_a", 4), ("r_k", 4), ("ln_g", 4), ("ln_b", 4), ("q_g", 1),
                  ("k_g", 1), ("norm2_g", 8), ("c", 8)):
    COLS[_name] = (_at, _n)
    _at += _n
N_COLS = _at
M_GROUP, M_LORA, M_GUP, M_ROUTER = 0, 512, 1024, 2048
N_MATS = M_ROUTER + KD * NE


def build(nc, xd, stream, colsd, matsd, rowsd, badad, expert_u, expert_v, w_gate_up, w_down, bias_moe, out, dbg=None):
    with ExitStack() as ctx:
        def sb(name, shape, dt=F32):
            return ctx.enter_context(nc.sbuf_tensor(name, shape, dt))

        def sem(name):
            return ctx.enter_context(nc.semaphore(name))

        ring = sb("ring", [P, SLOTS, CHUNK])
        xres = sb("xres", [P, TT, D])
        gates = sb("gates", [P, 2, D])
        mats = sb("mats", [P, N_MATS])
        cols = sb("cols", [P, N_COLS])
        modcols = sb("modcols", [P, 4, KD])
        evcols = sb("evcols", [P, 2, KD])
        ident = sb("ident", [P, P])
        ones = sb("ones", [P, P])
        headblk = sb("headblk", [P, P])
        mask_st = sb("mask_st", [P, 2, P])
        mask_ts = sb("mask_ts", [P, P])
        before = sb("before", [P, P])
        iota16 = sb("iota16", [P, TOPK])
        iota_slot = sb("iota_slot", [P, 2 * CAP])
        iota_e = sb("iota_e", [P, NE])
        iota_e2 = sb("iota_e2", [P, NE + 1])
        half_e = sb("half_e", [P, P])
        brow_r = sb("brow_r", [P, NE])
        stat = sb("stat", [P, 8])
        AR = 20480
        arena = sb("arena", [P, AR])
        psum = ctx.enter_context(nc.psum_tensor("psum", [P, 8, 512], F32))

        def area(at, *dims, parts=P):
            n = int(np.prod(dims))
            assert at + n <= AR, (at, dims)
            v = arena[0:parts, at:at + n]
            if len(dims) == 2:
                v = v.rearrange("p (a b) -> p a b", a=dims[0])
            if len(dims) == 3:
                v = v.rearrange("p (a b c) -> p a b c", a=dims[0], b=dims[1])
            return v

        def col(name, i=0):
            at, n = COLS[name]
            assert i < n
            return cols[:, at + i:at + i + 1]

        xn = area(0, TT, D)
        hT = area(2048, KD, T)
        zT = area(4096, 28, T)
        PADW = 16 + T
        u_pad = area(11264, POOL_G, PADW)
        q_a = area(12352, POOL_G, PADW)
        q_b = area(13440, POOL_G, PADW)
        cnt = area(14528, POOL_G, T)
        pT = area(15552, POOL_G, T)
        aT = area(16576, POOL_G, T)
        cv = area(17600, 4, 2 + T)
        cT = area(18632, 4, T)
        mT = area(11264, KD, T)
        gffn = area(14528, D)
        h2 = area(0, TT, D)
        h2T = area(2048, KD, T)
        xn2 = area(4096, TT, D)
        qT = area(8192, TT, HP, P)
        S = area(4096, TT, HP, NK)
        gat = [area(at, D) for at in (8192, 9216, 13312, 19456, 10240, 11264, 2048, 3072)]
        cand = area(12288, PAIR, TOPK * TOPK)
        eq = area(12800, PAIR * TOPK, TOPK)
        brow = area(15552, 6 * CW)
        cb = area(17088, KD, P)
        mrow = area(18112, 2, CW)
        gfin = area(12288, D)
        sm = 18624
        top_s = area(sm, PAIR, 2, TOPK)
        top_i = area(sm + 64, PAIR, 2, TOPK).bitcast(U32)
        top_f = area(sm + 128, PAIR, 2, TOPK)
        fin_s = area(sm + 192, PAIR, TOPK)
        fin_p = area(sm + 224, PAIR, TOPK).bitcast(U32)
        pos_u = area(sm + 256, 2, PAIR * TOPK).bitcast(U32)
        pos_f = area(14336, 2, PAIR * TOPK)
        sel_f = area(14400, 2, PAIR * TOPK)
        stat_c = sb("stat_c", [P, KD])
        gsm = sb("gsm", [P, 4, HEADS])
        peer_g = sb("peer_g", [P, TT, HK])
        peer_i = area(14848, TT, HK).bitcast(U32)
        peer_h = area(15104, TT, HK)
        st_i = sb("st_i", [P, TOPK], U32)
        st_h = sb("st_h", [P, TOPK])

        xn3 = area(2048, TT, D)
        hT3 = area(0, KD, T)
        mqk = area(4096, 2 * 4, T)
        mv = area(6144, TT, W2)
        msq = area(7168, 2 * 4, T)
        mrs = area(9216, 2 * 4, T)
        dist0 = area(11264, P)
        dist1 = area(11392, T)
        sc0 = area(11776, NH, P)
        sc1 = area(12800, NH, T)
        prT = area(7168, NH, TT, P)
        ymT = area(2048, 4, T)
        PT1 = T + 1
        pt = area(16624, 15, PT1)
        ps = area(4096, 15, T)
        r_, k_, v_ = ps[:, 0:4, :], ps[:, 4:8, :], ps[:, 8:12, :]
        wd = area(7936, 4, T)
        aa = area(8960, 4, T)
        gg = area(9984, 4, T)
        kk = area(11008, 4, T)
        t1 = area(12032, 4, T)
        t2 = area(13056, 4, T)
        pc = area(14080, 4, T)
        ar = area(15104, 4, 2, T)
        bt = area(17152, 4, T)
        kt_ = area(18176, 4, T)
        bon = area(19200, 4, T)
        restart = area(3072, T)
        nak = area(0, NH, 2, P)
        pw_s = area(3072, NH, P)
        pw_t = area(4096, NH, P)
        inv = area(5120, NH, P)
        phi = area(3072, P // CL, 4, P)
        gam = area(5120, P // CL, 4, HD)
        tok = area(7168, 4, W2)
        rbk = area(11008, NH, 2, P)
        nts = area(13056, NH, P)
        qt = area(13056, 4, P)
        yT = area(14080, 4, T)
        states = [area(9216 + 256 * i, 4, HD) for i in range(3)]
        states += [mats[:, 256 * i:256 * i + 256].rearrange("p (a b) -> p a b", a=4) for i in range(2)]
        z2 = area(3072, NH, HD)
        dn = area(0, 4, T)
        dsq = area(11008, 4, T)
        drs = area(12032, 4, T)
        ga_t = area(3072, TT, CW)
        xn4 = area(0, TT, D)
        hT4 = area(2048, KD, T)
        acc = area(4096, TT, D)
        xs = area(6144, W2)
        xT = area(6656, 4, P)
        ag = area(7168, 512)
        au = area(7680, 512)
        sg = area(8192, 512)
        act_t = area(8704, 4, P)
        ye = area(9216, 512)
        sct = area(9728, TT, P)
        oh = area(9984, TT, CAP)
        ohw = area(10112, TT, 2 * CAP)
        sel_e = area(10368, P)
        bmoe = area(10496, 3, 512)
        m0 = 12032
        lg = area(m0, TT, NE)
        eqe = area(m0 + 64, TT, NE)
        picks = area(m0 + 128, TT, NE)
        wts = area(m0 + 192, TT, NE)
        rank = area(m0 + 256, TT, NE + 1)
        top8 = area(m0 + 392, TT, 8)
        top8i = area(m0 + 408, TT, 8).bitcast(U32)
        top8f = area(m0 + 424, TT, 8)
        w4 = area(m0 + 440, TT, TOPE)
        wsum = area(m0 + 448, 2, TT)
        most = area(m0 + 452, 1)
        most_i = area(m0 + 453, 1).bitcast(I32)
        mx = gsm[:, 0:2, :]
        pl = peer_g[:, 0, 0:4 * NC].rearrange("p (a b) -> p a b", a=4)

        loaded_x = sem("loaded_x")
        loaded_p = sem("loaded_p")
        loaded_rows = sem("loaded_rows")
        consts = sem("consts")
        const_step = sem("const_step")
        landed = [sem(f"landed{i}") for i in range(SLOTS)]
        chunk_done = sem("chunk_done")
        vec_step = sem("vec_step")
        ms_ready = sem("ms_ready")
        std_ready = sem("std_ready")
        xn_ready = [sem(f"xn_ready{i}") for i in range(4)]
        turned = [sem(f"turned{i}") for i in range(4)]
        hT_ready = [sem(f"hT_ready{i}") for i in range(4)]
        z_out = sem("z_out")
        p_ready = sem("p_ready")
        group_mm = sem("group_mm")
        a_ready = sem("a_ready")
        c_ready = sem("c_ready")
        br_mm = sem("br_mm")
        m_ready = sem("m_ready")
        x_mid = sem("x_mid")
        q_mm = sem("q_mm")
        q_out = sem("q_out")
        s_mm = sem("s_mm")
        s_out = sem("s_out")
        exp_in = sem("exp_in")
        exp_out = sem("exp_out")
        idx_ready = sem("idx_ready")
        staged = sem("staged")
        free_seen = sem("free_seen")
        row_in = [sem(f"row_in{i}") for i in range(GATHER_SLOTS)]
        row_used = sem("row_used")
        head_kept = sem("head_kept")
        dots_done = sem("dots_done")
        gelu_done = sem("gelu_done")
        cb_sig = sem("cb_sig")
        cb_ready = sem("cb_ready")
        ada_out = sem("ada_out")
        mcol_mm = sem("mcol_mm")
        mcol_out = sem("mcol_out")
        ev_ready = sem("ev_ready")
        stored = sem("stored")
        mb_out = sem("mb_out")
        rw_out = sem("rw_out")
        bias_made = sem("bias_made")
        msq_ready = sem("msq_ready")
        msum_mm = sem("msum_mm")
        m_norm = sem("m_norm")
        mqk_ready = sem("mqk_ready")
        sc_mm = sem("sc_mm")
        sc_read = sem("sc_read")
        mexp_in = sem("mexp_in")
        mexp_out = sem("mexp_out")
        prob_ready = sem("prob_ready")
        pr_mm = sem("pr_mm")
        prT_ready = sem("prT_ready")
        pv_mm = sem("pv_mm")
        ym_ready = sem("ym_ready")
        ps_ready = sem("ps_ready")
        lora_in = sem("lora_in")
        lora_mm = sem("lora_mm")
        sig_out = sem("sig_out")
        dec_out = sem("dec_out")
        ksq_ready = sem("ksq_ready")
        ksum_mm = sem("ksum_mm")
        kn_in = sem("kn_in")
        log_ready = sem("log_ready")
        knorm_out = sem("knorm_out")
        rkk_ready = sem("rkk_ready")
        bon_mm = sem("bon_mm")
        tilde = sem("tilde")
        tok_mm = sem("tok_mm")
        tok_ready = sem("tok_ready")
        gram_mm = sem("gram_mm")
        gram_out = sem("gram_out")
        nt_mm = sem("nt_mm")
        nt_out = sem("nt_out")
        ps_mm = sem("ps_mm")
        ps_out = sem("ps_out")
        pt_mm = sem("pt_mm")
        pt_out = sem("pt_out")
        ix_mm = sem("ix_mm")
        ix_out = sem("ix_out")
        wu_mm = sem("wu_mm")
        wu_out = sem("wu_out")
        q2_mm = sem("q2_mm")
        q2_out = sem("q2_out")
        yp_mm = sem("yp_mm")
        yp_out = sem("yp_out")
        fg_mm = sem("fg_mm")
        fg_out = sem("fg_out")
        st_mm = sem("st_mm")
        st_out = sem("st_out")
        ys_mm = sem("ys_mm")
        ys_out = sem("ys_out")
        ln_mm = sem("ln_mm")
        ln_sq = sem("ln_sq")
        ln_norm = sem("ln_norm")
        y_done = sem("y_done")
        router_mm = sem("router_mm")
        wexp_in = sem("wexp_in")
        wexp_out = sem("wexp_out")
        picks_ready = sem("picks_ready")
        count_ready = sem("count_ready")
        loaded_b = sem("loaded_b")
        oh_ready = sem("oh_ready")
        ohw_ready = sem("ohw_ready")
        sel_ready = sem("sel_ready")
        g_mm = sem("g_mm")
        xs_ready = sem("xs_ready")
        xt_mm = sem("xt_mm")
        xT_ready = sem("xT_ready")
        gu_mm = sem("gu_mm")
        xt_scaled = sem("xt_scaled")
        up_ready = sem("up_ready")
        rk_made = sem("rk_made")
        gate_ready = sem("gate_ready")
        gu_read = sem("gu_read")
        sg_ready = sem("sg_ready")
        act_ready = sem("act_ready")
        at_mm = sem("at_mm")
        actT_ready = sem("actT_ready")
        y_mm = sem("y_mm")
        ye_ready = sem("ye_ready")
        sct_mm = sem("sct_mm")
        sct_ready = sem("sct_ready")
        sum_mm = sem("sum_mm")
        acc_done = sem("acc_done")
        out_ready = sem("out_ready")

        def uses(n):
            return 16 * (n // SLOTS + 1)

        def slot(n):
            return ring[:, n % SLOTS, :]

        def wide(n):
            return slot(n).rearrange("p (k c) -> p k c", k=KD)

        def further_passes(eng, work):
            eng.wait_ge(count_ready, 1)
            count = eng.value_load(most_i[0:1, 0:1], min_val=0, max_val=T)
            with eng.Fori(1, PASSES) as p:
                with eng.If(count > p * CAP):
                    work(p)

        block = ctx.enter_context(nc.Block())

        @block.sync
        def _(sp):
            sp.dma_start(xres[:], xd.rearrange("(a p) d -> p a d", p=P)).then_inc(loaded_x, 16)
            for j in range(SLOTS):
                sp.dma_start(ring[:, j, :], stream[j]).then_inc(landed[j], 16)
            whole = C_MOE // SLOTS
            with sp.Fori(1, whole) as i:
                for j in range(SLOTS):
                    sp.wait_ge(chunk_done, i * SLOTS + (j - SLOTS + 1))
                    sp.dma_start(ring[:, j, :], stream[i * SLOTS + j]).then_inc(landed[j], 16)
            for n in range(whole * SLOTS, C_MOE):
                sp.wait_ge(chunk_done, n - SLOTS + 1)
                sp.dma_start(slot(n), stream[n]).then_inc(landed[n % SLOTS], 16)

            def experts(p):
                with sp.Fori(0, NE) as e:
                    for j in range(E_CHUNKS):
                        n = C_MOE + j
                        sp.wait_ge(chunk_done, e * E_CHUNKS + (p * (NE * E_CHUNKS) + (n - SLOTS + 1)))
                        if j < GU_CHUNKS:
                            src = w_gate_up[e, j * P:(j + 1) * P, :]
                            dst = slot(n)
                        else:
                            q = j - GU_CHUNKS
                            src = w_down[e, q * 2 * P:(q + 1) * 2 * P, :].rearrange("(k p) c -> p k c", p=P)
                            dst = slot(n).rearrange("p (k c) -> p k c", k=2)
                        sp.dma_start(dst, src).then_inc(landed[n % SLOTS], 16)

            experts(0)
            further_passes(sp, experts)
            sp.wait_ge(out_ready, TT)
            sp.dma_start(out.rearrange("(a p) d -> p a d", p=P), xres[:]).then_inc(stored, 16)
            sp.wait_ge(stored, 16)

        @block.gpsimd
        def _(pool):
            made = [0]

            def make(ins):
                made[0] += 1
                ins.then_inc(const_step, 1)
                pool.wait_ge(const_step, made[0])

            def number(out, pattern, base=0, by_row=0):
                return pool.iota(out, pattern, base=base, channel_multiplier=by_row,
                                 allow_small_or_imprecise_dtypes=True)

            def keep(m, src, pattern, op, base=0, by_row=0):
                return pool.affine_select(out=m, in_=src, compare_op=op, fill=0.0, base=base, pattern=pattern,
                                          channel_multiplier=by_row)

            make(pool.memset(ident[:], 0.0))
            make(pool.memset(ones[:], 1.0))
            make(pool.affine_select(out=ident[:], in_=ident[:], compare_op=ALU.not_equal, fill=1.0, base=0,
                                    pattern=[[-1, P]], channel_multiplier=1))
            make(number(cnt, [[0, POOL_G], [1, T]], base=1))
            make(number(iota16[:], [[1, TOPK]]))
            make(pool.memset(stat[:, 6:7], EPS))
            make(pool.memset(stat[:, 7:8], LN_EPS))
            make(number(iota_slot[:], [[0, 2], [1, CAP]]))
            make(number(iota_e[:], [[1, NE]]))
            make(number(iota_e2[:], [[2, NE + 1]]))
            make(number(half_e[0:2 * NE, :], [[-1, 2], [0, CAP]], by_row=1))
            hb = headblk[:].rearrange("p (b c) -> p b c", b=2)
            make(keep(hb, ones[:].rearrange("p (b c) -> p b c", b=2), [[-HD, 2], [0, HD]], ALU.is_ge, by_row=1))
            make(keep(hb, hb, [[HD, 2], [0, HD]], ALU.is_ge, base=HD - 1, by_row=-1))
            make(keep(before[:], ones[:], [[1, P]], ALU.is_gt, by_row=-1))
            in_chunks = [[-CL, P // CL], [0, CL]]
            for m, op in ((0, ALU.is_gt), (1, ALU.is_ge)):
                mm = mask_st[:, m, :]
                make(keep(mm, ones[:], [[1, P]], op, by_row=-1))
                mm = mm.rearrange("p (b c) -> p b c", c=CL)
                make(keep(mm, mm, in_chunks, ALU.is_ge, by_row=1))
            mm = mask_ts[:]
            make(keep(mm, ones[:], [[-1, P]], ALU.is_gt, by_row=1))
            mm = mm.rearrange("p (b c) -> p b c", c=CL)
            make(keep(mm, mm, [[CL, P // CL], [0, CL]], ALU.is_ge, base=CL - 1, by_row=-1))
            pool.sem_inc(consts, 1)

            def gather(table, tt, first):
                with pool.Fori(0, HEADS) as i:
                    for q in range(TOPK // GATHER_SLOTS):
                        at = q * GATHER_SLOTS
                        pool.wait_ge(idx_ready, i + (tt * HEADS + 1))
                        pool.sem_inc(free_seen, 1)
                        pool.tensor_copy(st_i[:, at:at + GATHER_SLOTS],
                                         peer_i[:, tt, bass.ds(i * TOPK + at, GATHER_SLOTS)]).then_inc(staged, 1)
                        pool.wait_ge(staged, i * (TOPK // GATHER_SLOTS) + (first // GATHER_SLOTS + q + 1))
                        for k in range(GATHER_SLOTS):
                            if k == GATHER_SLOTS // 2:
                                pool.wait_ge(s_mm, TT * HP // 4)
                            pool.wait_ge(row_used, i * TOPK + (first + at + k + 1))
                            pool.sem_inc(free_seen, 1)
                            pool.indirect_dma_start(gat[k], None, table,
                                                    bass.IndirectOffsetOnAxis(st_i[:, at + k:at + k + 1], 0)
                                                    ).then_inc(row_in[k], 16)

            for n, (table, tt) in enumerate(((expert_u, 0), (expert_v, 0), (expert_u, 1), (expert_v, 1))):
                gather(table, tt, n * HK)
            pool.wait_ge(xn_ready[2], TT)
            at = made[0]
            for tt, m in ((0, dist0), (1, dist1)):
                n = m.shape[-1]
                make(number(m, [[1, n]], base=-tt * P, by_row=-1))
                make(pool.affine_select(out=m, in_=m, compare_op=ALU.is_ge, fill=NEG, base=tt * P,
                                        pattern=[[-1, n]], channel_multiplier=1))
            for sc, m in ((sc0, dist0), (sc1, dist1)):
                for par in range(2):
                    for c in range(4):
                        pool.tensor_scalar(sc[:, 4 * par + c, :], m, 2.0 ** -(2 * c + par + 1), None,
                                           ALU.mult).then_inc(bias_made, 1)

        @block.scalar
        def _(act):
            act.dma_start(cols[:], colsd).then_inc(loaded_p, 16)
            act.dma_start(mats[:], matsd).then_inc(loaded_p, 16)
            act.dma_start(brow_r[:], rowsd[:, 2 * D:2 * D + NE].to_broadcast([P, NE])).then_inc(loaded_p, 16)

            def deviation(n):
                act.wait_ge(ms_ready, 2 * (n + 1))
                act.activation(stat[:, 2:4], stat[:, 0:2], ACT.Sqrt).then_inc(std_ready, 1)

            def turn_out(n, dst, scale=None, bias=None):
                for k in range(KD):
                    act.wait_ge(turned[n], k + 1)
                    src = psum[:, k % 4, 0:T]
                    if scale is None:
                        act.copy(dst[:, k, :], src).then_inc(hT_ready[n], 1)
                    elif bias is None:
                        act.activation(dst[:, k, :], src, ACT.Copy, scale=scale(k)).then_inc(hT_ready[n], 1)
                    else:
                        act.activation(dst[:, k, :], src, ACT.Identity, scale=scale(k),
                                       bias=bias(k)).then_inc(hT_ready[n], 1)

            act.sem_inc(ye_ready, 1)
            act.sem_inc(sct_ready, 1)
            act.wait_ge(loaded_p, 48)
            deviation(0)
            turn_out(0, hT, lambda k: col("g_mix", k))
            for n in range(N_Z):
                act.wait_ge(chunk_done, C_Z + n + 1)
                src = psum[:, 2 + n % 4, :].rearrange("p (a t) -> p a t", a=2)
                if n < 2:
                    act.copy(u_pad[:, 2 * n:2 * n + 2, 16:16 + T], src).then_inc(z_out, 1)
                elif n < 8:
                    act.copy(zT[:, 2 * n - 4:2 * n - 2, :], src).then_inc(z_out, 1)
                else:
                    act.activation(zT[:, 2 * n - 4:2 * n - 2, :], src, ACT.Sigmoid).then_inc(z_out, 1)
            act.wait_ge(group_mm, 1)
            for g in range(POOL_G):
                act.activation(aT[:, g, :], psum[:, 6 + g // 2, (g % 2) * T:(g % 2) * T + T], ACT.Copy,
                               scale=col("pool_scale", g)).then_inc(a_ready, 1)
            act.wait_ge(m_ready, KD)
            act.activation(modcols[:, 0, :], cols[:, COLS["c"][0]:COLS["c"][0] + KD], ACT.Sigmoid).then_inc(cb_sig, 1)
            act.dma_start(gffn, rowsd[:, 0:D].to_broadcast([P, D])).then_inc(loaded_rows, 16)
            act.dma_start(brow[0:97:32, :], badad).then_inc(loaded_rows, 16)
            deviation(1)
            turn_out(1, h2T)
            for tt in range(TT):
                for m in range(HP // 4):
                    if tt == 0:
                        act.wait_ge(q_mm, m + 1)
                    else:
                        act.wait_ge(chunk_done, C_Q + 2 * m + 2)
                    act.copy(qT[:, tt, 4 * m:4 * m + 4, :],
                             psum[:, 2 + m, :].rearrange("p (a t) -> p a t", a=4)).then_inc(q_out, 1)
                for m in range(HP // 4):
                    act.wait_ge(s_mm, tt * (HP // 4) + m + 1)
                    act.copy(S[:, tt, 4 * m:4 * m + 4, :],
                             psum[:, S_BANK[m], :].rearrange("p (a c) -> p a c", a=4)).then_inc(s_out, 1)

            def mod_chunk(n):
                act.wait_ge(chunk_done, C_ADA + n + 1)
                part, at = n // 4, (n % 4) * CW
                src = psum[:, 4 + n % 2, 0:CW]
                if part in (2, 5):
                    act.copy(gates[:, part // 3, at:at + CW], src).then_inc(ada_out, 1)
                else:
                    w = part if part < 2 else part - 1
                    act.copy(mrow[0:1, n % 2, :], src[0:1]).then_inc(ada_out, 1)
                    m = sum(1 for x in range(n) if x // 4 not in (2, 5))
                    act.wait_ge(mcol_mm, m + 1)
                    act.copy(modcols[:, w, 2 * (n % 4):2 * (n % 4) + 2], psum[:, 6, 0:2]).then_inc(mcol_out, 1)

            act.wait_ge(cb_ready, KD)
            for n in range(N_ADA):
                mod_chunk(n)
            for tt in range(TT):
                act.wait_ge(exp_in, (tt + 1) * (HEADS // PAIR))
                act.activation(peer_g[:, tt, :], peer_g[:, tt, :], ACT.Exp).then_inc(exp_out, 1)
                act.wait_ge(dots_done, tt + 1)
                act.activation(peer_h[:, tt, :], peer_h[:, tt, :], ACT.Gelu).then_inc(gelu_done, 1)
            act.wait_ge(idx_ready, TT * HEADS)
            act.dma_start(gfin, rowsd[:, D:2 * D].to_broadcast([P, D])).then_inc(loaded_rows, 16)
            deviation(2)
            deviation(3)
            act.wait_ge(ev_ready, 2)
            turn_out(2, hT3, lambda k: evcols[:, 0, k:k + 1], lambda k: modcols[:, 0, k:k + 1])
            def mb_copy(n):
                act.wait_ge(chunk_done, C_MB + n + 1)
                src = psum[:, 2 + n % 4, :].rearrange("p (a t) -> p a t", a=2)
                dst = mqk[:, 2 * n:2 * n + 2, :] if n < 4 else mv[:, :, (n - 4) * CW:(n - 3) * CW]
                act.copy(dst, src).then_inc(mb_out, 1)

            def rw_copy(n):
                act.wait_ge(chunk_done, C_RW + n + 1)
                src = psum[:, 2 + (N_MB + n) % 4, :].rearrange("p (a t) -> p a t", a=2)
                if n < N_RW - 1:
                    act.copy(pt[:, 2 * n:2 * n + 2, 1:], src).then_inc(rw_out, 1)
                else:
                    act.copy(pt[0:32, 14, 1:], src[0:32, 0, :]).then_inc(rw_out, 1)

            def weights(tt, sc):
                act.wait_ge(mexp_in, tt + 1)
                act.activation(sc, sc, ACT.Exp).then_inc(mexp_out, 1)

            def turned_weights(i):
                act.wait_ge(pr_mm, i + 1)
                src = psum[:, PR_BANK[i], :]
                if i < 2:
                    act.copy(prT[:, 4 * i:4 * i + 4, 0, :], src.rearrange("p (a t) -> p a t", a=4)).then_inc(prT_ready, 1)
                else:
                    act.copy(prT[:, 2 * i - 4:2 * i - 2, :, :],
                             src.rearrange("p (a b t) -> p a b t", a=2, b=2)).then_inc(prT_ready, 1)

            def attended(tt):
                act.wait_ge(pv_mm, tt + 1)
                act.copy(ymT[:, :, tt * P:(tt + 1) * P],
                         psum[:, 6, :].rearrange("p (a t) -> p a t", a=4)).then_inc(ym_ready, 1)

            for n in range(5):
                mb_copy(n)
            for b in range(4):
                act.wait_ge(msum_mm, b + 1)
                act.activation(mrs[:, 2 * b:2 * b + 2, :], psum[:, (6, 7, 0, 1)[b], :].rearrange("p (a t) -> p a t", a=2),
                               ACT.Ln, scale=1.0 / HD, bias=stat[:, 6:7]).then_inc(m_norm, 1)
            for i in range(2):
                act.wait_ge(m_norm, 2 * i + 2)
                act.activation(mrs[:, 4 * i:4 * i + 4, :], mrs[:, 4 * i:4 * i + 4, :], ACT.Exp,
                               scale=-0.5).then_inc(m_norm, 1)
            mb_copy(5)
            rw_copy(0)
            weights(0, sc0)
            rw_copy(1)
            rw_copy(2)
            weights(1, sc1)
            turned_weights(0)
            turned_weights(1)
            rw_copy(3)
            attended(0)
            for i in range(2, 5):
                turned_weights(i)
            rw_copy(4)
            turned_weights(5)
            rw_copy(5)
            attended(1)
            rw_copy(6)
            rw_copy(7)
            act.wait_ge(ps_ready, 1)
            act.activation(ps[0:64, 12, :], ps[0:64, 12, :], ACT.Tanh).then_inc(lora_in, 1)
            act.activation(ps[:, 13, :], ps[:, 13, :], ACT.Sigmoid).then_inc(lora_in, 1)
            act.activation(ps[0:32, 14, :], ps[0:32, 14, :], ACT.Sigmoid).then_inc(lora_in, 1)
            for i, dst, bias in ((0, wd, "w0"), (1, aa, "a0")):
                act.wait_ge(lora_mm, i + 1)
                for c in range(4):
                    src = psum[:, 2 * i + c // 2, (c % 2) * T:(c % 2) * T + T]
                    act.activation(dst[:, c, :], src, ACT.Sigmoid, bias=col(bias, c)).then_inc(sig_out, 1)
            act.wait_ge(lora_mm, 3)
            for b in range(2):
                act.copy(gg[:, 2 * b:2 * b + 2, :],
                         psum[:, 4 + b, :].rearrange("p (a t) -> p a t", a=2)).then_inc(sig_out, 1)
            act.wait_ge(kn_in, 2)
            act.activation(t1, t1, ACT.Ln).then_inc(knorm_out, 1)
            act.wait_ge(knorm_out, 1)
            act.activation(t1, t1, ACT.Exp, scale=-0.5).then_inc(knorm_out, 1)
            c = float(np.exp(-0.5))
            act.wait_ge(log_ready, 1)
            act.activation(bt, pc, ACT.Exp, scale=c).then_inc(dec_out, 1)
            act.wait_ge(dec_out, 1)
            act.activation(pc, pc, ACT.Exp, scale=-c).then_inc(dec_out, 1)
            act.activation(wd, wd, ACT.Exp, scale=-c).then_inc(dec_out, 1)
            for tt in range(TT):
                for i in range(0, 4, 2):
                    act.wait_ge(tok_mm, 4 * tt + i + 1)
                    act.copy(tok[:, i, :], psum[:, i, :]).then_inc(tok_ready, 1)
                for lv in range(1, 5):
                    dst = (nts, pw_t)[lv % 2]
                    for q in range(2):
                        act.wait_ge(pt_mm, 8 * tt + 2 * (lv - 1) + q + 1)
                        act.copy(dst[:, 4 * q:4 * q + 4, :],
                                 psum[:, 2 + q, :].rearrange("p (a t) -> p a t", a=4)).then_inc(pt_out, 1)
                act.wait_ge(yp_mm, tt + 1)
                act.copy(yT[:, :, tt * P:(tt + 1) * P],
                         psum[:, 1, :].rearrange("p (a t) -> p a t", a=4)).then_inc(yp_out, 1)
            for b in range(2):
                act.wait_ge(ln_mm, 3 + b)
                act.activation(drs[:, 2 * b:2 * b + 2, :], psum[:, 2 + b, :].rearrange("p (a t) -> p a t", a=2),
                               ACT.Ln, scale=1.0 / HD, bias=stat[:, 7:8]).then_inc(ln_norm, 1)
            act.wait_ge(ln_norm, 2)
            act.activation(drs, drs, ACT.Exp, scale=-0.5).then_inc(ln_norm, 1)
            deviation(4)
            turn_out(3, hT4, lambda k: evcols[:, 1, k:k + 1], lambda k: modcols[:, 2, k:k + 1])
            act.dma_start(bmoe[0:2 * NE], bias_moe.rearrange("r (a c) -> r a c", a=3)).then_inc(loaded_b, 16)
            act.wait_ge(wexp_in, 1)
            act.activation(w4, w4, ACT.Exp).then_inc(wexp_out, 1)

            def front(f):
                act.wait_ge(g_mm, f + 2)
                act.copy(xs, psum[:, 2, :]).then_inc(xs_ready, 1)

            def experts(p):
                front(p * (NE + 1))
                with act.Fori(0, NE) as e:
                    it = p * NE + e
                    f = p * (NE + 1) + e
                    act.wait_ge(gate_ready, it + 1)
                    act.activation(sg, ag, ACT.Sigmoid, scale=ALPHA).then_inc(sg_ready, 1)
                    front(f + 1)
                    act.wait_ge(at_mm, it + 1)
                    act.copy(act_t, psum[:, 4, :].rearrange("p (a t) -> p a t", a=4)).then_inc(actT_ready, 1)
                    act.wait_ge(y_mm, it + 1)
                    act.copy(ye, psum[:, 5, :]).then_inc(ye_ready, 1)
                    act.wait_ge(sct_mm, it + 2)
                    act.copy(sct, psum[:, 2, 0:2 * P].rearrange("p (a t) -> p a t", a=2)).then_inc(sct_ready, 1)

            experts(0)
            further_passes(act, experts)

        @block.vector
        def _(dve):
            steps = [0]

            def ordered(ins):
                steps[0] += 1
                ins.then_inc(vec_step, 1)
                dve.wait_ge(vec_step, steps[0])

            def norm(n, dst, src):
                for tt in range(TT):
                    dve.tensor_tensor_reduce(dst[:, tt, :], src[:, tt, :], src[:, tt, :], 1.0 / D, EPS,
                                             ALU.mult, ALU.add, stat[:, tt:tt + 1]).then_inc(ms_ready, 1)
                dve.wait_ge(std_ready, n + 1)
                ordered(dve.reciprocal(stat[:, 4:6], stat[:, 2:4]))
                dve.wait_ge(ms_ready, 2 * (n + 1))

            dve.sem_inc(row_used, GATHER_SLOTS)
            dve.sem_inc(gu_read, 1)
            dve.sem_inc(acc_done, 1)
            dve.memset(u_pad[:, :, 0:16], 0.0)
            dve.memset(q_a[:, :, 0:16], 0.0)
            dve.memset(q_b[:, :, 0:16], 0.0)
            ordered(dve.memset(cv[:, :, 0:2], 0.0))
            dve.wait_ge(loaded_x, 16)
            norm(0, xn, xres)
            for tt in range(TT):
                dve.tensor_scalar(xn[:, tt, :], xres[:, tt, :], stat[:, 4 + tt:5 + tt], None,
                                  ALU.mult).then_inc(xn_ready[0], 1)
            dve.wait_ge(consts, 1)
            for g in range(POOL_G):
                dve.tensor_scalar(cnt[:, g, :], cnt[:, g, :], float(2 << g), None, ALU.min).then_inc(vec_step, 1)
            steps[0] += POOL_G
            dve.wait_ge(vec_step, steps[0])
            ordered(dve.reciprocal(cnt, cnt))
            dve.wait_ge(z_out, 2)
            ordered(dve.tensor_tensor(q_a[:, :, 16:], u_pad[:, :, 16:], u_pad[:, :, 15:15 + T], ALU.add))
            ordered(dve.tensor_tensor(q_b[:, 1:, 16:], q_a[:, 1:, 16:], q_a[:, 1:, 14:14 + T], ALU.add))
            ordered(dve.tensor_tensor(q_a[:, 2:, 16:], q_b[:, 2:, 16:], q_b[:, 2:, 12:12 + T], ALU.add))
            ordered(dve.tensor_tensor(q_b[:, 3:, 16:], q_a[:, 3:, 16:], q_a[:, 3:, 8:8 + T], ALU.add))
            dve.tensor_tensor(pT[:, 0:4:2, :], q_a[:, 0:4:2, 16:], cnt[:, 0:4:2, :], ALU.mult).then_inc(vec_step, 1)
            steps[0] += 1
            ordered(dve.tensor_tensor(pT[:, 1:4:2, :], q_b[:, 1:4:2, 16:], cnt[:, 1:4:2, :], ALU.mult))
            dve.tensor_tensor(pT, pT, u_pad[:, :, 16:], ALU.subtract).then_inc(p_ready, 1)
            dve.wait_ge(z_out, 8)
            ordered(dve.tensor_tensor(cv[:, :, 2:], zT[:, 0:4, :], zT[:, 8:12, :], ALU.mult))
            for t in range(4):
                dve.tensor_scalar(cT[:, t, :], cv[:, t, 0:T], col("conv_w", t), None, ALU.mult).then_inc(vec_step, 1)
            steps[0] += 4
            dve.wait_ge(vec_step, steps[0])
            for w in (1, 2):
                for t in range(4):
                    dve.scalar_tensor_tensor(cT[:, t, :], cv[:, t, w:w + T], col("conv_w", 4 * w + t), cT[:, t, :],
                                             ALU.mult, ALU.add).then_inc(vec_step, 1)
                steps[0] += 4
                dve.wait_ge(vec_step, steps[0])
            dve.tensor_tensor(cT, cT, zT[:, 4:8, :], ALU.mult).then_inc(c_ready, 1)
            dve.wait_ge(z_out, N_Z)
            dve.wait_ge(p_ready, 1)
            for k in range(KD):
                dve.wait_ge(br_mm, k + 1)
                ab = psum[:, 2 + k % 4, :].rearrange("p (a t) -> p a t", a=2)
                ga = zT[:, 12 + k, :]
                gb = zT[:, 20 + k, :]
                dve.tensor_tensor(ga, ab[:, 0, :], ga, ALU.mult).then_inc(vec_step, 1)
                steps[0] += 1
                ordered(dve.tensor_tensor(gb, ab[:, 1, :], gb, ALU.mult))
                dve.tensor_tensor(mT[:, k, :], ga, gb, ALU.add).then_inc(m_ready, 1)
            for n in range(N_O1):
                dve.wait_ge(chunk_done, C_O1 + n + 1)
                dve.tensor_tensor(xres[:, :, n * CW:(n + 1) * CW],
                                  psum[:, 2 + n % 4, :].rearrange("p (a c) -> p a c", a=TT),
                                  xres[:, :, n * CW:(n + 1) * CW], ALU.add).then_inc(x_mid, 1)
            dve.wait_ge(x_mid, N_O1)
            norm(1, xn2, xres)
            dve.wait_ge(loaded_rows, 32)
            for tt in range(TT):
                ordered(dve.tensor_scalar(xn2[:, tt, :], xres[:, tt, :], stat[:, 4 + tt:5 + tt], None, ALU.mult))
                dve.tensor_tensor(h2[:, tt, :], xn2[:, tt, :], gffn, ALU.mult).then_inc(xn_ready[1], 1)
            dve.wait_ge(cb_sig, 1)
            at = COLS["c"][0]
            ordered(dve.tensor_tensor(stat_c[:], cols[:, at:at + KD], modcols[:, 0, :], ALU.mult))
            for k in range(KD):
                dve.tensor_scalar(cb[:, k, :], ones[:], stat_c[:, k:k + 1], None, ALU.mult).then_inc(cb_ready, 1)

            def top16(n, val, ind, of):
                for r in range(2):
                    for i in range(n):
                        dve.max(val(i, r), of(i)).then_inc(vec_step, 1)
                    steps[0] += n
                    dve.wait_ge(vec_step, steps[0])
                    for i in range(n):
                        dve.max_index(ind(i, r), val(i, r), of(i)).then_inc(vec_step, 1)
                    steps[0] += n
                    dve.wait_ge(vec_step, steps[0])
                    if r == 0:
                        for i in range(n):
                            dve.match_replace(of(i), val(i, r), of(i), LOWEST).then_inc(vec_step, 1)
                        steps[0] += n
                        dve.wait_ge(vec_step, steps[0])

            def select_keys(tt, pair):
                top16(2 * PAIR, lambda i, r: top_s[:, i // 2, i % 2, 8 * r:8 * r + 8],
                      lambda i, r: top_i[:, i // 2, i % 2, 8 * r:8 * r + 8], lambda i: S[:, tt, 2 * PAIR * pair + i, :])

            def select_experts(tt, pair):
                c4 = cand.rearrange("p h (a b) -> p h a b", a=TOPK)
                shape = [P, PAIR, TOPK, TOPK]
                ordered(dve.tensor_tensor(c4, top_s[:, :, 0, :].unsqueeze(3).to_broadcast(shape),
                                          top_s[:, :, 1, :].unsqueeze(2).to_broadcast(shape), ALU.add))
                top16(PAIR, lambda i, r: fin_s[:, i, 8 * r:8 * r + 8], lambda i, r: fin_p[:, i, 8 * r:8 * r + 8],
                      lambda i: cand[:, i, :])
                at = slice(PAIR * pair * TOPK, PAIR * (pair + 1) * TOPK)
                dve.tensor_tensor(peer_g[:, tt, at].rearrange("p (h k) -> p h k", h=PAIR), fin_s,
                                  fin_s[:, :, 0:1].to_broadcast([P, PAIR, TOPK]), ALU.subtract).then_inc(exp_in, 1)
                flat_p = fin_p.rearrange("p h k -> p (h k)")
                ordered(dve.tensor_copy(top_f, top_i))
                ordered(dve.tensor_scalar(pos_u[:, 0, :], flat_p, 4, None, ALU.logical_shift_right))
                ordered(dve.tensor_scalar(pos_u[:, 1, :], flat_p, 15, None, ALU.bitwise_and))
                ordered(dve.tensor_copy(pos_f, pos_u))
                sh = [P, PAIR * TOPK, TOPK]
                for half in range(2):
                    ordered(dve.tensor_tensor(eq, pos_f[:, half, :].unsqueeze(2).to_broadcast(sh),
                                              iota16[:].unsqueeze(1).to_broadcast(sh), ALU.is_equal))
                    e4 = eq.rearrange("p (h k) a -> p h k a", h=PAIR)
                    ordered(dve.tensor_tensor(e4, e4, top_f[:, :, half, :].unsqueeze(2).to_broadcast(shape), ALU.mult))
                    ordered(dve.tensor_reduce(sel_f[:, half, :], eq, AX_X, ALU.add))
                ordered(dve.scalar_tensor_tensor(sel_f[:, 0, :], sel_f[:, 0, :], float(NK), sel_f[:, 1, :],
                                                 ALU.mult, ALU.add))
                dve.tensor_copy(peer_i[:, tt, at], sel_f[:, 0, :]).then_inc(idx_ready, PAIR)

            def arrivals(i, first, k):
                return i * (16 * TOPK // GATHER_SLOTS) + 16 * ((first + k) // GATHER_SLOTS + 1)

            def dots(tt, pair):
                h0 = 2 * tt * HEADS + PAIR * pair
                first = h0 * TOPK
                with dve.Fori(0, PAIR) as i:
                    for k in range(TOPK):
                        dve.wait_ge(row_in[k % GATHER_SLOTS], arrivals(i, first, k))
                        g = gat[k % GATHER_SLOTS]
                        dve.tensor_tensor_reduce(g, g, h2[:, tt, :], 1.0, 0.0, ALU.mult, ALU.add,
                                                 st_h[:, k:k + 1]).then_inc(row_used, 1)
                    dve.wait_ge(row_used, i * TOPK + (first + TOPK + GATHER_SLOTS))
                    dve.tensor_copy(peer_h[:, tt, bass.ds(i * TOPK + PAIR * pair * TOPK, TOPK)],
                                    st_h[:]).then_inc(head_kept, 1)
                    dve.wait_ge(head_kept, i + (h0 + 1))

            def weights(tt):
                dve.wait_ge(exp_out, tt + 1)
                g3 = peer_g[:, tt, :].rearrange("p (h k) -> p h k", h=HEADS)
                ordered(dve.tensor_reduce(gsm[:, tt, :], g3, AX_X, ALU.add))
                ordered(dve.reciprocal(gsm[:, 2 + tt, :], gsm[:, tt, :]))
                ordered(dve.tensor_tensor(g3, g3, gsm[:, 2 + tt, :].unsqueeze(2).to_broadcast([P, HEADS, TOPK]),
                                          ALU.mult))
                dve.wait_ge(gelu_done, tt + 1)
                ordered(dve.tensor_tensor(peer_h[:, tt, :], peer_h[:, tt, :], peer_g[:, tt, :], ALU.mult))

            def weighted(tt, pair):
                h0 = (2 * tt + 1) * HEADS + PAIR * pair
                first = h0 * TOPK
                with dve.Fori(0, PAIR) as i:
                    dve.tensor_copy(st_h[:], peer_h[:, tt, bass.ds(i * TOPK + PAIR * pair * TOPK, TOPK)]
                                    ).then_inc(head_kept, 1)
                    dve.wait_ge(head_kept, i + (h0 + 1))
                    for k in range(TOPK):
                        dve.wait_ge(row_in[k % GATHER_SLOTS], arrivals(i, first, k))
                        dve.scalar_tensor_tensor(xres[:, tt, :], gat[k % GATHER_SLOTS], st_h[:, k:k + 1],
                                                 xres[:, tt, :], ALU.mult, ALU.add).then_inc(row_used, 1)
                        dve.wait_ge(row_used, i * TOPK + (first + k + 1 + GATHER_SLOTS))

            def select(tt, pair):
                select_keys(tt, pair)
                select_experts(tt, pair)

            dve.wait_ge(s_out, HP // 4)
            select(0, 0)
            select(0, 1)
            dots(0, 0)
            select(0, 2)
            select(0, 3)
            dots(0, 1)
            dve.wait_ge(s_out, TT * HP // 4)
            select(1, 0)
            dots(0, 2)
            select(1, 1)
            dots(0, 3)
            dve.sem_inc(dots_done, 1)
            weights(0)
            for pair in range(HEADS // PAIR):
                weighted(0, pair)
                (select_keys, select_experts)[pair % 2](1, 2 + pair // 2)
            for pair in range(HEADS // PAIR):
                dots(1, pair)
            dve.sem_inc(dots_done, 1)
            weights(1)
            for pair in range(HEADS // PAIR):
                weighted(1, pair)
            norm(2, h2, xres)
            dve.wait_ge(loaded_rows, 48)
            for tt in range(TT):
                ordered(dve.tensor_scalar(xres[:, tt, :], xres[:, tt, :], stat[:, 4 + tt:5 + tt], None, ALU.mult))
                ordered(dve.tensor_tensor(xres[:, tt, :], xres[:, tt, :], gfin, ALU.mult))
            dve.wait_ge(mcol_out, 16)
            for i, name in ((0, "norm1_g"), (1, "norm2_g")):
                at, n = COLS[name]
                dve.scalar_tensor_tensor(evcols[:, i, :], modcols[:, 2 * i + 1, :], 1.0, cols[:, at:at + n],
                                         ALU.add, ALU.mult).then_inc(ev_ready, 1)
            norm(3, xn3, xres)
            for tt in range(TT):
                dve.tensor_scalar(xn3[:, tt, :], xres[:, tt, :], stat[:, 4 + tt:5 + tt], None,
                                  ALU.mult).then_inc(xn_ready[2], 1)
            ordered(dve.memset(pt[:, :, 0:1], 0.0))
            dve.wait_ge(mb_out, 4)
            dve.tensor_tensor(msq, mqk, mqk, ALU.mult).then_inc(msq_ready, 1)
            ordered(dve.memset(restart, 1.0))
            ordered(dve.memset(restart[:, 0:T:CL], 0.0))
            for i, name in ((0, "q_g"), (1, "k_g")):
                dve.wait_ge(m_norm, 5 + i)
                dve.scalar_tensor_tensor(mqk[:, 4 * i:4 * i + 4, :], mqk[:, 4 * i:4 * i + 4, :], col(name),
                                         mrs[:, 4 * i:4 * i + 4, :], ALU.mult, ALU.mult).then_inc(mqk_ready, 1)
            dve.wait_ge(bias_made, 2 * NH)
            for tt, sc in ((0, sc0), (1, sc1)):
                hb = 4 // (tt + 1)
                for b in range(2 * (tt + 1)):
                    dve.wait_ge(sc_mm, 2 * tt + b + 1)
                    s3 = sc[:, hb * b:hb * b + hb, :]
                    src = psum[:, SC_BANK[2 * tt + b], :].rearrange("p (a t) -> p a t", a=hb)
                    dve.scalar_tensor_tensor(s3, src, float(HD) ** -0.5, s3, ALU.mult, ALU.add).then_inc(sc_read, 1)
                dve.wait_ge(sc_read, 2 * tt + 2 * (tt + 1))
                ordered(dve.tensor_reduce(mx[:, 0, :], sc, AX_X, ALU.max))
                dve.tensor_tensor(sc, sc, mx[:, 0, :].unsqueeze(2).to_broadcast([P, NH, (tt + 1) * P]),
                                  ALU.subtract).then_inc(mexp_in, 1)
            dve.wait_ge(mexp_in, TT)
            for tt, sc in ((0, sc0), (1, sc1)):
                dve.wait_ge(mexp_out, tt + 1)
                ordered(dve.tensor_reduce(mx[:, 0, :], sc, AX_X, ALU.add))
                ordered(dve.reciprocal(mx[:, 1, :], mx[:, 0, :]))
                dve.tensor_tensor(sc, sc, mx[:, 1, :].unsqueeze(2).to_broadcast([P, NH, (tt + 1) * P]),
                                  ALU.mult).then_inc(prob_ready, 1)
                dve.wait_ge(prob_ready, tt + 1)
            dve.wait_ge(ym_ready, TT)
            dve.wait_ge(rw_out, N_RW)

            def differences(a, b):
                return dve.tensor_tensor(ps[:, a:b, :], pt[:, a:b, 0:T], pt[:, a:b, 1:], ALU.subtract)

            def mixed(t):
                n = P if t < 14 else 32
                at = COLS["mu"][0] + t
                return dve.scalar_tensor_tensor(ps[0:n, t, :], ps[0:n, t, :], cols[0:n, at:at + 1], pt[0:n, t, 1:],
                                                ALU.mult, ALU.add)

            differences(12, 14).then_inc(vec_step, 1)
            steps[0] += 1
            ordered(dve.tensor_tensor(ps[0:32, 14, :], pt[0:32, 14, 0:T], pt[0:32, 14, 1:], ALU.subtract))
            for t in (12, 13):
                mixed(t)
            mixed(14).then_inc(ps_ready, 1)
            ordered(differences(4, 8))
            for t in range(4, 7):
                mixed(t)
            ordered(mixed(7))
            for c in range(4):
                dve.tensor_scalar(kk[:, c, :], k_[:, c, :], col("k_k", c), None, ALU.mult).then_inc(vec_step, 1)
            steps[0] += 4
            dve.wait_ge(vec_step, steps[0])
            dve.tensor_tensor(t1, kk, kk, ALU.mult).then_inc(ksq_ready, 1)
            differences(0, 4).then_inc(vec_step, 1)
            steps[0] += 1
            ordered(differences(8, 12))
            for t in (0, 1, 2, 3, 8, 9, 10):
                mixed(t)
            ordered(mixed(11))
            dve.wait_ge(sig_out, 4)
            for c in range(4):
                dve.tensor_tensor_scan(pc[:, c, :], restart, wd[:, c, :], 0.0, ALU.mult, ALU.add).then_inc(vec_step, 1)
            steps[0] += 4
            dve.wait_ge(vec_step, steps[0])
            dve.tensor_tensor(wd, pc, wd, ALU.subtract).then_inc(log_ready, 1)
            for b in range(2):
                dve.wait_ge(ksum_mm, 1)
                dve.tensor_scalar(t1[:, 2 * b:2 * b + 2, :], psum[:, 6 + b, :].rearrange("p (a t) -> p a t", a=2),
                                  1e-24, None, ALU.max).then_inc(kn_in, 1)
            dve.wait_ge(sig_out, 8)
            for c in range(4):
                dve.tensor_scalar(t2[:, c, :], aa[:, c, :], -1.0, col("k_a", c), ALU.add, ALU.mult).then_inc(vec_step, 1)
            steps[0] += 4
            dve.wait_ge(vec_step, steps[0])
            ordered(dve.scalar_tensor_tensor(k_, t2, 1.0, k_, ALU.add, ALU.mult))
            for c in range(4):
                dve.scalar_tensor_tensor(t2[:, c, :], r_[:, c, :], col("r_k", c), k_[:, c, :],
                                         ALU.mult, ALU.mult).then_inc(rkk_ready, 1)
            dve.wait_ge(knorm_out, 2)
            ordered(dve.tensor_tensor(kk, kk, t1, ALU.mult))
            ordered(dve.tensor_tensor(aa, kk, aa, ALU.mult))
            dve.wait_ge(dec_out, 1)
            ordered(dve.tensor_tensor(kt_, k_, bt, ALU.mult))
            dve.tensor_tensor(bt, bt, aa, ALU.mult).then_inc(vec_step, 1)
            steps[0] += 1
            dve.wait_ge(dec_out, 3)
            dve.tensor_copy(pl, pc[:, :, CL - 1:T:CL]).then_inc(vec_step, 1)
            steps[0] += 1
            dve.scalar_tensor_tensor(ar[:, :, 0, :], kk, -1.0, wd, ALU.mult, ALU.mult).then_inc(vec_step, 1)
            steps[0] += 1
            ordered(dve.tensor_tensor(ar[:, :, 1, :], r_, pc, ALU.mult))
            dve.wait_ge(bon_mm, 1)
            for b in range(2):
                dve.tensor_tensor(bon[:, 2 * b:2 * b + 2, :], psum[:, b, :].rearrange("p (a t) -> p a t", a=2),
                                  v_[:, 2 * b:2 * b + 2, :], ALU.mult).then_inc(tilde, 1)
            ordered(dve.memset(states[0], 0.0))

            def pair4(bank):
                return psum[:, bank, :].rearrange("p (a t) -> p a t", a=4)

            for tt in range(TT):
                for i in range(1, 4, 2):
                    dve.wait_ge(tok_mm, 4 * tt + i + 1)
                    dve.tensor_copy(tok[:, i, :], psum[:, i, :]).then_inc(tok_ready, 1)
                for c in range(4):
                    for par in range(2):
                        h = 2 * c + par
                        dve.wait_ge(gram_mm, 8 * tt + h + 1)
                        g = psum[:, 4 + 2 * (c % 2) + par, :].rearrange("p (a b t) -> p b a t", a=2, b=2)
                        m = [P, 2, P]
                        dve.tensor_tensor(nak[:, h, :, :], g[:, 0, :, :], mask_st[:, 0:1, :].to_broadcast(m),
                                          ALU.mult).then_inc(vec_step, 1)
                        steps[0] += 1
                        dve.tensor_tensor(rbk[:, h, :, :], g[:, 1, :, :], mask_st[:, 1:2, :].to_broadcast(m),
                                          ALU.mult).then_inc(gram_out, 1)
                dve.wait_ge(nt_mm, tt + 1)
                for par in range(2):
                    dve.tensor_tensor(nts[:, par:NH:2, :], pair4(2 + par), mask_ts[:].unsqueeze(1).to_broadcast([P, 4, P]),
                                      ALU.mult).then_inc(nt_out, 1)
                dve.wait_ge(vec_step, steps[0])
                dve.tensor_tensor(inv, nak[:, :, 0, :], ident[:].unsqueeze(1).to_broadcast([P, NH, P]),
                                  ALU.add).then_inc(nt_out, 1)
                for lv in range(1, 5):
                    for q in range(2):
                        if lv < 4:
                            dve.wait_ge(ps_mm, 6 * tt + 2 * (lv - 1) + q + 1)
                            dst = pw_s[:, 4 * q:4 * q + 4, :] if lv % 2 else nak[:, 4 * q:4 * q + 4, 0, :]
                            dve.tensor_copy(dst, pair4(q)).then_inc(ps_out, 1)
                    for q in range(2):
                        dve.wait_ge(ix_mm, 8 * tt + 2 * (lv - 1) + q + 1)
                        iv = inv[:, 4 * q:4 * q + 4, :]
                        dve.tensor_tensor(iv, iv, pair4(4 + q), ALU.add).then_inc(ix_out, 1)
                dve.wait_ge(wu_mm, 3 * tt + 1)
                dve.tensor_copy(z2, psum[:, 6, :].rearrange("p (h c) -> p h c", h=NH)).then_inc(wu_out, 1)
                for q in range(2):
                    dve.wait_ge(wu_mm, 3 * tt + q + 2)
                    dve.tensor_copy(nak[:, 4 * q:4 * q + 4, 1, :], pair4((7, 0)[q])).then_inc(wu_out, 1)
                dve.wait_ge(q2_mm, tt + 1)
                dve.tensor_tensor(qt, pair4(0), ar[:, :, 1, tt * P:(tt + 1) * P], ALU.add).then_inc(q2_out, 1)
                ordered(dve.memset(phi, 0.0))
                for c in range(P // CL):
                    dve.wait_ge(fg_mm, 4 * tt + c + 1)
                    f4 = psum[:, 2 + c, 0:T].rearrange("p (a j) -> p a j", a=4)
                    for par in range(2):
                        a, b = HD * par, HD * par + HD
                        dve.tensor_tensor(phi[a:b, c, :, a:b], f4[a:b], ident[a:b, a:b].unsqueeze(1).to_broadcast([HD, 4, HD]),
                                          ALU.add).then_inc(vec_step, 1)
                        steps[0] += 1
                    dve.tensor_copy(gam[:, c, :, :],
                                    psum[:, 2 + c, T:2 * T].rearrange("p (a j) -> p a j", a=4)).then_inc(fg_out, 1)
                for c in range(P // CL):
                    g = tt * (P // CL) + c
                    if g == NC - 1:
                        break
                    nx = states[(g + 1) % 5]
                    dve.wait_ge(st_mm, g + 1)
                    dve.wait_ge(fg_out, 4 * tt + 4)
                    ordered(dve.tensor_tensor(nx, psum[:, 6 + g % 2, 0:T].rearrange("p (a i) -> p a i", a=4),
                                              gam[:, c, :, :], ALU.add))
                    dve.tensor_tensor(nx, nx, pl[:, :, g:g + 1].to_broadcast([P, 4, HD]), ALU.mult).then_inc(st_out, 1)
                dve.wait_ge(yp_out, tt + 1)
                for par in range(2):
                    dve.wait_ge(ys_mm, 2 * tt + par + 1)
                    a, b = HD * par, HD * par + HD
                    yv = yT[a:b, :, tt * P:(tt + 1) * P]
                    dve.tensor_tensor(yv, yv, pair4(4 + par)[a:b], ALU.add).then_inc(ys_out, 1)
            dve.wait_ge(ys_out, 4)
            for b in range(2):
                dve.wait_ge(ln_mm, b + 1)
                s2 = slice(2 * b, 2 * b + 2)
                dve.scalar_tensor_tensor(dn[:, s2, :], psum[:, b, :].rearrange("p (a t) -> p a t", a=2), -1.0 / HD,
                                         yT[:, s2, :], ALU.mult, ALU.add).then_inc(vec_step, 1)
            steps[0] += 2
            dve.wait_ge(vec_step, steps[0])
            dve.tensor_tensor(dsq, dn, dn, ALU.mult).then_inc(ln_sq, 1)
            dve.wait_ge(ln_norm, 3)
            ordered(dve.tensor_tensor(dn, dn, drs, ALU.mult))
            for c in range(4):
                dve.tensor_scalar(dn[:, c, :], dn[:, c, :], col("ln_g", c), col("ln_b", c), ALU.mult,
                                  ALU.add).then_inc(vec_step, 1)
            steps[0] += 4
            dve.wait_ge(vec_step, steps[0])
            ordered(dve.tensor_tensor(dn, dn, bon, ALU.add))
            dve.tensor_tensor(yT, dn, gg, ALU.mult).then_inc(y_done, 1)
            for n in range(N_O2):
                dve.wait_ge(chunk_done, C_O2 + n + 1)
                cs = slice(n * CW, (n + 1) * CW)
                ordered(dve.tensor_tensor(ga_t, psum[:, 4 + n, :].rearrange("p (a c) -> p a c", a=TT),
                                          gates[:, 0:1, cs].to_broadcast([P, TT, CW]), ALU.mult))
                ordered(dve.tensor_tensor(xres[:, :, cs], xres[:, :, cs], ga_t, ALU.add))
            norm(4, xn4, xres)
            for tt in range(TT):
                dve.tensor_scalar(xn4[:, tt, :], xres[:, tt, :], stat[:, 4 + tt:5 + tt], None,
                                  ALU.mult).then_inc(xn_ready[3], 1)
            dve.wait_ge(router_mm, 1)
            sh = [P, TT, NE]
            ordered(dve.tensor_tensor(lg, psum[:, 5, 0:TT * NE].rearrange("p (a e) -> p a e", a=TT),
                                      brow_r[:].unsqueeze(1).to_broadcast(sh), ALU.add))
            for tt in range(TT):
                ordered(dve.max(top8[:, tt, :], lg[:, tt, :]))
                ordered(dve.max_index(top8i[:, tt, :], top8[:, tt, :], lg[:, tt, :]))
            ordered(dve.tensor_copy(top8f, top8i))
            dve.tensor_tensor(w4, top8[:, :, 0:TOPE], top8[:, :, 0:1].to_broadcast([P, TT, TOPE]),
                              ALU.subtract).then_inc(wexp_in, 1)
            ordered(dve.memset(picks, 0.0))
            dve.wait_ge(wexp_out, 1)
            ordered(dve.tensor_reduce(wsum[:, 0, :], w4, AX_X, ALU.add))
            ordered(dve.reciprocal(wsum[:, 1, :], wsum[:, 0, :]))
            ordered(dve.tensor_tensor(w4, w4, wsum[:, 1, :].unsqueeze(2).to_broadcast([P, TT, TOPE]), ALU.mult))
            ordered(dve.memset(wts, 0.0))
            for k in range(TOPE):
                ordered(dve.tensor_tensor(eqe, top8f[:, :, k:k + 1].to_broadcast(sh),
                                          iota_e[:].unsqueeze(1).to_broadcast(sh), ALU.is_equal))
                ordered(dve.tensor_tensor(picks, picks, eqe, ALU.add))
                ordered(dve.tensor_tensor(eqe, eqe, w4[:, :, k:k + 1].to_broadcast(sh), ALU.mult))
                ordered(dve.tensor_tensor(wts, wts, eqe, ALU.add))
            dve.memset(acc, 0.0).then_inc(picks_ready, 1)
            dve.wait_ge(router_mm, 2)
            ordered(dve.memset(rank, -1.0))
            ordered(dve.scalar_tensor_tensor(rank[:, :, 0:NE], psum[:, 6, 0:TT * NE].rearrange("p (a e) -> p a e", a=TT),
                                             1.0, picks, ALU.add, ALU.mult))
            dve.tensor_scalar(rank[:, :, 0:NE], rank[:, :, 0:NE], -1.0, None, ALU.add).then_inc(rk_made, 1)
            ordered(dve.tensor_reduce(most, psum[:, 6, TT * NE:TT * NE + NE], AX_X, ALU.max))
            dve.tensor_copy(most_i, most).then_inc(count_ready, 1)

            def front_in(f, e):
                dve.wait_ge(g_mm, f + 1)
                for tt in range(TT):
                    ins = dve.tensor_scalar(oh[:, tt, :], iota_slot[:, 0:CAP], rank[:, tt, bass.ds(e, 1)], None, ALU.is_equal)
                ins.then_inc(oh_ready, 1)

            def bias_rows(e):
                dve.tensor_scalar(sel_e[0:2 * NE], half_e[0:2 * NE, :], iota_e2[0:2 * NE, bass.ds(e, 1)], None,
                                  ALU.is_equal).then_inc(sel_ready, 1)

            def front_out(f):
                dve.wait_ge(xt_mm, f + 1)
                sh4 = [P, 4, 2, CAP]
                x4 = xT.rearrange("p j (h s) -> p j h s", h=2)
                src = psum[:, 3, :].rearrange("p (j h s) -> p j h s", j=4, h=2)
                sc_ = evcols[:, 1, :].rearrange("p (h j) -> p j h", h=2).unsqueeze(3).to_broadcast(sh4)
                sf_ = modcols[:, 2, :].rearrange("p (h j) -> p j h", h=2).unsqueeze(3).to_broadcast(sh4)
                dve.tensor_tensor(x4, src, sc_, ALU.mult).then_inc(xt_scaled, 1)
                dve.wait_ge(xt_scaled, f + 1)
                dve.tensor_tensor(x4, x4, sf_, ALU.add).then_inc(xT_ready, 1)

            def experts(p):
                dve.wait_ge(rk_made, p + 1)
                f0 = p * (NE + 1)
                front_in(f0, 0)
                bias_rows(0)
                front_out(f0)
                with dve.Fori(0, NE) as e:
                    it = p * NE + e
                    f = p * (NE + 1) + e
                    front_in(f + 1, e + 1)
                    dve.wait_ge(sct_mm, it + 1)
                    for tt in range(TT):
                        ins = dve.tensor_scalar(ohw[:, tt, :], iota_slot[:], rank[:, tt, bass.ds(e, 1)],
                                                wts[:, tt, bass.ds(e, 1)], ALU.is_equal, ALU.mult)
                    ins.then_inc(ohw_ready, 1)
                    dve.wait_ge(gu_mm, it + 1)
                    dve.tensor_scalar(ag, psum[:, 0, :], LIMIT, None, ALU.min).then_inc(gate_ready, 1)
                    dve.tensor_scalar(au, psum[:, 1, :], LIMIT, -LIMIT, ALU.min, ALU.max).then_inc(gu_read, 1)
                    bias_rows(e + 1)
                    dve.wait_ge(gu_read, it + 2)
                    dve.scalar_tensor_tensor(au, au, 1.0, ag, ALU.add, ALU.mult).then_inc(up_ready, 1)
                    dve.wait_ge(up_ready, it + 1)
                    dve.wait_ge(sg_ready, it + 1)
                    dve.tensor_tensor(ag, au, sg, ALU.mult).then_inc(act_ready, 1)
                    front_out(f + 1)
                    for tt in range(TT):
                        dve.wait_ge(sum_mm, it * TT + (tt + 1))
                        dve.tensor_tensor(acc[:, tt, :], acc[:, tt, :],
                                          psum[:, (6, 3)[tt]:(8, 5)[tt], :].rearrange("p a c -> p (a c)"),
                                          ALU.add).then_inc(acc_done, 1)
                dve.wait_ge(acc_done, (p + 1) * (NE * TT) + 1)
                dve.tensor_scalar(rank, rank, -float(CAP), None, ALU.add).then_inc(rk_made, 1)

            experts(0)
            further_passes(dve, experts)
            for tt in range(TT):
                ordered(dve.tensor_tensor(acc[:, tt, :], acc[:, tt, :], gates[:, 1, :], ALU.mult))
                dve.tensor_tensor(xres[:, tt, :], xres[:, tt, :], acc[:, tt, :], ALU.add).then_inc(out_ready, 1)

        @block.tensor
        def _(pe):
            def turn(n, src):
                pe.wait_ge(xn_ready[n], TT)
                for k in range(KD):
                    if k >= 4:
                        pe.wait_ge(hT_ready[n], k - 3)
                    for tt in range(TT):
                        last = pe.transpose(psum[:, k % 4, tt * P:(tt + 1) * P], src[:, tt, k * P:(k + 1) * P], ident[:])
                    last.then_inc(turned[n], 1)

            def chunk(n):
                pe.wait_ge(landed[n % SLOTS], uses(n))

            def channels(n, acts, bank, width=2):
                chunk(n)
                for c in range(width):
                    for k in range(KD):
                        last = pe.matmul(psum[:, bank, c * T:(c + 1) * T], wide(n)[:, k, c * P:(c + 1) * P],
                                         acts[:, k, :], start=(k == 0), stop=(k == KD - 1))
                return last

            def tokens(n, acts, bank, owed=False):
                chunk(n)
                for tt in range(TT):
                    for k in range(KD):
                        last = pe.matmul(psum[:, bank, tt * CW:(tt + 1) * CW], acts[:, k, tt * P:(tt + 1) * P],
                                         wide(n)[:, k, :], start=(k == 0), stop=(k == KD - 1))
                        if owed and tt == 0 and k == 0:
                            last.then_inc(chunk_done, 1)
                return last

            pe.sem_inc(g_mm, 1)
            pe.sem_inc(sct_mm, 1)
            pe.wait_ge(consts, 1)
            turn(0, xn)
            pe.wait_ge(hT_ready[0], KD)
            for n in range(N_Z):
                if n >= 4:
                    pe.wait_ge(z_out, n - 3)
                channels(C_Z + n, hT, 2 + n % 4).then_inc(chunk_done, 1)
            pe.wait_ge(p_ready, 1)
            pe.wait_ge(loaded_p, 48)
            for g in range(POOL_G):
                last = pe.matmul(psum[:, 6 + g // 2, (g % 2) * T:(g % 2) * T + T],
                                 mats[:, M_GROUP + g * P:M_GROUP + (g + 1) * P], pT[:, g, :], start=True, stop=True)
            last.then_inc(group_mm, 1)
            pe.wait_ge(a_ready, POOL_G)
            pe.wait_ge(c_ready, 1)
            for k in range(KD):
                pair = k // 4
                if k % 4 == 0:
                    chunk(C_BR + 2 * pair)
                    chunk(C_BR + 2 * pair + 1)
                if k >= 4:
                    pe.wait_ge(m_ready, k - 3)
                elif k == 0:
                    pe.wait_ge(z_out, N_Z)
                for b, act_in in ((0, aT), (1, cT)):
                    w = slot(C_BR + 2 * pair + b).rearrange("p (k c) -> p k c", k=4)
                    for q in range(4):
                        last = pe.matmul(psum[:, 2 + k % 4, b * T:(b + 1) * T], w[:, q, (k % 4) * P:(k % 4 + 1) * P],
                                         act_in[:, q, :], start=(q == 0), stop=(q == 3))
                        if k == 4 and b == 0 and q == 0:
                            last.then_inc(chunk_done, 1)
                    if k % 4 == 3 and b == 0:
                        last.then_inc(chunk_done, 1)
                last.then_inc(br_mm, 1)
            pe.wait_ge(m_ready, KD)
            for n in range(N_O1):
                tokens(C_O1 + n, mT, 2 + n % 4, owed=(n == 0)).then_inc(chunk_done, 1)
            turn(1, h2)
            pe.wait_ge(hT_ready[1], KD)
            pe.wait_ge(x_mid, N_O1)
            for tt in range(TT):
                for n in range(N_Q):
                    if tt == 0:
                        chunk(C_Q + n)
                    elif n % 2 == 0:
                        pe.wait_ge(q_out, n // 2 + 1)
                    for c in range(2):
                        at = (2 * (n % 2) + c) * P
                        for k in range(KD):
                            last = pe.matmul(psum[:, 2 + n // 2, at:at + P], wide(C_Q + n)[:, k, c * P:(c + 1) * P],
                                             h2T[:, k, tt * P:(tt + 1) * P], start=(k == 0), stop=(k == KD - 1))
                    if tt:
                        last.then_inc(chunk_done, 1)
                    elif n % 2:
                        last.then_inc(q_mm, 1)
                chunk(C_KEYS)
                for m in range(HP // 4):
                    pe.wait_ge(q_out, tt * (HP // 4) + m + 1)
                    if tt:
                        pe.wait_ge(s_out, m + 1)
                    for i in range(4):
                        hp = 4 * m + i
                        last = pe.matmul(psum[:, S_BANK[m], i * NK:(i + 1) * NK], qT[:, tt, hp, :],
                                         slot(C_KEYS)[:, hp * NK:(hp + 1) * NK], start=True, stop=True)
                    last.then_inc(s_mm, 1)
            pe.wait_ge(cb_ready, KD)
            pe.wait_ge(loaded_rows, 32)
            pe.wait_ge(s_out, TT * HP // 4)
            m = 0
            for n in range(N_ADA):
                chunk(C_ADA + n)
                if n >= 2:
                    pe.wait_ge(ada_out, n - 1)
                for k in range(KD):
                    first = pe.matmul(psum[:, 4 + n % 2, 0:CW], cb[:, k, :], wide(C_ADA + n)[:, k, :],
                                      start=(k == 0), stop=False)
                    if n == 0 and k == 0:
                        first.then_inc(chunk_done, 1)
                r = 32 * (n // 6)
                last = pe.matmul(psum[:, 4 + n % 2, 0:CW], ones[r:r + 1, :], brow[r:r + 1, (n % 6) * CW:(n % 6 + 1) * CW],
                                 start=False, stop=True)
                last.then_inc(chunk_done, 1)
                if n // 4 not in (2, 5):
                    pe.wait_ge(ada_out, n + 1)
                    if m:
                        pe.wait_ge(mcol_out, m)
                    for i in range(2):
                        last = pe.matmul(psum[:, 6, i:i + 1], mrow[0:1, n % 2, i * P:(i + 1) * P], ones[0:1, 0:1],
                                         start=True, stop=True)
                    last.then_inc(mcol_mm, 1)
                    m += 1
            turn(2, xn3)
            pe.wait_ge(hT_ready[2], KD)

            def mb_chunk(n):
                if n >= 4:
                    pe.wait_ge(mb_out, n - 3)
                ins = channels(C_MB + n, hT3, 2 + n % 4) if n < 4 else tokens(C_MB + n, hT3, 2 + n % 4)
                ins.then_inc(chunk_done, 1)

            def rw_chunk(n):
                k = N_MB + n
                pe.wait_ge(mb_out, min(k - 3, N_MB))
                if k - 3 > N_MB:
                    pe.wait_ge(rw_out, k - 3 - N_MB)
                if n < N_RW - 1:
                    channels(C_RW + n, hT3, 2 + k % 4).then_inc(chunk_done, 1)
                else:
                    chunk(C_RW + n)
                    for q in range(KD):
                        last = pe.matmul(psum[0:32, 2 + k % 4, 0:T], wide(C_RW + n)[:, q, 0:32], hT3[:, q, :],
                                         start=(q == 0), stop=(q == KD - 1))
                    last.then_inc(chunk_done, 1)

            def scores(j):
                tt = 0 if j < 2 else 1
                b = j - 2 * tt
                nk = (tt + 1) * P
                hb = 4 // (tt + 1)
                rows = slice(HD * (b // (tt + 1)), HD * (b // (tt + 1)) + HD)
                if j >= 4:
                    pe.wait_ge(sc_read, j - 3)
                for i in range(hb):
                    c = (hb * b + i) % 4
                    last = pe.matmul(psum[:, SC_BANK[j], i * nk:(i + 1) * nk], mqk[rows, c, tt * P:(tt + 1) * P],
                                     mqk[rows, 4 + c, 0:nk], start=True, stop=True)
                last.then_inc(sc_mm, 1)

            def turn_weights(j):
                tt, sc = (0, sc0) if j < 2 else (1, sc1)
                b = j - 2 * tt
                hb = 4 // (tt + 1)
                pe.wait_ge(prob_ready, tt + 1)
                pe.wait_ge(sc_read, 6)
                if j >= 3:
                    pe.wait_ge(prT_ready, j - 2)
                for i in range(hb):
                    for kt in range(tt + 1):
                        at = (i * (tt + 1) + kt) * P
                        last = pe.transpose(psum[:, PR_BANK[j], at:at + P], sc[:, hb * b + i, kt * P:(kt + 1) * P], ident[:])
                last.then_inc(pr_mm, 1)

            def attend(tt):
                pe.wait_ge(prT_ready, (2, 6)[tt])
                if tt:
                    pe.wait_ge(ym_ready, 1)
                for par in range(2):
                    for c in range(4):
                        for kt in range(tt + 1):
                            h = 2 * c + par
                            last = pe.matmul(psum[HD * par:HD * par + HD, 6, c * P:(c + 1) * P],
                                             mv[:, kt, h * HD:(h + 1) * HD], prT[:, 4 * par + c, kt, :],
                                             start=(kt == 0), stop=(kt == tt))
                last.then_inc(pv_mm, 1)

            for n in range(5):
                mb_chunk(n)
            pe.wait_ge(msq_ready, 1)
            for b in range(4):
                pe.matmul(psum[:, (6, 7, 0, 1)[b], :], headblk[:], msq[:, 2 * b:2 * b + 2, :].rearrange("p a t -> p (a t)"),
                          start=True, stop=True).then_inc(msum_mm, 1)
            mb_chunk(5)
            rw_chunk(0)
            pe.wait_ge(mqk_ready, 2)
            pe.wait_ge(m_norm, 4)
            for j in range(4):
                scores(j)
            rw_chunk(1)
            scores(4)
            scores(5)
            rw_chunk(2)
            turn_weights(0)
            turn_weights(1)
            rw_chunk(3)
            attend(0)
            for j in range(2, 5):
                turn_weights(j)
            rw_chunk(4)
            turn_weights(5)
            rw_chunk(5)
            attend(1)
            rw_chunk(6)
            rw_chunk(7)
            pe.wait_ge(lora_in, 3)
            pe.wait_ge(ym_ready, TT)
            for i, rows in ((0, slice(0, 64)), (1, slice(64, 128))):
                for c in range(4):
                    last = pe.matmul(psum[:, 2 * i + c // 2, (c % 2) * T:(c % 2) * T + T],
                                     mats[rows, M_LORA + c * P:M_LORA + (c + 1) * P], ps[rows, 12, :],
                                     start=True, stop=True)
                last.then_inc(lora_mm, 1)
            pe.wait_ge(ksq_ready, 1)
            for b in range(2):
                last = pe.matmul(psum[:, 6 + b, :], headblk[:], t1[:, 2 * b:2 * b + 2, :].rearrange("p a t -> p (a t)"),
                                 start=True, stop=True)
            last.then_inc(ksum_mm, 1)
            for c in range(4):
                o = psum[:, 4 + c // 2, (c % 2) * T:(c % 2) * T + T]
                pe.matmul(o, mats[:, M_GUP + c * P:M_GUP + (c + 1) * P], ps[:, 13, :], start=True, stop=False)
                last = pe.matmul(o, mats[0:32, M_GUP + W2 + c * P:M_GUP + W2 + (c + 1) * P], ps[0:32, 14, :],
                                 start=False, stop=True)
            last.then_inc(lora_mm, 1)
            pe.wait_ge(rkk_ready, 4)
            pe.wait_ge(sig_out, 4)
            for b in range(2):
                last = pe.matmul(psum[:, b, :], headblk[:], t2[:, 2 * b:2 * b + 2, :].rearrange("p a t -> p (a t)"),
                                 start=True, stop=True)
            last.then_inc(bon_mm, 1)
            pe.wait_ge(tilde, 2)
            pe.wait_ge(sig_out, 10)
            for tt in range(TT):
                ts = slice(tt * P, (tt + 1) * P)
                if tt:
                    pe.wait_ge(ys_out, 2)
                for i, src in enumerate((ar[:, :, 0, :], bt, kt_, v_)):
                    for c in range(4):
                        last = pe.transpose(psum[:, i, c * P:(c + 1) * P], src[:, c, ts], ident[:])
                    last.then_inc(tok_mm, 1)
                for c in range(4):
                    for par in range(2):
                        h = 2 * c + par
                        rows = slice(HD * par, HD * par + HD)
                        if c >= 2:
                            pe.wait_ge(gram_out, 8 * tt + h - 3)
                        for i, src in enumerate((bt, kt_)):
                            last = pe.matmul(psum[:, 4 + 2 * (c % 2) + par, i * 2 * P:(i + 1) * 2 * P], src[rows, c, ts],
                                             ar[rows, c, :, ts], start=True, stop=True)
                        last.then_inc(gram_mm, 1)
                pe.wait_ge(tok_ready, 4 * tt + 4)
                for par in range(2):
                    rows = slice(HD * par, HD * par + HD)
                    for c in range(4):
                        last = pe.matmul(psum[:, 2 + par, c * P:(c + 1) * P], ar[rows, c, 0, ts], bt[rows, c, ts],
                                         start=True, stop=True)
                last.then_inc(nt_mm, 1)
                pe.wait_ge(nt_out, 3 * tt + 3)
                for lv in range(1, 5):
                    s_src = (lambda h: nak[:, h, 0, :]) if lv % 2 else (lambda h: pw_s[:, h, :])
                    t_src, t_dst = (nts, pw_t) if lv % 2 else (pw_t, nts)
                    if lv > 1:
                        pe.wait_ge(ps_out, 6 * tt + 2 * (lv - 1))
                        pe.wait_ge(pt_out, 8 * tt + 2 * (lv - 1))
                    for q in range(2):
                        hs = range(4 * q, 4 * q + 4)
                        for h in hs:
                            last = pe.matmul(psum[:, 2 + q, (h % 4) * P:(h % 4 + 1) * P], s_src(h), t_src[:, h, :],
                                             start=True, stop=True)
                        last.then_inc(pt_mm, 1)
                        if lv < 4:
                            for h in hs:
                                last = pe.matmul(psum[:, q, (h % 4) * P:(h % 4 + 1) * P], t_src[:, h, :], s_src(h),
                                                 start=True, stop=True)
                            last.then_inc(ps_mm, 1)
                    for q in range(2):
                        pe.wait_ge(pt_out, 8 * tt + 2 * (lv - 1) + q + 1)
                        if lv > 1:
                            pe.wait_ge(ix_out, 8 * tt + 2 * (lv - 2) + q + 1)
                        for h in range(4 * q, 4 * q + 4):
                            last = pe.matmul(psum[:, 4 + q, (h % 4) * P:(h % 4 + 1) * P], t_dst[:, h, :], inv[:, h, :],
                                             start=True, stop=True)
                        last.then_inc(ix_mm, 1)
                for h in range(NH):
                    last = pe.matmul(psum[:, 6, h * HD:(h + 1) * HD], nak[:, h, 1, :], tok[:, 3, h * HD:(h + 1) * HD],
                                     start=True, stop=True)
                last.then_inc(wu_mm, 1)
                pe.wait_ge(ix_out, 8 * tt + 8)
                pe.wait_ge(wu_out, 3 * tt + 1)
                for h in range(NH):
                    b = (7, 0)[h // 4]
                    at = (h % 4) * P
                    pe.matmul(psum[:, b, at:at + HD], inv[:, h, :], tok[:, 0, h * HD:(h + 1) * HD], start=True, stop=True)
                    last = pe.matmul(psum[:, b, at + HD:at + P], inv[:, h, :], z2[:, h, :], start=True, stop=True)
                    if h % 4 == 3:
                        last.then_inc(wu_mm, 1)
                pe.wait_ge(wu_out, 3 * tt + 3)
                for par in range(2):
                    for c in range(4):
                        h = 2 * c + par
                        last = pe.matmul(psum[HD * par:HD * par + HD, 0, c * P:(c + 1) * P], nak[:, h, 1, 0:HD],
                                         rbk[:, h, 0, :], start=True, stop=True)
                last.then_inc(q2_mm, 1)
                for par in range(2):
                    for c in range(4):
                        h = 2 * c + par
                        o = psum[HD * par:HD * par + HD, 1, c * P:(c + 1) * P]
                        pe.matmul(o, tok[:, 3, h * HD:(h + 1) * HD], rbk[:, h, 1, :], start=True, stop=False)
                        last = pe.matmul(o, nak[:, h, 1, HD:P], rbk[:, h, 0, :], start=False, stop=True)
                last.then_inc(yp_mm, 1)
                for ch in range(P // CL):
                    rows = slice(CL * ch, CL * ch + CL)
                    for par in range(2):
                        for c in range(4):
                            h = 2 * c + par
                            hs = slice(h * HD, (h + 1) * HD)
                            orow = slice(HD * par, HD * par + HD)
                            pe.matmul(psum[orow, 2 + ch, c * HD:(c + 1) * HD], nak[rows, h, 1, 0:HD], tok[rows, 1, hs],
                                      start=True, stop=True)
                            o = psum[orow, 2 + ch, T + c * HD:T + (c + 1) * HD]
                            pe.matmul(o, tok[rows, 1, hs], nak[rows, h, 1, HD:P], start=True, stop=False)
                            last = pe.matmul(o, tok[rows, 2, hs], tok[rows, 3, hs], start=False, stop=True)
                    last.then_inc(fg_mm, 1)
                for ch in range(P // CL):
                    g = tt * (P // CL) + ch
                    if g == NC - 1:
                        break
                    pe.wait_ge(fg_out, 4 * tt + ch + 1)
                    if g:
                        pe.wait_ge(st_out, g)
                    for c in range(4):
                        last = pe.matmul(psum[:, 6 + g % 2, c * HD:(c + 1) * HD], phi[:, ch, c, :], states[g % 5][:, c, :],
                                         start=True, stop=True)
                    last.then_inc(st_mm, 1)
                pe.wait_ge(q2_out, tt + 1)
                pe.wait_ge(fg_out, 4 * tt + 4)
                if tt:
                    pe.wait_ge(st_out, NC - 1)
                else:
                    pe.wait_ge(st_out, P // CL - 1)
                for par in range(2):
                    rows = slice(HD * par, HD * par + HD)
                    for c in range(4):
                        for ch in range(P // CL):
                            g = tt * (P // CL) + ch
                            at = c * P + ch * CL
                            last = pe.matmul(psum[rows, 4 + par, at:at + CL], states[g % 5][rows, c, :],
                                             qt[rows, c, ch * CL:(ch + 1) * CL], start=True, stop=True)
                    last.then_inc(ys_mm, 1)
            pe.wait_ge(ys_out, 4)
            for b in range(2):
                pe.matmul(psum[:, b, :], headblk[:], yT[:, 2 * b:2 * b + 2, :].rearrange("p a t -> p (a t)"),
                          start=True, stop=True).then_inc(ln_mm, 1)
            def out_half(n, y, half):
                for tt in range(TT):
                    for k in range(4):
                        last = pe.matmul(psum[:, 4 + n, tt * CW:(tt + 1) * CW], y[:, k, tt * P:(tt + 1) * P],
                                         wide(C_O2 + n)[:, 4 * half + k, :], start=(half == 1 and tt == 0 and k == 0),
                                         stop=(half == 0 and k == 3), skip_group_check=True)
                return last

            for n in range(N_O2):
                chunk(C_O2 + n)
                out_half(n, ymT, 1)
                if n == 1:
                    pe.wait_ge(ln_sq, 1)
                    for b in range(2):
                        pe.matmul(psum[:, 2 + b, :], headblk[:], dsq[:, 2 * b:2 * b + 2, :].rearrange("p a t -> p (a t)"),
                                  start=True, stop=True).then_inc(ln_mm, 1)
            pe.wait_ge(y_done, 1)
            for n in range(N_O2):
                out_half(n, yT, 0).then_inc(chunk_done, 1)
            turn(3, xn4)
            pe.wait_ge(hT_ready[3], KD)
            for tt in range(TT):
                for k in range(KD):
                    last = pe.matmul(psum[:, 5, tt * NE:(tt + 1) * NE], hT4[:, k, tt * P:(tt + 1) * P],
                                     mats[:, M_ROUTER + k * NE:M_ROUTER + (k + 1) * NE],
                                     start=(k == 0), stop=(k == KD - 1))
            last.then_inc(router_mm, 1)
            pe.wait_ge(picks_ready, 1)
            pe.matmul(psum[:, 6, 0:NE], before[:], picks[:, 0, :], start=True, stop=True)
            pe.matmul(psum[:, 6, NE:2 * NE], ones[:], picks[:, 0, :], start=True, stop=False)
            pe.matmul(psum[:, 6, NE:2 * NE], before[:], picks[:, 1, :], start=False, stop=True)
            pe.matmul(psum[:, 6, 2 * NE:3 * NE], ones[:], picks[:, 0, :], start=True, stop=False)
            pe.matmul(psum[:, 6, 2 * NE:3 * NE], ones[:], picks[:, 1, :], start=False, stop=True).then_inc(router_mm, 1)
            pe.wait_ge(loaded_b, 16)
            pe.wait_ge(count_ready, 1)

            def front_gather(f):
                pe.wait_ge(oh_ready, f + 1)
                for tt in range(TT):
                    for h in range(2):
                        last = pe.matmul(psum[CAP * h:CAP * h + CAP, 2, :], oh[:, tt, :], xn4[:, tt, h * 512:(h + 1) * 512],
                                         start=(tt == 0), stop=(tt == TT - 1))
                last.then_inc(g_mm, 1)

            def front_turn(f):
                pe.wait_ge(xs_ready, f + 1)
                for j in range(4):
                    last = pe.transpose(psum[:, 3, j * P:(j + 1) * P], xs[:, j * P:(j + 1) * P], ident[:])
                last.then_inc(xt_mm, 1)

            def experts(p):
                f0 = p * (NE + 1)
                front_gather(f0)
                front_turn(f0)
                with pe.Fori(0, NE) as e:
                    it = p * NE + e
                    f = p * (NE + 1) + e

                    def moe_chunk(j):
                        n = C_MOE + j
                        pe.wait_ge(landed[n % SLOTS], it * 16 + uses(n))
                        return slot(n)

                    pe.wait_ge(xT_ready, f + 1)
                    pe.wait_ge(gu_read, it + 1)
                    for kt in range(GU_CHUNKS):
                        w = moe_chunk(kt)
                        x = xT[:, kt % 4, CAP * (kt // 4):CAP * (kt // 4) + CAP]
                        for gu in range(2):
                            for h in range(2):
                                at = gu * FF + h * 512
                                last = pe.matmul(psum[CAP * h:CAP * h + CAP, gu, :], x, w[:, at:at + 512],
                                                 start=(kt == 0), stop=False, skip_group_check=True)
                        last.then_inc(chunk_done, 1)
                    pe.wait_ge(sel_ready, f + 1)
                    for gu in range(2):
                        last = pe.matmul(psum[:, gu, :], sel_e[0:2 * NE], bmoe[0:2 * NE, gu, :], start=False, stop=True,
                                         skip_group_check=True)
                    pe.wait_ge(ye_ready, it + 1)
                    last = pe.matmul(psum[:, 5, :], sel_e[0:2 * NE], bmoe[0:2 * NE, 2, :], start=True, stop=False,
                                     skip_group_check=True)
                    last.then_inc(gu_mm, 1)
                    pe.wait_ge(sct_ready, it + 1)
                    front_gather(f + 1)
                    pe.wait_ge(act_ready, it + 1)
                    pe.wait_ge(acc_done, it * TT + 1)
                    for j in range(4):
                        last = pe.transpose(psum[:, 4, j * P:(j + 1) * P], ag[:, j * P:(j + 1) * P], ident[:])
                    last.then_inc(at_mm, 1)
                    front_turn(f + 1)
                    pe.wait_ge(actT_ready, it + 1)
                    for q in range(DN_CHUNKS):
                        w = moe_chunk(GU_CHUNKS + q)
                        for i in range(2):
                            kt = 2 * q + i
                            a_in = act_t[:, kt % 4, CAP * (kt // 4):CAP * (kt // 4) + CAP]
                            for h in range(2):
                                last = pe.matmul(psum[CAP * h:CAP * h + CAP, 5, :], a_in,
                                                 w[:, i * D + h * 512:i * D + h * 512 + 512],
                                                 start=False, stop=(kt == KD - 1), skip_group_check=True)
                        if q < DN_CHUNKS - 1:
                            last.then_inc(chunk_done, 1)
                    last.then_inc(y_mm, 1)
                    pe.wait_ge(ohw_ready, it + 1)
                    for tt in range(TT):
                        last = pe.transpose(psum[:, 2, tt * P:(tt + 1) * P], ohw[:, tt, :], ident[:])
                        if tt == 0:
                            last.then_inc(chunk_done, 1)
                    last.then_inc(sct_mm, 1)
                    pe.wait_ge(sct_ready, it + 2)
                    pe.wait_ge(ye_ready, it + 2)
                    pe.wait_ge(xT_ready, f + 2)
                    for tt in range(TT):
                        for h in range(2):
                            rows = slice(CAP * h, CAP * h + CAP)
                            last = pe.matmul(psum[:, (6, 3)[tt] + h, :], sct[rows, tt, :], ye[rows, :],
                                             start=True, stop=True)
                        last.then_inc(sum_mm, 1)

            experts(0)
            further_passes(pe, experts)


def kernel(**inputs):
    from concourse import bacc
    from concourse.bass_utils import run_bass_kernel_spmd

    a = {n: np.asarray(v) for n, v in inputs.items()}
    f = np.float32

    def chunks(w):
        n = w.shape[1] // CW
        return w.reshape(KD, P, n, CW).transpose(2, 1, 0, 3).reshape(n, P, CHUNK)

    def branch(w):
        return w.reshape(4, P, 2, 512).transpose(2, 1, 0, 3).reshape(2, P, CHUNK)

    pool_b, conv_b = branch(a["w_branch_pool"][0]), branch(a["w_branch_conv"][0])
    keys = a["sub_keys"][0].reshape(HP, NK, P).transpose(2, 0, 1).reshape(1, P, CHUNK)
    w2 = a["w_in_2"][0]
    w2 = np.concatenate([w2[:, RW:], w2[:, :RW], np.zeros((D, RWP - RW), f)], axis=1)
    stream = np.concatenate([
        chunks(a["w_in"][0]), pool_b[0:1], conv_b[0:1], pool_b[1:2], conv_b[1:2], chunks(a["w_out"][0]),
        chunks(a["w_q"][0]), keys, chunks(a["w_ada_2"][0]), chunks(w2), chunks(a["w_out_2"][0])])

    def column(v, n):
        v = v.reshape(-1)
        return np.concatenate([v, np.zeros(n * P - v.size, f)]).reshape(n, P).T

    vectors = {
        "g_mix": a["g_mix"], "pool_scale": a["pool_scale"], "conv_w": a["conv_w"], "norm1_g": a["norm1_g_2"],
        "mu": a["rwkv_mu_2"], "w0": a["rwkv_w0_2"], "a0": a["rwkv_a0_2"], "k_k": a["rwkv_k_k_2"],
        "k_a": a["rwkv_k_a_2"], "r_k": a["rwkv_r_k_2"], "ln_g": a["rwkv_ln_g_2"], "ln_b": a["rwkv_ln_b_2"],
        "q_g": np.tile(a["q_norm_g_2"].reshape(-1), 2), "k_g": np.tile(a["k_norm_g_2"].reshape(-1), 2),
        "norm2_g": a["norm2_g_2"], "c": a["c_2"]}
    cols = np.concatenate([column(vectors[n], COLS[n][1]) for n in COLS], axis=1)
    group = a["pool_group_w"][0].transpose(1, 0, 2).reshape(P, 512)
    lora = np.concatenate([a["rwkv_w_up_2"][0], a["rwkv_a_up_2"][0]], axis=0)
    gup = np.concatenate([a["rwkv_g_up_2"][0], np.zeros((2 * P - 160, W2), f)]).reshape(2, P, W2)
    gup = gup.transpose(1, 0, 2).reshape(P, 2 * W2)
    router = a["w_router_2"][0].reshape(KD, P, NE).transpose(1, 0, 2).reshape(P, KD * NE)
    mats = np.concatenate([group, lora, gup, router], axis=1)
    rows = np.concatenate([a["g_ffn"].reshape(-1), a["g_final"].reshape(-1), a["b_router_2"].reshape(-1)])[None]
    bada = a["b_ada_2"].reshape(4, 6 * CW)
    bg = a["b_gate_up_2"][0].reshape(NE, 2, 2, 512).transpose(0, 2, 1, 3).reshape(2 * NE, D)
    bias_moe = np.concatenate([bg, a["b_down_2"][0].reshape(2 * NE, 512)], axis=1)
    arrays = {
        "x": a["x"][0], "stream": stream, "cols": cols, "mats": mats, "rows": rows, "bada": bada,
        "expert_u": a["expert_u"][0], "expert_v": a["expert_v"][0], "w_gate_up": a["w_gate_up_2"][0],
        "w_down": a["w_down_2"][0], "bias_moe": bias_moe}
    arrays = {n: np.ascontiguousarray(v) for n, v in arrays.items()}
    nc = bacc.Bacc("TRN2", target_bir_lowering=False, num_devices=1)
    args = [nc.dram_tensor("in_" + n, v.shape, mybir.dt.from_np(v.dtype), kind="ExternalInput").ap()
            for n, v in arrays.items()]
    out = nc.dram_tensor("out", (T, D), F32, kind="ExternalOutput").ap()
    build(nc, *args, out)
    r = run_bass_kernel_spmd(nc, [{"in_" + n: v for n, v in arrays.items()}], core_ids=[0])
    return r.results[0]["out"].reshape(1, T, D)
```

```python
from contextlib import ExitStack

import numpy as np

import concourse.bass as bass
from concourse import mybir

F32 = mybir.dt.float32
U32 = mybir.dt.uint32
I32 = mybir.dt.int32
ALU = mybir.AluOpType
ACT = mybir.ActivationFunctionType
AX_X = mybir.AxisListType.X

P = 128
D = 1024
T = 256
TT = T // P
KD = D // P
CW = 256
CHUNK = KD * CW
SLOTS = 12

D_IN = 4096
POOL_G = 4
HEADS = 8
HP = 2 * HEADS
NK = 128
TOPK = 16
HK = HEADS * TOPK
EPS = 1e-6
GATHER_SLOTS = 8
PAIR = 2

W2 = 512
RW = 1824
MB = 1536
NH = 8
HD = 64
CL = 32
NC = T // CL
LN_EPS = 64e-5
NE = 32
TOPE = 4
CAP = 64
PASSES = T // CAP
FF = 1024
LIMIT = 7.0
ALPHA = 1.702
NEG = -1.0e30
LOWEST = -3.0e38

S_BANK = (0, 1, 6, 7)

SC_BANK = (6, 7, 0, 1, 6, 7)
PR_BANK = (0, 1, 7, 0, 1, 7)

GRAM_BANK = ((4, 5), (0, 1))

N_Z = D_IN // CW
N_BR = 4
N_O1 = D // CW
N_Q = 2048 // CW
N_KEYS = 1
N_ADA = 6 * D // CW
N_MB = MB // CW
N_RW = -(-RW // CW)
N_O2 = D // CW
C_Z = 0
C_BR = C_Z + N_Z
C_O1 = C_BR + N_BR
C_Q = C_O1 + N_O1
C_KEYS = C_Q + N_Q
C_ADA = C_KEYS + N_KEYS
C_MB = C_ADA + N_ADA
C_RW = C_MB + N_MB
C_O2 = C_RW + N_RW
C_MOE = C_O2 + N_O2
GU_CHUNKS = KD
DN_CHUNKS = 4
E_CHUNKS = GU_CHUNKS + DN_CHUNKS
assert E_CHUNKS == SLOTS
N_PROJ = N_MB + N_RW
LAST = RW % CW
MOD_HEADS = (0,) * 6 + (2,) * 3 + (4,) * 3 + (6,) * 4 + (10,) * 4 + (12,) * 4
MOD_FIRST = 16
assert len(MOD_HEADS) == N_ADA and MOD_HEADS[MOD_FIRST - 1] < HEADS and MOD_HEADS[-1] < 2 * HEADS

N_EARLY = SLOTS - 1
assert N_MB < N_EARLY < N_PROJ - 2

COLS = {}
_at = 0
for _name, _n in (("g_mix", 8), ("pool_scale", 4), ("conv_w", 12), ("norm1_g", 8), ("mu", 16), ("w0", 4),
                  ("a0", 4), ("k_k", 4), ("k_a", 4), ("r_k", 4), ("ln_g", 4), ("ln_b", 4), ("q_g", 1),
                  ("k_g", 1), ("norm2_g", 8), ("c", 8)):
    COLS[_name] = (_at, _n)
    _at += _n
N_COLS = _at
M_GROUP, M_LORA, M_GUP, M_ROUTER = 0, 512, 1024, 2048
N_MATS = M_ROUTER + KD * NE


def build(nc, xd, stream, colsd, matsd, rowsd, badad, expert_u, expert_v, w_gate_up, w_down, bias_moe, out):
    with ExitStack() as ctx:
        def sb(name, shape, dt=F32):
            return ctx.enter_context(nc.sbuf_tensor(name, shape, dt))

        def sem(name):
            return ctx.enter_context(nc.semaphore(name))

        ring = sb("ring", [P, SLOTS, CHUNK])
        xres = sb("xres", [P, TT, D])
        gates = sb("gates", [P, 2, D])
        mats = sb("mats", [P, N_MATS])
        cols = sb("cols", [P, N_COLS])
        modcols = sb("modcols", [P, 4, KD])
        evcols = sb("evcols", [P, 2, KD])
        ident = sb("ident", [P, P])
        ones = sb("ones", [P, P])
        headblk = sb("headblk", [P, P])
        mask_st = sb("mask_st", [P, 2, P])
        mask_ts = sb("mask_ts", [P, P])
        before = sb("before", [P, P])
        iota16 = sb("iota16", [P, TOPK])
        iota_slot = sb("iota_slot", [P, 2 * CAP])
        iota_e = sb("iota_e", [P, NE])
        iota_e2 = sb("iota_e2", [P, NE + 1])
        half_e = sb("half_e", [P, P])
        brow_r = sb("brow_r", [P, NE])
        stat = sb("stat", [P, 8])
        AR = 20480
        arena = sb("arena", [P, AR])
        psum = ctx.enter_context(nc.psum_tensor("psum", [P, 8, 512], F32))

        def area(at, *dims, parts=P):
            n = int(np.prod(dims))
            assert at + n <= AR, (at, dims)
            v = arena[0:parts, at:at + n]
            if len(dims) == 2:
                v = v.rearrange("p (a b) -> p a b", a=dims[0])
            if len(dims) == 3:
                v = v.rearrange("p (a b c) -> p a b c", a=dims[0], b=dims[1])
            return v

        def col(name, i=0):
            at, n = COLS[name]
            assert i < n
            return cols[:, at + i:at + i + 1]

        xn = area(0, TT, D)
        hT = area(2048, KD, T)
        zT = area(4096, 28, T)
        PADW = 16 + T
        u_pad = area(11264, POOL_G, PADW)
        q_a = area(12352, POOL_G, PADW)
        q_b = area(13440, POOL_G, PADW)
        cnt = area(14528, POOL_G, T)
        pT = area(15552, POOL_G, T)
        aT = area(16576, POOL_G, T)
        cv = area(17600, 4, 2 + T)
        cT = area(18632, 4, T)
        mT = area(11264, KD, T)
        gffn = area(14528, D)
        h2 = area(0, TT, D)
        h2T = area(2048, KD, T)
        xn2 = area(4096, TT, D)
        qT = area(10240, HEADS // PAIR, 2 * PAIR, P)
        S = area(4096, TT, HP, NK)
        gat = [area(at, D) for at in (13312, 14528, 19456, 8192, 9216, 10240, 11264, 2048)]
        odd = [area(0, D), area(7168, D)]
        cand = area(12288, PAIR, TOPK * TOPK)
        eq = area(12800, PAIR * TOPK, TOPK)
        brow = area(15552, 6 * CW)
        cb = area(17088, KD, P)
        mrow = area(18112, 2, CW)
        gfin = area(12288, D)
        sm = 18624
        top_s = area(sm, PAIR, 2, TOPK)
        top_i = area(sm + 64, PAIR, 2, TOPK).bitcast(U32)
        top_f = area(sm + 128, PAIR, 2, TOPK)
        fin_s = area(sm + 192, PAIR, TOPK)
        fin_p = area(sm + 224, PAIR, TOPK).bitcast(U32)
        pos_u = area(sm + 256, 2, PAIR * TOPK).bitcast(U32)
        pos_f = area(14336, 2, PAIR * TOPK)
        sel_f = area(14400, 2, PAIR * TOPK)
        stat_c = sb("stat_c", [P, KD])
        gsm = sb("gsm", [P, 4, HEADS])
        peer_g = sb("peer_g", [P, TT, HK])
        peer_i = area(18944, TT, HK).bitcast(U32)
        peer_h = area(19200, TT, HK)
        st_i = sb("st_i", [P, TOPK], U32)
        st_h = sb("st_h", [P, TOPK])

        xn3 = [area(15552, D), area(2048, D)]
        hT3 = area(0, KD, T)
        mqk = area(4096, 2 * 4, T)
        mv = area(6144, TT, W2)
        msq = area(7168, 2 * 4, T)
        mrs = area(9216, 2 * 4, T)
        dist0 = area(11264, P)
        dist1 = area(11392, T)
        sc0 = area(11776, NH, P)
        sc1 = area(12800, NH, T)
        prT = area(7168, NH, TT, P)
        ymT = area(2048, 4, T)
        PT1 = T + 1
        pt = area(16624, 15, PT1)
        ps = area(4096, 15, T)
        r_, k_, v_ = ps[:, 0:4, :], ps[:, 4:8, :], ps[:, 8:12, :]
        wd = area(7936, 4, T)
        aa = area(8960, 4, T)
        gg = area(9984, 4, T)
        kk = area(11008, 4, T)
        t1 = area(12032, 4, T)
        t2 = area(13056, 4, T)
        pc = area(14080, 4, T)
        ar = area(15104, 4, 2, T)
        bt = area(17152, 4, T)
        kt_ = area(18176, 4, T)
        bon = area(19200, 4, T)
        restart = area(3072, T)
        nak = area(0, NH, 2, P)
        pw_s = area(3072, NH, P)
        pw_t = area(4096, NH, P)
        inv = area(5120, NH, P)
        phi = area(3072, P // CL, 4, P)
        gam = area(5120, P // CL, 4, HD)
        tok = area(7168, 4, W2)
        rbk = area(11008, NH, 2, P)
        nts = area(13056, NH, P)
        qt = area(13056, 4, P)
        yT = area(14080, 4, T)
        states = [area(9216 + 256 * i, 4, HD) for i in range(3)]
        states += [mats[:, 256 * i:256 * i + 256].rearrange("p (a b) -> p a b", a=4) for i in range(2)]
        z2 = area(3072, NH, HD)
        dn = area(0, 4, T)
        dsq = area(11008, 4, T)
        drs = area(12032, 4, T)
        ga_t = area(18176, 512)
        xn4 = area(0, TT, D)
        hT4 = area(2048, KD, T)
        acc = area(4096, TT, D)
        xs = area(6144, W2)
        xT = area(6656, 4, P)
        ag = area(7168, 512)
        au = area(7680, 512)
        sg = area(8192, 512)
        act_t = area(8704, 4, P)
        ye = area(9216, 512)
        sct = area(9728, TT, P)
        oh = area(9984, TT, CAP)
        ohw = area(10112, TT, 2 * CAP)
        sel_e = area(10368, P)
        bmoe = area(10496, 3, 512)
        m0 = 12032
        lg = area(m0, TT, NE)
        eqe = area(m0 + 64, TT, NE)
        picks = area(m0 + 128, TT, NE)
        wts = area(m0 + 192, TT, NE)
        rank = area(m0 + 256, TT, NE + 1)
        top8 = area(m0 + 392, TT, 8)
        top8i = area(m0 + 408, TT, 8).bitcast(U32)
        top8f = area(m0 + 424, TT, 8)
        w4 = area(m0 + 440, TT, TOPE)
        wsum = area(m0 + 448, 2, TT)
        most = area(m0 + 452, 1)
        most_i = area(m0 + 453, 1).bitcast(I32)
        mx = gsm[:, 0:2, :]
        pl = peer_g[:, 0, 0:4 * NC].rearrange("p (a b) -> p a b", a=4)

        loaded_x = sem("loaded_x")
        loaded_p = sem("loaded_p")
        loaded_rows = sem("loaded_rows")
        consts = sem("consts")
        const_step = sem("const_step")
        landed = [sem(f"landed{i}") for i in range(SLOTS)]
        chunk_done = sem("chunk_done")
        vec_step = sem("vec_step")
        ms_ready = sem("ms_ready")
        std_ready = sem("std_ready")
        xn_ready = [sem(f"xn_ready{i}") for i in range(4)]
        turned = [sem(f"turned{i}") for i in range(4)]
        hT_ready = [sem(f"hT_ready{i}") for i in range(4)]
        z_out = sem("z_out")
        p_ready = sem("p_ready")
        group_mm = sem("group_mm")
        a_ready = sem("a_ready")
        c_ready = sem("c_ready")
        br_mm = sem("br_mm")
        m_ready = sem("m_ready")
        x_mid = sem("x_mid")
        part_mm = sem("part_mm")
        part_out = sem("part_out")
        s_mm = sem("s_mm")
        s_out = sem("s_out")
        exp_in = sem("exp_in")
        exp_out = sem("exp_out")
        idx_ready = sem("idx_ready")
        staged = sem("staged")
        free_seen = sem("free_seen")
        row_in = [sem(f"row_in{i}") for i in range(GATHER_SLOTS)]
        row_used = sem("row_used")
        head_kept = sem("head_kept")
        dots_done = sem("dots_done")
        gelu_done = sem("gelu_done")
        cb_sig = sem("cb_sig")
        cb_ready = sem("cb_ready")
        ada_out = sem("ada_out")
        mcol_mm = sem("mcol_mm")
        mcol_out = sem("mcol_out")
        ev_ready = sem("ev_ready")
        stored = sem("stored")
        proj_out = sem("proj_out")
        bias_made = sem("bias_made")
        msq_ready = sem("msq_ready")
        msum_mm = sem("msum_mm")
        m_norm = sem("m_norm")
        mqk_ready = sem("mqk_ready")
        sc_mm = sem("sc_mm")
        sc_read = sem("sc_read")
        mexp_in = sem("mexp_in")
        mexp_out = sem("mexp_out")
        prob_ready = sem("prob_ready")
        pr_mm = sem("pr_mm")
        prT_ready = sem("prT_ready")
        pv_mm = sem("pv_mm")
        ym_ready = sem("ym_ready")
        ps_ready = sem("ps_ready")
        lora_in = sem("lora_in")
        lora_mm = sem("lora_mm")
        sig_out = sem("sig_out")
        dec_out = sem("dec_out")
        ksq_ready = sem("ksq_ready")
        ksum_mm = sem("ksum_mm")
        kn_in = sem("kn_in")
        log_ready = sem("log_ready")
        knorm_out = sem("knorm_out")
        rkk_ready = sem("rkk_ready")
        bon_mm = sem("bon_mm")
        tilde = sem("tilde")
        tok_mm = sem("tok_mm")
        tok_ready = sem("tok_ready")
        gram_mm = sem("gram_mm")
        gram_out = sem("gram_out")
        nt_mm = sem("nt_mm")
        nt_out = sem("nt_out")
        ps_mm = sem("ps_mm")
        ps_out = sem("ps_out")
        pt_mm = sem("pt_mm")
        pt_out = sem("pt_out")
        ix_mm = sem("ix_mm")
        ix_out = sem("ix_out")
        wu_mm = sem("wu_mm")
        wu_out = sem("wu_out")
        q2_mm = sem("q2_mm")
        q2_out = sem("q2_out")
        yp_mm = sem("yp_mm")
        yp_out = sem("yp_out")
        fg_mm = sem("fg_mm")
        fg_out = sem("fg_out")
        st_mm = sem("st_mm")
        st_out = sem("st_out")
        ys_mm = sem("ys_mm")
        ys_out = sem("ys_out")
        ln_mm = sem("ln_mm")
        ln_sq = sem("ln_sq")
        ln_norm = sem("ln_norm")
        y_done = sem("y_done")
        router_mm = sem("router_mm")
        wexp_in = sem("wexp_in")
        wexp_out = sem("wexp_out")
        picks_ready = sem("picks_ready")
        count_ready = sem("count_ready")
        loaded_b = sem("loaded_b")
        oh_ready = sem("oh_ready")
        ohw_ready = sem("ohw_ready")
        sel_ready = sem("sel_ready")
        g_mm = sem("g_mm")
        xs_ready = sem("xs_ready")
        xt_mm = sem("xt_mm")
        xT_ready = sem("xT_ready")
        gu_mm = sem("gu_mm")
        xt_scaled = sem("xt_scaled")
        up_ready = sem("up_ready")
        rk_made = sem("rk_made")
        gate_ready = sem("gate_ready")
        gu_read = sem("gu_read")
        sg_ready = sem("sg_ready")
        act_ready = sem("act_ready")
        at_mm = sem("at_mm")
        actT_ready = sem("actT_ready")
        y_mm = sem("y_mm")
        ye_ready = sem("ye_ready")
        sct_mm = sem("sct_mm")
        sct_ready = sem("sct_ready")
        sum_mm = sem("sum_mm")
        acc_done = sem("acc_done")
        out_ready = sem("out_ready")

        def uses(n):
            return 16 * (n // SLOTS + 1)

        def slot(n):
            return ring[:, n % SLOTS, :]

        def wide(n):
            return slot(n).rearrange("p (k c) -> p k c", k=KD)

        def further_passes(eng, work):
            eng.wait_ge(count_ready, 1)
            count = eng.value_load(most_i[0:1, 0:1], min_val=0, max_val=T)
            with eng.Fori(1, PASSES) as p:
                with eng.If(count > p * CAP):
                    work(p)

        block = ctx.enter_context(nc.Block())

        @block.sync
        def _(sp):
            sp.dma_start(cols[:], colsd).then_inc(loaded_x, 16)
            sp.dma_start(xres[:], xd.rearrange("(a p) d -> p a d", p=P)).then_inc(loaded_x, 16)
            for j in range(SLOTS):
                sp.dma_start(ring[:, j, :], stream[j]).then_inc(landed[j], 16)
            whole = (C_MB + N_PROJ - 1) // SLOTS
            with sp.Fori(1, whole) as i:
                for j in range(SLOTS):
                    sp.wait_ge(chunk_done, i * SLOTS + (j - SLOTS + 1))
                    sp.dma_start(ring[:, j, :], stream[i * SLOTS + j]).then_inc(landed[j], 16)
            for n in range(whole * SLOTS, C_MOE):
                sp.wait_ge(chunk_done, n - SLOTS + 1)
                width = KD * LAST if n == C_MB + N_PROJ - 1 else CHUNK
                sp.dma_start(slot(n)[:, 0:width], stream[n, :, 0:width]).then_inc(landed[n % SLOTS], 16)

            def experts(p):
                with sp.Fori(0, NE) as e:
                    for j in range(E_CHUNKS):
                        n = C_MOE + j
                        sp.wait_ge(chunk_done, e * E_CHUNKS + (p * (NE * E_CHUNKS) + (n - SLOTS + 1)))
                        if j < GU_CHUNKS:
                            src = w_gate_up[e, j * P:(j + 1) * P, :]
                            dst = slot(n)
                        else:
                            q = j - GU_CHUNKS
                            src = w_down[e, q * 2 * P:(q + 1) * 2 * P, :].rearrange("(k p) c -> p k c", p=P)
                            dst = slot(n).rearrange("p (k c) -> p k c", k=2)
                        sp.dma_start(dst, src).then_inc(landed[n % SLOTS], 16)

            experts(0)
            further_passes(sp, experts)
            for tt in range(TT):
                sp.wait_ge(out_ready, tt + 1)
                sp.dma_start(out[tt * P:(tt + 1) * P, :], xres[:, tt, :]).then_inc(stored, 16)
            sp.wait_ge(stored, 16 * TT)

        @block.gpsimd
        def _(pool):
            made = [0]

            def make(ins):
                made[0] += 1
                ins.then_inc(const_step, 1)
                pool.wait_ge(const_step, made[0])

            def number(out, pattern, base=0, by_row=0):
                return pool.iota(out, pattern, base=base, channel_multiplier=by_row,
                                 allow_small_or_imprecise_dtypes=True)

            def keep(m, src, pattern, op, base=0, by_row=0):
                return pool.affine_select(out=m, in_=src, compare_op=op, fill=0.0, base=base, pattern=pattern,
                                          channel_multiplier=by_row)

            make(pool.memset(ident[:], 0.0))
            make(pool.memset(ones[:], 1.0))
            make(pool.affine_select(out=ident[:], in_=ident[:], compare_op=ALU.not_equal, fill=1.0, base=0,
                                    pattern=[[-1, P]], channel_multiplier=1))
            make(number(cnt, [[0, POOL_G], [1, T]], base=1))
            make(number(iota16[:], [[1, TOPK]]))
            make(pool.memset(stat[:, 6:7], EPS))
            make(pool.memset(stat[:, 7:8], LN_EPS))
            make(number(iota_slot[:], [[0, 2], [1, CAP]]))
            make(number(iota_e[:], [[1, NE]]))
            make(number(iota_e2[:], [[2, NE + 1]]))
            make(number(half_e[0:2 * NE, :], [[-1, 2], [0, CAP]], by_row=1))
            hb = headblk[:].rearrange("p (b c) -> p b c", b=2)
            make(keep(hb, ones[:].rearrange("p (b c) -> p b c", b=2), [[-HD, 2], [0, HD]], ALU.is_ge, by_row=1))
            make(keep(hb, hb, [[HD, 2], [0, HD]], ALU.is_ge, base=HD - 1, by_row=-1))
            make(keep(before[:], ones[:], [[1, P]], ALU.is_gt, by_row=-1))
            in_chunks = [[-CL, P // CL], [0, CL]]
            for m, op in ((0, ALU.is_gt), (1, ALU.is_ge)):
                mm = mask_st[:, m, :]
                make(keep(mm, ones[:], [[1, P]], op, by_row=-1))
                mm = mm.rearrange("p (b c) -> p b c", c=CL)
                make(keep(mm, mm, in_chunks, ALU.is_ge, by_row=1))
            mm = mask_ts[:]
            make(keep(mm, ones[:], [[-1, P]], ALU.is_gt, by_row=1))
            mm = mm.rearrange("p (b c) -> p b c", c=CL)
            make(keep(mm, mm, [[CL, P // CL], [0, CL]], ALU.is_ge, base=CL - 1, by_row=-1))
            pool.sem_inc(consts, 1)

            def gather(table, tt, first):
                with pool.Fori(0, HEADS) as i:
                    for q in range(TOPK // GATHER_SLOTS):
                        at = q * GATHER_SLOTS
                        pool.wait_ge(idx_ready, i + (tt * HEADS + 1))
                        pool.sem_inc(free_seen, 1)
                        pool.tensor_copy(st_i[:, at:at + GATHER_SLOTS],
                                         peer_i[:, tt, bass.ds(i * TOPK + at, GATHER_SLOTS)]).then_inc(staged, 1)
                        pool.wait_ge(staged, i * (TOPK // GATHER_SLOTS) + (first // GATHER_SLOTS + q + 1))
                        for k in range(GATHER_SLOTS):
                            if k == 5:
                                pool.wait_ge(s_mm, TT * HP // 4)
                            pool.wait_ge(row_used, i * TOPK + (first + at + k + 1))
                            pool.sem_inc(free_seen, 1)
                            pool.indirect_dma_start(gat[k], None, table,
                                                    bass.IndirectOffsetOnAxis(st_i[:, at + k:at + k + 1], 0)
                                                    ).then_inc(row_in[k], 16)

            for n, (table, tt) in enumerate(((expert_u, 0), (expert_v, 0), (expert_u, 1), (expert_v, 1))):
                gather(table, tt, n * HK)
            pool.wait_ge(xn_ready[2], TT)
            at = made[0]
            for tt, m in ((0, dist0), (1, dist1)):
                n = m.shape[-1]
                make(number(m, [[1, n]], base=-tt * P, by_row=-1))
                make(pool.affine_select(out=m, in_=m, compare_op=ALU.is_ge, fill=NEG, base=tt * P,
                                        pattern=[[-1, n]], channel_multiplier=1))
            for sc, m in ((sc0, dist0), (sc1, dist1)):
                for par in range(2):
                    for c in range(4):
                        pool.tensor_scalar(sc[:, 4 * par + c, :], m, 2.0 ** -(2 * c + par + 1), None,
                                           ALU.mult).then_inc(bias_made, 1)
            pool.wait_ge(y_done, 1)
            pool.memset(acc, 0.0).then_inc(consts, 1)

        @block.scalar
        def _(act):
            act.dma_start(mats[:], matsd).then_inc(loaded_p, 16)
            act.dma_start(brow_r[:], rowsd[:, 2 * D:2 * D + NE].to_broadcast([P, NE])).then_inc(loaded_p, 16)

            norms = [0]

            def deviation(tt):
                norms[0] += 1
                act.wait_ge(ms_ready, norms[0])
                act.activation(stat[:, 2 + tt:3 + tt], stat[:, tt:tt + 1], ACT.Sqrt).then_inc(std_ready, 1)

            def tile_turned(n, dst, tt, banks, scale=None, bias=None):
                for j in range(2):
                    act.wait_ge(turned[n], 2 * tt + j + 1)
                    ts = slice(tt * P, (tt + 1) * P)
                    src = psum[:, banks[j], :].rearrange("p (a t) -> p a t", a=4)
                    if scale is None:
                        act.copy(dst[:, 4 * j:4 * j + 4, ts], src).then_inc(hT_ready[n], 4)
                    else:
                        for i in range(4):
                            k = 4 * j + i
                            act.activation(dst[:, k, ts], src[:, i, :], ACT.Identity, scale=scale(k),
                                           bias=bias(k)).then_inc(hT_ready[n], 1)

            act.sem_inc(ye_ready, 1)
            act.sem_inc(sct_ready, 1)
            for tt in range(TT):
                deviation(tt)
            for k in range(KD):
                act.wait_ge(turned[0], k + 1)
                act.activation(hT[:, k, :], psum[:, k % 4, 0:T], ACT.Copy, scale=col("g_mix", k)).then_inc(hT_ready[0], 1)
            for n in range(N_Z):
                act.wait_ge(chunk_done, C_Z + n + 1)
                src = psum[:, 2 + n % 4, :].rearrange("p (a t) -> p a t", a=2)
                if n < 2:
                    act.copy(u_pad[:, 2 * n:2 * n + 2, 16:16 + T], src).then_inc(z_out, 1)
                elif n < 8:
                    act.copy(zT[:, 2 * n - 4:2 * n - 2, :], src).then_inc(z_out, 1)
                else:
                    act.activation(zT[:, 2 * n - 4:2 * n - 2, :], src, ACT.Sigmoid).then_inc(z_out, 1)
            act.wait_ge(group_mm, 1)
            for g in range(POOL_G):
                act.activation(aT[:, g, :], psum[:, 6 + g // 2, (g % 2) * T:(g % 2) * T + T], ACT.Copy,
                               scale=col("pool_scale", g)).then_inc(a_ready, 1)
            act.wait_ge(m_ready, KD)
            act.activation(modcols[:, 0, :], cols[:, COLS["c"][0]:COLS["c"][0] + KD], ACT.Sigmoid).then_inc(cb_sig, 1)
            act.dma_start(gffn, rowsd[:, 0:D].to_broadcast([P, D])).then_inc(loaded_rows, 16)
            act.dma_start(brow[0:97:32, :], badad).then_inc(loaded_rows, 16)
            for tt in range(TT):
                deviation(tt)
            tile_turned(1, h2T, 0, (0, 1))
            def scores_kept(n):
                act.wait_ge(s_mm, n + 1)
                act.copy(S[:, n // 4, 4 * (n % 4):4 * (n % 4) + 4, :],
                         psum[:, S_BANK[n % 4], :].rearrange("p (a c) -> p a c", a=4)).then_inc(s_out, 1)

            for n in range(TT * HEADS // PAIR):
                m = n % 4
                if n < 4:
                    act.wait_ge(part_mm, 2 + m + 1)
                else:
                    act.wait_ge(chunk_done, C_Q + 2 * m + 2)
                act.copy(qT[:, m, :, :], psum[:, 2 + m, :].rearrange("p (a t) -> p a t", a=4)).then_inc(part_out, 1)
                if n == 0:
                    tile_turned(1, h2T, 1, (6, 7))
                    scores_kept(0)
                elif n > 1:
                    scores_kept(n - 1)
            scores_kept(TT * HEADS // PAIR - 1)

            def mod_chunk(n):
                act.wait_ge(chunk_done, C_ADA + n + 1)
                part, at = n // 4, (n % 4) * CW
                src = psum[:, 4 + n % 2, 0:CW]
                if part in (2, 5):
                    act.copy(gates[:, part // 3, at:at + CW], src).then_inc(ada_out, 1)
                else:
                    w = part if part < 2 else part - 1
                    act.copy(mrow[0:1, n % 2, :], src[0:1]).then_inc(ada_out, 1)
                    m = sum(1 for x in range(n) if x // 4 not in (2, 5))
                    act.wait_ge(mcol_mm, m + 1)
                    act.copy(modcols[:, w, 2 * (n % 4):2 * (n % 4) + 2], psum[:, 6, 0:2]).then_inc(mcol_out, 1)

            act.wait_ge(cb_ready, KD)
            def gate_exp(tt):
                act.wait_ge(exp_in, (tt + 1) * (HEADS // PAIR))
                act.activation(peer_g[:, tt, :], peer_g[:, tt, :], ACT.Exp).then_inc(exp_out, 1)

            def gelu(tt):
                act.wait_ge(dots_done, tt + 1)
                act.activation(peer_h[:, tt, :], peer_h[:, tt, :], ACT.Gelu).then_inc(gelu_done, 1)

            def shifted(tt, banks):
                act.wait_ge(ev_ready, 2)
                tile_turned(2, hT3, tt, banks, lambda k: evcols[:, 0, k:k + 1], lambda k: modcols[:, 0, k:k + 1])

            def projected(n, tt=None):
                a, b = (0, T) if tt is None else (tt * P, (tt + 1) * P)
                src = psum[:, 2 + n % 4, 0:2 * (b - a)].rearrange("p (a t) -> p a t", a=2)
                if n < 4:
                    return act.copy(mqk[:, 2 * n:2 * n + 2, a:b], src)
                if n < N_MB:
                    return act.copy(mv[:, tt, (n - 4) * CW:(n - 3) * CW], psum[:, 2 + n % 4, 0:CW])
                m = n - N_MB
                if n < N_PROJ - 1:
                    return act.copy(pt[:, 2 * m:2 * m + 2, 1 + a:1 + b], src)
                return act.copy(pt[0:LAST, 14, 1 + a:1 + b], src[0:LAST, 0, :])

            for n in range(MOD_FIRST):
                mod_chunk(n)
            gate_exp(0)
            gelu(0)
            for n in range(MOD_FIRST, N_ADA):
                mod_chunk(n)
            gate_exp(1)
            act.wait_ge(idx_ready, TT * HEADS)
            act.dma_start(gfin, rowsd[:, D:2 * D].to_broadcast([P, D])).then_inc(loaded_rows, 16)
            deviation(0)
            deviation(0)
            gelu(1)
            shifted(0, (0, 1))
            for n in range(N_EARLY):
                act.wait_ge(part_mm, 2 + HP // 4 + n + 1)
                projected(n, 0).then_inc(part_out, 1)
            deviation(1)
            deviation(1)
            shifted(1, (6, 7))

            def late(n):
                act.wait_ge(chunk_done, C_MB + n + 1)
                projected(n, 1 if n < N_EARLY else None).then_inc(proj_out, 1)

            def weights(tt, sc):
                act.wait_ge(mexp_in, tt + 1)
                act.activation(sc, sc, ACT.Exp).then_inc(mexp_out, 1)

            def turned_weights(i):
                act.wait_ge(pr_mm, i + 1)
                src = psum[:, PR_BANK[i], :]
                if i < 2:
                    act.copy(prT[:, 4 * i:4 * i + 4, 0, :], src.rearrange("p (a t) -> p a t", a=4)).then_inc(prT_ready, 1)
                else:
                    act.copy(prT[:, 2 * i - 4:2 * i - 2, :, :],
                             src.rearrange("p (a b t) -> p a b t", a=2, b=2)).then_inc(prT_ready, 1)

            def attended(tt):
                act.wait_ge(pv_mm, tt + 1)
                act.copy(ymT[:, :, tt * P:(tt + 1) * P],
                         psum[:, 6, :].rearrange("p (a t) -> p a t", a=4)).then_inc(ym_ready, 1)

            for n in range(5):
                late(n)
            for b in range(4):
                act.wait_ge(msum_mm, b + 1)
                act.activation(mrs[:, 2 * b:2 * b + 2, :], psum[:, (6, 7, 0, 1)[b], :].rearrange("p (a t) -> p a t", a=2),
                               ACT.Ln, scale=1.0 / HD, bias=stat[:, 6:7]).then_inc(m_norm, 1)
            for i in range(2):
                act.wait_ge(m_norm, 2 * i + 2)
                act.activation(mrs[:, 4 * i:4 * i + 4, :], mrs[:, 4 * i:4 * i + 4, :], ACT.Exp,
                               scale=-0.5).then_inc(m_norm, 1)
            late(5)
            late(N_MB + 0)
            weights(0, sc0)
            late(N_MB + 1)
            late(N_MB + 2)
            weights(1, sc1)
            turned_weights(0)
            turned_weights(1)
            late(N_MB + 3)
            attended(0)
            for i in range(2, 5):
                turned_weights(i)
            late(N_MB + 4)
            turned_weights(5)
            late(N_MB + 5)
            attended(1)
            late(N_MB + 6)
            late(N_MB + 7)
            act.wait_ge(ps_ready, 1)
            act.activation(ps[0:64, 12, :], ps[0:64, 12, :], ACT.Tanh).then_inc(lora_in, 1)
            act.activation(ps[:, 13, :], ps[:, 13, :], ACT.Sigmoid).then_inc(lora_in, 1)
            act.activation(ps[0:LAST, 14, :], ps[0:LAST, 14, :], ACT.Sigmoid).then_inc(lora_in, 1)
            for i, dst, bias in ((0, wd, "w0"), (1, aa, "a0")):
                act.wait_ge(lora_mm, i + 1)
                for c in range(4):
                    src = psum[:, 2 * i + c // 2, (c % 2) * T:(c % 2) * T + T]
                    act.activation(dst[:, c, :], src, ACT.Sigmoid, bias=col(bias, c)).then_inc(sig_out, 1)
            act.wait_ge(lora_mm, 3)
            for b in range(2):
                act.copy(gg[:, 2 * b:2 * b + 2, :],
                         psum[:, 4 + b, :].rearrange("p (a t) -> p a t", a=2)).then_inc(sig_out, 1)
            act.wait_ge(kn_in, 2)
            act.activation(t1, t1, ACT.Ln).then_inc(knorm_out, 1)
            act.wait_ge(knorm_out, 1)
            act.activation(t1, t1, ACT.Exp, scale=-0.5).then_inc(knorm_out, 1)
            c = float(np.exp(-0.5))
            act.wait_ge(log_ready, 1)
            act.activation(bt, pc, ACT.Exp, scale=c).then_inc(dec_out, 1)
            act.wait_ge(dec_out, 1)
            act.activation(pc, pc, ACT.Exp, scale=-c).then_inc(dec_out, 1)
            act.activation(wd, wd, ACT.Exp, scale=-c).then_inc(dec_out, 1)
            for tt in range(TT):
                for i in range(0, 4, 2):
                    act.wait_ge(tok_mm, 4 * tt + i + 1)
                    act.copy(tok[:, i, :], psum[:, i, :]).then_inc(tok_ready, 1)
                for lv in range(1, 5):
                    dst = (nts, pw_t)[lv % 2]
                    for q in range(2):
                        act.wait_ge(pt_mm, 8 * tt + 2 * (lv - 1) + q + 1)
                        act.copy(dst[:, 4 * q:4 * q + 4, :],
                                 psum[:, 2 + q, :].rearrange("p (a t) -> p a t", a=4)).then_inc(pt_out, 1)
                act.wait_ge(yp_mm, tt + 1)
                act.copy(yT[:, :, tt * P:(tt + 1) * P],
                         psum[:, 1, :].rearrange("p (a t) -> p a t", a=4)).then_inc(yp_out, 1)
            for b in range(2):
                act.wait_ge(ln_mm, 3 + b)
                act.activation(drs[:, 2 * b:2 * b + 2, :], psum[:, 2 + b, :].rearrange("p (a t) -> p a t", a=2),
                               ACT.Ln, scale=1.0 / HD, bias=stat[:, 7:8]).then_inc(ln_norm, 1)
            act.wait_ge(ln_norm, 2)
            act.activation(drs, drs, ACT.Exp, scale=-0.5).then_inc(ln_norm, 1)
            for tt in range(TT):
                deviation(tt)
                tile_turned(3, hT4, tt, (0, 1) if tt == 0 else (2, 3), lambda k: evcols[:, 1, k:k + 1],
                            lambda k: modcols[:, 2, k:k + 1])
            act.dma_start(bmoe[0:2 * NE], bias_moe.rearrange("r (a c) -> r a c", a=3)).then_inc(loaded_b, 16)
            act.wait_ge(wexp_in, 1)
            act.activation(w4, w4, ACT.Exp).then_inc(wexp_out, 1)

            def front(f):
                act.wait_ge(g_mm, f + 2)
                act.copy(xs, psum[:, 2, :]).then_inc(xs_ready, 1)

            def experts(p):
                front(p * (NE + 1))
                with act.Fori(0, NE) as e:
                    it = p * NE + e
                    f = p * (NE + 1) + e
                    act.wait_ge(gate_ready, it + 1)
                    act.activation(sg, ag, ACT.Sigmoid, scale=ALPHA).then_inc(sg_ready, 1)
                    front(f + 1)
                    act.wait_ge(at_mm, it + 1)
                    act.copy(act_t, psum[:, 4, :].rearrange("p (a t) -> p a t", a=4)).then_inc(actT_ready, 1)
                    act.wait_ge(sct_mm, it + 2)
                    act.copy(sct, psum[:, 2, 0:2 * P].rearrange("p (a t) -> p a t", a=2)).then_inc(sct_ready, 1)
                    act.wait_ge(y_mm, it + 1)
                    act.copy(ye, psum[:, 5, :]).then_inc(ye_ready, 1)

            experts(0)
            further_passes(act, experts)

        @block.vector
        def _(dve):
            steps = [0]

            def ordered(ins):
                steps[0] += 1
                ins.then_inc(vec_step, 1)
                dve.wait_ge(vec_step, steps[0])

            norms = [0]

            def norm(tt, dst, src):
                norms[0] += 1
                dve.tensor_tensor_reduce(dst, src, src, 1.0 / D, EPS, ALU.mult, ALU.add,
                                         stat[:, tt:tt + 1]).then_inc(ms_ready, 1)
                dve.wait_ge(std_ready, norms[0])
                ordered(dve.reciprocal(stat[:, 4 + tt:5 + tt], stat[:, 2 + tt:3 + tt]))
                dve.wait_ge(ms_ready, norms[0])

            def scaled(tt, dst, src):
                return dve.tensor_scalar(dst, src, stat[:, 4 + tt:5 + tt], None, ALU.mult)

            dve.sem_inc(row_used, GATHER_SLOTS)
            dve.sem_inc(gu_read, 1)
            dve.sem_inc(acc_done, 1)
            dve.memset(u_pad[:, :, 0:16], 0.0)
            dve.memset(q_a[:, :, 0:16], 0.0)
            dve.memset(q_b[:, :, 0:16], 0.0)
            ordered(dve.memset(cv[:, :, 0:2], 0.0))
            dve.wait_ge(loaded_x, 32)
            for tt in range(TT):
                norm(tt, xn[:, tt, :], xres[:, tt, :])
                scaled(tt, xn[:, tt, :], xres[:, tt, :]).then_inc(xn_ready[0], 1)
            dve.wait_ge(consts, 1)
            for g in range(POOL_G):
                dve.tensor_scalar(cnt[:, g, :], cnt[:, g, :], float(2 << g), None, ALU.min).then_inc(vec_step, 1)
            steps[0] += POOL_G
            dve.wait_ge(vec_step, steps[0])
            ordered(dve.reciprocal(cnt, cnt))
            dve.wait_ge(z_out, 2)
            ordered(dve.tensor_tensor(q_a[:, :, 16:], u_pad[:, :, 16:], u_pad[:, :, 15:15 + T], ALU.add))
            ordered(dve.tensor_tensor(q_b[:, 1:, 16:], q_a[:, 1:, 16:], q_a[:, 1:, 14:14 + T], ALU.add))
            ordered(dve.tensor_tensor(q_a[:, 2:, 16:], q_b[:, 2:, 16:], q_b[:, 2:, 12:12 + T], ALU.add))
            ordered(dve.tensor_tensor(q_b[:, 3:, 16:], q_a[:, 3:, 16:], q_a[:, 3:, 8:8 + T], ALU.add))
            dve.tensor_tensor(pT[:, 0:4:2, :], q_a[:, 0:4:2, 16:], cnt[:, 0:4:2, :], ALU.mult).then_inc(vec_step, 1)
            steps[0] += 1
            ordered(dve.tensor_tensor(pT[:, 1:4:2, :], q_b[:, 1:4:2, 16:], cnt[:, 1:4:2, :], ALU.mult))
            dve.tensor_tensor(pT, pT, u_pad[:, :, 16:], ALU.subtract).then_inc(p_ready, 1)
            dve.wait_ge(z_out, 8)
            ordered(dve.tensor_tensor(cv[:, :, 2:], zT[:, 0:4, :], zT[:, 8:12, :], ALU.mult))
            for t in range(4):
                dve.tensor_scalar(cT[:, t, :], cv[:, t, 0:T], col("conv_w", t), None, ALU.mult).then_inc(vec_step, 1)
            steps[0] += 4
            dve.wait_ge(vec_step, steps[0])
            for w in (1, 2):
                for t in range(4):
                    dve.scalar_tensor_tensor(cT[:, t, :], cv[:, t, w:w + T], col("conv_w", 4 * w + t), cT[:, t, :],
                                             ALU.mult, ALU.add).then_inc(vec_step, 1)
                steps[0] += 4
                dve.wait_ge(vec_step, steps[0])
            dve.tensor_tensor(cT, cT, zT[:, 4:8, :], ALU.mult).then_inc(c_ready, 1)
            dve.wait_ge(z_out, N_Z)
            dve.wait_ge(p_ready, 1)
            for k in range(KD):
                dve.wait_ge(br_mm, k + 1)
                ab = psum[:, 2 + k % 4, :].rearrange("p (a t) -> p a t", a=2)
                ga = zT[:, 12 + k, :]
                gb = zT[:, 20 + k, :]
                dve.tensor_tensor(ga, ab[:, 0, :], ga, ALU.mult).then_inc(vec_step, 1)
                steps[0] += 1
                ordered(dve.tensor_tensor(gb, ab[:, 1, :], gb, ALU.mult))
                dve.tensor_tensor(mT[:, k, :], ga, gb, ALU.add).then_inc(m_ready, 1)
            for tt in range(TT):
                for m in range(N_O1 // 2):
                    if tt == 0:
                        dve.wait_ge(part_mm, m + 1)
                    else:
                        dve.wait_ge(chunk_done, C_O1 + 2 * m + 2)
                    cs = slice(2 * m * CW, 2 * (m + 1) * CW)
                    dve.tensor_tensor(xres[:, tt, cs], psum[:, 2 + 2 * tt + m, :], xres[:, tt, cs],
                                      ALU.add).then_inc(x_mid, 1)
                dve.wait_ge(x_mid, (tt + 1) * (N_O1 // 2))
                norm(tt, xn2[:, tt, :], xres[:, tt, :])
                dve.wait_ge(loaded_rows, 32)
                ordered(scaled(tt, xn2[:, tt, :], xres[:, tt, :]))
                dve.tensor_tensor(h2[:, tt, :], xn2[:, tt, :], gffn, ALU.mult).then_inc(xn_ready[1], 1)
            dve.wait_ge(cb_sig, 1)
            at = COLS["c"][0]
            ordered(dve.tensor_tensor(stat_c[:], cols[:, at:at + KD], modcols[:, 0, :], ALU.mult))
            for k in range(KD):
                dve.tensor_scalar(cb[:, k, :], ones[:], stat_c[:, k:k + 1], None, ALU.mult).then_inc(cb_ready, 1)

            def top16(n, val, ind, of):
                for r in range(2):
                    for i in range(n):
                        dve.max(val(i, r), of(i)).then_inc(vec_step, 1)
                    steps[0] += n
                    dve.wait_ge(vec_step, steps[0])
                    for i in range(n):
                        dve.max_index(ind(i, r), val(i, r), of(i)).then_inc(vec_step, 1)
                    steps[0] += n
                    dve.wait_ge(vec_step, steps[0])
                    if r == 0:
                        for i in range(n):
                            dve.match_replace(of(i), val(i, r), of(i), LOWEST).then_inc(vec_step, 1)
                        steps[0] += n
                        dve.wait_ge(vec_step, steps[0])

            def select_keys(tt, pair):
                dve.wait_ge(s_out, tt * (HP // 4) + pair + 1)
                top16(2 * PAIR, lambda i, r: top_s[:, i // 2, i % 2, 8 * r:8 * r + 8],
                      lambda i, r: top_i[:, i // 2, i % 2, 8 * r:8 * r + 8], lambda i: S[:, tt, 2 * PAIR * pair + i, :])

            def select_experts(tt, pair):
                c4 = cand.rearrange("p h (a b) -> p h a b", a=TOPK)
                shape = [P, PAIR, TOPK, TOPK]
                ordered(dve.tensor_tensor(c4, top_s[:, :, 0, :].unsqueeze(3).to_broadcast(shape),
                                          top_s[:, :, 1, :].unsqueeze(2).to_broadcast(shape), ALU.add))
                top16(PAIR, lambda i, r: fin_s[:, i, 8 * r:8 * r + 8], lambda i, r: fin_p[:, i, 8 * r:8 * r + 8],
                      lambda i: cand[:, i, :])
                at = slice(PAIR * pair * TOPK, PAIR * (pair + 1) * TOPK)
                dve.tensor_tensor(peer_g[:, tt, at].rearrange("p (h k) -> p h k", h=PAIR), fin_s,
                                  fin_s[:, :, 0:1].to_broadcast([P, PAIR, TOPK]), ALU.subtract).then_inc(exp_in, 1)
                flat_p = fin_p.rearrange("p h k -> p (h k)")
                ordered(dve.tensor_copy(top_f, top_i))
                ordered(dve.tensor_scalar(pos_u[:, 0, :], flat_p, 4, None, ALU.logical_shift_right))
                ordered(dve.tensor_scalar(pos_u[:, 1, :], flat_p, 15, None, ALU.bitwise_and))
                ordered(dve.tensor_copy(pos_f, pos_u))
                sh = [P, PAIR * TOPK, TOPK]
                for half in range(2):
                    ordered(dve.tensor_tensor(eq, pos_f[:, half, :].unsqueeze(2).to_broadcast(sh),
                                              iota16[:].unsqueeze(1).to_broadcast(sh), ALU.is_equal))
                    e4 = eq.rearrange("p (h k) a -> p h k a", h=PAIR)
                    ordered(dve.tensor_tensor(e4, e4, top_f[:, :, half, :].unsqueeze(2).to_broadcast(shape), ALU.mult))
                    ordered(dve.tensor_reduce(sel_f[:, half, :], eq, AX_X, ALU.add))
                ordered(dve.scalar_tensor_tensor(sel_f[:, 0, :], sel_f[:, 0, :], float(NK), sel_f[:, 1, :],
                                                 ALU.mult, ALU.add))
                dve.tensor_copy(peer_i[:, tt, at], sel_f[:, 0, :]).then_inc(idx_ready, PAIR)

            def arrivals(i, first, k):
                return i * (16 * TOPK // GATHER_SLOTS) + 16 * ((first + k) // GATHER_SLOTS + 1)

            def dots(tt, pair):
                h0 = 2 * tt * HEADS + PAIR * pair
                first = h0 * TOPK
                with dve.Fori(0, PAIR) as i:
                    for k in range(TOPK):
                        dve.wait_ge(row_in[k % GATHER_SLOTS], arrivals(i, first, k))
                        g = gat[k % GATHER_SLOTS]
                        dve.tensor_tensor_reduce(g, g, h2[:, tt, :], 1.0, 0.0, ALU.mult, ALU.add,
                                                 st_h[:, k:k + 1]).then_inc(row_used, 1)
                    dve.wait_ge(row_used, i * TOPK + (first + TOPK + GATHER_SLOTS))
                    dve.tensor_copy(peer_h[:, tt, bass.ds(i * TOPK + PAIR * pair * TOPK, TOPK)],
                                    st_h[:]).then_inc(head_kept, 1)
                    dve.wait_ge(head_kept, i + (h0 + 1))

            def weights(tt):
                dve.wait_ge(exp_out, tt + 1)
                g3 = peer_g[:, tt, :].rearrange("p (h k) -> p h k", h=HEADS)
                ordered(dve.tensor_reduce(gsm[:, tt, :], g3, AX_X, ALU.add))
                ordered(dve.reciprocal(gsm[:, 2 + tt, :], gsm[:, tt, :]))
                ordered(dve.tensor_tensor(g3, g3, gsm[:, 2 + tt, :].unsqueeze(2).to_broadcast([P, HEADS, TOPK]),
                                          ALU.mult))
                ordered(dve.memset(odd[tt], 0.0))
                dve.wait_ge(gelu_done, tt + 1)
                ordered(dve.tensor_tensor(peer_h[:, tt, :], peer_h[:, tt, :], peer_g[:, tt, :], ALU.mult))

            def weighted(tt, pair):
                h0 = (2 * tt + 1) * HEADS + PAIR * pair
                first = h0 * TOPK
                with dve.Fori(0, PAIR) as i:
                    dve.wait_ge(row_used, i * TOPK + (first + GATHER_SLOTS))
                    dve.tensor_copy(st_h[:], peer_h[:, tt, bass.ds(i * TOPK + PAIR * pair * TOPK, TOPK)]
                                    ).then_inc(head_kept, 1)
                    dve.wait_ge(head_kept, i + (h0 + 1))
                    for k in range(TOPK):
                        dve.wait_ge(row_in[k % GATHER_SLOTS], arrivals(i, first, k))
                        if k >= 2:
                            dve.wait_ge(row_used, i * TOPK + (first + k - 1 + GATHER_SLOTS))
                        to = (xres[:, tt, :], odd[tt])[k % 2]
                        dve.scalar_tensor_tensor(to, gat[k % GATHER_SLOTS], st_h[:, k:k + 1], to,
                                                 ALU.mult, ALU.add).then_inc(row_used, 1)

            def select(tt, pair):
                select_keys(tt, pair)
                select_experts(tt, pair)

            select(0, 0)
            select(0, 1)
            dots(0, 0)
            select(0, 2)
            dots(0, 1)
            select(0, 3)
            dots(0, 2)
            select(1, 0)
            dots(0, 3)
            dve.sem_inc(dots_done, 1)
            weights(0)
            for pair in range(HEADS // PAIR):
                weighted(0, pair)
                if pair < 3:
                    select(1, 1 + pair)
            dve.wait_ge(mcol_out, 16)
            for i, name in ((0, "norm1_g"), (1, "norm2_g")):
                at, n = COLS[name]
                dve.scalar_tensor_tensor(evcols[:, i, :], modcols[:, 2 * i + 1, :], 1.0, cols[:, at:at + n],
                                         ALU.add, ALU.mult).then_inc(ev_ready, 1)

            def finish(tt):
                dve.wait_ge(row_used, (2 * tt + 2) * HK + GATHER_SLOTS)
                ordered(dve.tensor_tensor(xres[:, tt, :], xres[:, tt, :], odd[tt], ALU.add))
                norm(tt, xn3[tt], xres[:, tt, :])
                dve.wait_ge(loaded_rows, 48)
                ordered(scaled(tt, xres[:, tt, :], xres[:, tt, :]))
                ordered(dve.tensor_tensor(xres[:, tt, :], xres[:, tt, :], gfin, ALU.mult))
                norm(tt, xn3[tt], xres[:, tt, :])
                scaled(tt, xn3[tt], xres[:, tt, :]).then_inc(xn_ready[2], 1)

            dve.wait_ge(ada_out, N_ADA)
            finish(0)
            for pair in range(HEADS // PAIR):
                dots(1, pair)
            dve.sem_inc(dots_done, 1)
            weights(1)
            for pair in range(HEADS // PAIR):
                weighted(1, pair)
            finish(1)
            ordered(dve.memset(pt[:, :, 0:1], 0.0))
            dve.wait_ge(proj_out, 4)
            dve.tensor_tensor(msq, mqk, mqk, ALU.mult).then_inc(msq_ready, 1)
            ordered(dve.memset(restart, 1.0))
            ordered(dve.memset(restart[:, 0:T:CL], 0.0))
            for i, name in ((0, "q_g"), (1, "k_g")):
                dve.wait_ge(m_norm, 5 + i)
                dve.scalar_tensor_tensor(mqk[:, 4 * i:4 * i + 4, :], mqk[:, 4 * i:4 * i + 4, :], col(name),
                                         mrs[:, 4 * i:4 * i + 4, :], ALU.mult, ALU.mult).then_inc(mqk_ready, 1)
            dve.wait_ge(bias_made, 2 * NH)
            for tt, sc in ((0, sc0), (1, sc1)):
                hb = 4 // (tt + 1)
                for b in range(2 * (tt + 1)):
                    dve.wait_ge(sc_mm, 2 * tt + b + 1)
                    s3 = sc[:, hb * b:hb * b + hb, :]
                    src = psum[:, SC_BANK[2 * tt + b], :].rearrange("p (a t) -> p a t", a=hb)
                    dve.scalar_tensor_tensor(s3, src, float(HD) ** -0.5, s3, ALU.mult, ALU.add).then_inc(sc_read, 1)
                dve.wait_ge(sc_read, 2 * tt + 2 * (tt + 1))
                ordered(dve.tensor_reduce(mx[:, 0, :], sc, AX_X, ALU.max))
                dve.tensor_tensor(sc, sc, mx[:, 0, :].unsqueeze(2).to_broadcast([P, NH, (tt + 1) * P]),
                                  ALU.subtract).then_inc(mexp_in, 1)
            dve.wait_ge(mexp_in, TT)
            for tt, sc in ((0, sc0), (1, sc1)):
                dve.wait_ge(mexp_out, tt + 1)
                ordered(dve.tensor_reduce(mx[:, 0, :], sc, AX_X, ALU.add))
                ordered(dve.reciprocal(mx[:, 1, :], mx[:, 0, :]))
                dve.tensor_tensor(sc, sc, mx[:, 1, :].unsqueeze(2).to_broadcast([P, NH, (tt + 1) * P]),
                                  ALU.mult).then_inc(prob_ready, 1)
                dve.wait_ge(prob_ready, tt + 1)
            dve.wait_ge(ym_ready, TT)
            dve.wait_ge(proj_out, N_PROJ)

            def differences(a, b):
                return dve.tensor_tensor(ps[:, a:b, :], pt[:, a:b, 0:T], pt[:, a:b, 1:], ALU.subtract)

            def mixed(t):
                n = P if t < 14 else LAST
                at = COLS["mu"][0] + t
                return dve.scalar_tensor_tensor(ps[0:n, t, :], ps[0:n, t, :], cols[0:n, at:at + 1], pt[0:n, t, 1:],
                                                ALU.mult, ALU.add)

            differences(12, 14).then_inc(vec_step, 1)
            steps[0] += 1
            ordered(dve.tensor_tensor(ps[0:LAST, 14, :], pt[0:LAST, 14, 0:T], pt[0:LAST, 14, 1:], ALU.subtract))
            for t in (12, 13):
                mixed(t)
            mixed(14).then_inc(ps_ready, 1)
            ordered(differences(4, 8))
            for t in range(4, 7):
                mixed(t)
            ordered(mixed(7))
            for c in range(4):
                dve.tensor_scalar(kk[:, c, :], k_[:, c, :], col("k_k", c), None, ALU.mult).then_inc(vec_step, 1)
            steps[0] += 4
            dve.wait_ge(vec_step, steps[0])
            dve.tensor_tensor(t1, kk, kk, ALU.mult).then_inc(ksq_ready, 1)
            differences(0, 4).then_inc(vec_step, 1)
            steps[0] += 1
            ordered(differences(8, 12))
            for t in (0, 1, 2, 3, 8, 9, 10):
                mixed(t)
            ordered(mixed(11))
            dve.wait_ge(sig_out, 4)
            for c in range(4):
                dve.tensor_tensor_scan(pc[:, c, :], restart, wd[:, c, :], 0.0, ALU.mult, ALU.add).then_inc(vec_step, 1)
            steps[0] += 4
            dve.wait_ge(vec_step, steps[0])
            dve.tensor_tensor(wd, pc, wd, ALU.subtract).then_inc(log_ready, 1)
            for b in range(2):
                dve.wait_ge(ksum_mm, 1)
                dve.tensor_scalar(t1[:, 2 * b:2 * b + 2, :], psum[:, 6 + b, :].rearrange("p (a t) -> p a t", a=2),
                                  1e-24, None, ALU.max).then_inc(kn_in, 1)
            dve.wait_ge(sig_out, 8)
            for c in range(4):
                dve.tensor_scalar(t2[:, c, :], aa[:, c, :], -1.0, col("k_a", c), ALU.add, ALU.mult).then_inc(vec_step, 1)
            steps[0] += 4
            dve.wait_ge(vec_step, steps[0])
            ordered(dve.scalar_tensor_tensor(k_, t2, 1.0, k_, ALU.add, ALU.mult))
            for c in range(4):
                dve.scalar_tensor_tensor(t2[:, c, :], r_[:, c, :], col("r_k", c), k_[:, c, :],
                                         ALU.mult, ALU.mult).then_inc(rkk_ready, 1)
            dve.wait_ge(knorm_out, 2)
            ordered(dve.tensor_tensor(kk, kk, t1, ALU.mult))
            ordered(dve.tensor_tensor(aa, kk, aa, ALU.mult))
            dve.wait_ge(dec_out, 1)
            ordered(dve.tensor_tensor(kt_, k_, bt, ALU.mult))
            dve.tensor_tensor(bt, bt, aa, ALU.mult).then_inc(vec_step, 1)
            steps[0] += 1
            dve.wait_ge(dec_out, 3)
            dve.tensor_copy(pl, pc[:, :, CL - 1:T:CL]).then_inc(vec_step, 1)
            steps[0] += 1
            dve.scalar_tensor_tensor(ar[:, :, 0, :], kk, -1.0, wd, ALU.mult, ALU.mult).then_inc(vec_step, 1)
            steps[0] += 1
            ordered(dve.tensor_tensor(ar[:, :, 1, :], r_, pc, ALU.mult))
            dve.wait_ge(bon_mm, 1)
            for b in range(2):
                dve.tensor_tensor(bon[:, 2 * b:2 * b + 2, :], psum[:, b, :].rearrange("p (a t) -> p a t", a=2),
                                  v_[:, 2 * b:2 * b + 2, :], ALU.mult).then_inc(tilde, 1)
            ordered(dve.memset(states[0], 0.0))

            def pair4(bank):
                return psum[:, bank, :].rearrange("p (a t) -> p a t", a=4)

            def tokens_kept(tt, i):
                dve.wait_ge(tok_mm, 4 * tt + i + 1)
                dve.tensor_copy(tok[:, i, :], psum[:, i, :]).then_inc(tok_ready, 1)

            def grams_masked(tt, c):
                for par in range(2):
                    h = 2 * c + par
                    dve.wait_ge(gram_mm, 8 * tt + h + 1)
                    g = psum[:, GRAM_BANK[c % 2][par], :].rearrange("p (a b t) -> p b a t", a=2, b=2)
                    m = [P, 2, P]
                    dve.tensor_tensor(nak[:, h, :, :], g[:, 0, :, :], mask_st[:, 0:1, :].to_broadcast(m),
                                      ALU.mult).then_inc(vec_step, 1)
                    steps[0] += 1
                    dve.tensor_tensor(rbk[:, h, :, :], g[:, 1, :, :], mask_st[:, 1:2, :].to_broadcast(m),
                                      ALU.mult).then_inc(gram_out, 1)

            tokens_kept(0, 1)
            tokens_kept(0, 3)
            for c in range(4):
                grams_masked(0, c)
            for tt in range(TT):
                dve.wait_ge(nt_mm, tt + 1)
                for par in range(2):
                    dve.tensor_tensor(nts[:, par:NH:2, :], pair4(2 + par), mask_ts[:].unsqueeze(1).to_broadcast([P, 4, P]),
                                      ALU.mult).then_inc(nt_out, 1)
                dve.wait_ge(vec_step, steps[0])
                dve.tensor_tensor(inv, nak[:, :, 0, :], ident[:].unsqueeze(1).to_broadcast([P, NH, P]),
                                  ALU.add).then_inc(nt_out, 1)
                for lv in range(1, 5):
                    for q in range(2):
                        if lv < 4:
                            dve.wait_ge(ps_mm, 6 * tt + 2 * (lv - 1) + q + 1)
                            dst = pw_s[:, 4 * q:4 * q + 4, :] if lv % 2 else nak[:, 4 * q:4 * q + 4, 0, :]
                            dve.tensor_copy(dst, pair4(q)).then_inc(ps_out, 1)
                    for q in range(2):
                        dve.wait_ge(ix_mm, 8 * tt + 2 * (lv - 1) + q + 1)
                        iv = inv[:, 4 * q:4 * q + 4, :]
                        dve.tensor_tensor(iv, iv, pair4(4 + q), ALU.add).then_inc(ix_out, 1)
                dve.wait_ge(wu_mm, 3 * tt + 1)
                dve.tensor_copy(z2, psum[:, 6, :].rearrange("p (h c) -> p h c", h=NH)).then_inc(wu_out, 1)
                for q in range(2):
                    dve.wait_ge(wu_mm, 3 * tt + q + 2)
                    dve.tensor_copy(nak[:, 4 * q:4 * q + 4, 1, :], pair4((7, 0)[q])).then_inc(wu_out, 1)
                dve.wait_ge(q2_mm, tt + 1)
                dve.tensor_tensor(qt, pair4(0), ar[:, :, 1, tt * P:(tt + 1) * P], ALU.add).then_inc(q2_out, 1)
                ordered(dve.memset(phi, 0.0))
                for c in range(P // CL):
                    dve.wait_ge(fg_mm, 4 * tt + c + 1)
                    f4 = psum[:, 2 + c, 0:T].rearrange("p (a j) -> p a j", a=4)
                    for par in range(2):
                        a, b = HD * par, HD * par + HD
                        dve.tensor_tensor(phi[a:b, c, :, a:b], f4[a:b], ident[a:b, a:b].unsqueeze(1).to_broadcast([HD, 4, HD]),
                                          ALU.add).then_inc(vec_step, 1)
                        steps[0] += 1
                    dve.tensor_copy(gam[:, c, :, :],
                                    psum[:, 2 + c, T:2 * T].rearrange("p (a j) -> p a j", a=4)).then_inc(fg_out, 1)
                for c in range(P // CL):
                    g = tt * (P // CL) + c
                    if g == NC - 1:
                        break
                    nx = states[(g + 1) % 5]
                    dve.wait_ge(st_mm, g + 1)
                    dve.wait_ge(fg_out, 4 * tt + 4)
                    ordered(dve.tensor_tensor(nx, psum[:, 6 + g % 2, 0:T].rearrange("p (a i) -> p a i", a=4),
                                              gam[:, c, :, :], ALU.add))
                    dve.tensor_tensor(nx, nx, pl[:, :, g:g + 1].to_broadcast([P, 4, HD]), ALU.mult).then_inc(st_out, 1)
                    if tt == 0 and c < 2:
                        tokens_kept(1, (1, 3)[c])
                    elif tt == 0:
                        grams_masked(1, c - 2)
                dve.wait_ge(yp_out, tt + 1)
                for par in range(2):
                    dve.wait_ge(ys_mm, 2 * tt + par + 1)
                    a, b = HD * par, HD * par + HD
                    yv = yT[a:b, :, tt * P:(tt + 1) * P]
                    dve.tensor_tensor(yv, yv, pair4(6 + par)[a:b], ALU.add).then_inc(ys_out, 1)
                if tt == 0:
                    grams_masked(1, 2)
                    grams_masked(1, 3)
            dve.wait_ge(ys_out, 4)
            for b in range(2):
                dve.wait_ge(ln_mm, b + 1)
                s2 = slice(2 * b, 2 * b + 2)
                dve.scalar_tensor_tensor(dn[:, s2, :], psum[:, b, :].rearrange("p (a t) -> p a t", a=2), -1.0 / HD,
                                         yT[:, s2, :], ALU.mult, ALU.add).then_inc(vec_step, 1)
            steps[0] += 2
            dve.wait_ge(vec_step, steps[0])
            dve.tensor_tensor(dsq, dn, dn, ALU.mult).then_inc(ln_sq, 1)
            dve.wait_ge(ln_norm, 3)
            ordered(dve.tensor_tensor(dn, dn, drs, ALU.mult))
            for c in range(4):
                dve.tensor_scalar(dn[:, c, :], dn[:, c, :], col("ln_g", c), col("ln_b", c), ALU.mult,
                                  ALU.add).then_inc(vec_step, 1)
            steps[0] += 4
            dve.wait_ge(vec_step, steps[0])
            ordered(dve.tensor_tensor(dn, dn, bon, ALU.add))
            dve.tensor_tensor(yT, dn, gg, ALU.mult).then_inc(y_done, 1)
            for tt in range(TT):
                for m in range(N_O2 // 2):
                    if tt == 0:
                        dve.wait_ge(part_mm, 2 + HP // 4 + N_EARLY + m + 1)
                    else:
                        dve.wait_ge(chunk_done, C_O2 + 2 * m + 2)
                    cs = slice(2 * m * CW, 2 * (m + 1) * CW)
                    ordered(dve.tensor_tensor(ga_t, psum[:, 4 + 2 * tt + m, :], gates[:, 0, cs], ALU.mult))
                    ordered(dve.tensor_tensor(xres[:, tt, cs], xres[:, tt, cs], ga_t, ALU.add))
                norm(tt, xn4[:, tt, :], xres[:, tt, :])
                scaled(tt, xn4[:, tt, :], xres[:, tt, :]).then_inc(xn_ready[3], 1)
            dve.wait_ge(router_mm, 1)
            sh = [P, TT, NE]
            ordered(dve.tensor_tensor(lg, psum[:, 5, 0:TT * NE].rearrange("p (a e) -> p a e", a=TT),
                                      brow_r[:].unsqueeze(1).to_broadcast(sh), ALU.add))
            for tt in range(TT):
                ordered(dve.max(top8[:, tt, :], lg[:, tt, :]))
                ordered(dve.max_index(top8i[:, tt, :], top8[:, tt, :], lg[:, tt, :]))
            ordered(dve.tensor_copy(top8f, top8i))
            dve.tensor_tensor(w4, top8[:, :, 0:TOPE], top8[:, :, 0:1].to_broadcast([P, TT, TOPE]),
                              ALU.subtract).then_inc(wexp_in, 1)

            def picked(k):
                return dve.tensor_tensor(eqe, top8f[:, :, k:k + 1].to_broadcast(sh),
                                         iota_e[:].unsqueeze(1).to_broadcast(sh), ALU.is_equal)

            ordered(dve.memset(picks, 0.0))
            for k in range(TOPE):
                ordered(picked(k))
                ordered(dve.tensor_tensor(picks, picks, eqe, ALU.add))
            dve.sem_inc(picks_ready, 1)
            dve.wait_ge(router_mm, 2)
            ordered(dve.memset(rank, -1.0))
            ordered(dve.scalar_tensor_tensor(rank[:, :, 0:NE], psum[:, 6, 0:TT * NE].rearrange("p (a e) -> p a e", a=TT),
                                             1.0, picks, ALU.add, ALU.mult))
            dve.tensor_scalar(rank[:, :, 0:NE], rank[:, :, 0:NE], -1.0, None, ALU.add).then_inc(rk_made, 1)
            ordered(dve.tensor_reduce(most, psum[:, 6, TT * NE:TT * NE + NE], AX_X, ALU.max))
            dve.tensor_copy(most_i, most).then_inc(count_ready, 1)

            def router_weights():
                dve.wait_ge(wexp_out, 1)
                ordered(dve.tensor_reduce(wsum[:, 0, :], w4, AX_X, ALU.add))
                ordered(dve.reciprocal(wsum[:, 1, :], wsum[:, 0, :]))
                ordered(dve.tensor_tensor(w4, w4, wsum[:, 1, :].unsqueeze(2).to_broadcast([P, TT, TOPE]), ALU.mult))
                ordered(dve.memset(wts, 0.0))
                for k in range(TOPE):
                    ordered(picked(k))
                    ordered(dve.tensor_tensor(eqe, eqe, w4[:, :, k:k + 1].to_broadcast(sh), ALU.mult))
                    ordered(dve.tensor_tensor(wts, wts, eqe, ALU.add))
                dve.wait_ge(consts, 2)

            def front_in(f, e):
                dve.wait_ge(g_mm, f + 1)
                for tt in range(TT):
                    ins = dve.tensor_scalar(oh[:, tt, :], iota_slot[:, 0:CAP], rank[:, tt, bass.ds(e, 1)], None, ALU.is_equal)
                ins.then_inc(oh_ready, 1)

            def bias_rows(e):
                dve.tensor_scalar(sel_e[0:2 * NE], half_e[0:2 * NE, :], iota_e2[0:2 * NE, bass.ds(e, 1)], None,
                                  ALU.is_equal).then_inc(sel_ready, 1)

            def front_out(f):
                dve.wait_ge(xt_mm, f + 1)
                sh4 = [P, 4, 2, CAP]
                x4 = xT.rearrange("p j (h s) -> p j h s", h=2)
                src = psum[:, 3, :].rearrange("p (j h s) -> p j h s", j=4, h=2)
                sc_ = evcols[:, 1, :].rearrange("p (h j) -> p j h", h=2).unsqueeze(3).to_broadcast(sh4)
                sf_ = modcols[:, 2, :].rearrange("p (h j) -> p j h", h=2).unsqueeze(3).to_broadcast(sh4)
                dve.tensor_tensor(x4, src, sc_, ALU.mult).then_inc(xt_scaled, 1)
                dve.wait_ge(xt_scaled, f + 1)
                dve.tensor_tensor(x4, x4, sf_, ALU.add).then_inc(xT_ready, 1)

            def experts(p):
                dve.wait_ge(rk_made, p + 1)
                f0 = p * (NE + 1)
                front_in(f0, 0)
                bias_rows(0)
                front_out(f0)
                if isinstance(p, int):
                    router_weights()
                with dve.Fori(0, NE) as e:
                    it = p * NE + e
                    f = p * (NE + 1) + e
                    front_in(f + 1, e + 1)
                    dve.wait_ge(sct_mm, it + 1)
                    for tt in range(TT):
                        ins = dve.tensor_scalar(ohw[:, tt, :], iota_slot[:], rank[:, tt, bass.ds(e, 1)],
                                                wts[:, tt, bass.ds(e, 1)], ALU.is_equal, ALU.mult)
                    ins.then_inc(ohw_ready, 1)
                    dve.wait_ge(gu_mm, it + 1)
                    dve.tensor_scalar(ag, psum[:, 0, :], LIMIT, None, ALU.min).then_inc(gate_ready, 1)
                    dve.tensor_scalar(au, psum[:, 1, :], LIMIT, -LIMIT, ALU.min, ALU.max).then_inc(gu_read, 1)
                    bias_rows(e + 1)
                    dve.wait_ge(gu_read, it + 2)
                    dve.scalar_tensor_tensor(au, au, 1.0, ag, ALU.add, ALU.mult).then_inc(up_ready, 1)
                    dve.wait_ge(up_ready, it + 1)
                    dve.wait_ge(sg_ready, it + 1)
                    dve.tensor_tensor(ag, au, sg, ALU.mult).then_inc(act_ready, 1)
                    front_out(f + 1)
                    for tt in range(TT):
                        dve.wait_ge(sum_mm, it * TT + (tt + 1))
                        dve.tensor_tensor(acc[:, tt, :], acc[:, tt, :],
                                          psum[:, (6, 3)[tt]:(8, 5)[tt], :].rearrange("p a c -> p (a c)"),
                                          ALU.add).then_inc(acc_done, 1)
                dve.wait_ge(acc_done, (p + 1) * (NE * TT) + 1)
                dve.tensor_scalar(rank, rank, -float(CAP), None, ALU.add).then_inc(rk_made, 1)

            experts(0)
            further_passes(dve, experts)
            for tt in range(TT):
                ordered(dve.tensor_tensor(acc[:, tt, :], acc[:, tt, :], gates[:, 1, :], ALU.mult))
                dve.tensor_tensor(xres[:, tt, :], xres[:, tt, :], acc[:, tt, :], ALU.add).then_inc(out_ready, 1)

        @block.tensor
        def _(pe):
            def turn(n, src):
                pe.wait_ge(xn_ready[n], TT)
                for k in range(KD):
                    if k >= 4:
                        pe.wait_ge(hT_ready[n], k - 3)
                    for tt in range(TT):
                        last = pe.transpose(psum[:, k % 4, tt * P:(tt + 1) * P], src[:, tt, k * P:(k + 1) * P], ident[:])
                    last.then_inc(turned[n], 1)

            def turn_tile(n, src, tt, banks):
                pe.wait_ge(xn_ready[n], tt + 1)
                for k in range(KD):
                    last = pe.transpose(psum[:, banks[k // 4], (k % 4) * P:(k % 4 + 1) * P], src[:, k * P:(k + 1) * P],
                                        ident[:])
                    if k % 4 == 3:
                        last.then_inc(turned[n], 1)

            def chunk(n):
                pe.wait_ge(landed[n % SLOTS], uses(n))

            def channels(n, acts, bank, width=2):
                chunk(n)
                for c in range(width):
                    for k in range(KD):
                        last = pe.matmul(psum[:, bank, c * T:(c + 1) * T], wide(n)[:, k, c * P:(c + 1) * P],
                                         acts[:, k, :], start=(k == 0), stop=(k == KD - 1))
                return last

            pe.sem_inc(g_mm, 1)
            pe.sem_inc(sct_mm, 1)
            pe.wait_ge(consts, 1)
            turn(0, xn)
            pe.wait_ge(hT_ready[0], KD)
            for n in range(N_Z):
                if n >= 4:
                    pe.wait_ge(z_out, n - 3)
                channels(C_Z + n, hT, 2 + n % 4).then_inc(chunk_done, 1)
            pe.wait_ge(p_ready, 1)
            pe.wait_ge(loaded_p, 32)
            for g in range(POOL_G):
                last = pe.matmul(psum[:, 6 + g // 2, (g % 2) * T:(g % 2) * T + T],
                                 mats[:, M_GROUP + g * P:M_GROUP + (g + 1) * P], pT[:, g, :], start=True, stop=True)
            last.then_inc(group_mm, 1)
            pe.wait_ge(a_ready, POOL_G)
            pe.wait_ge(c_ready, 1)
            for k in range(KD):
                pair = k // 4
                if k % 4 == 0:
                    chunk(C_BR + 2 * pair)
                    chunk(C_BR + 2 * pair + 1)
                if k >= 4:
                    pe.wait_ge(m_ready, k - 3)
                elif k == 0:
                    pe.wait_ge(z_out, N_Z)
                for b, act_in in ((0, aT), (1, cT)):
                    w = slot(C_BR + 2 * pair + b).rearrange("p (k c) -> p k c", k=4)
                    for q in range(4):
                        last = pe.matmul(psum[:, 2 + k % 4, b * T:(b + 1) * T], w[:, q, (k % 4) * P:(k % 4 + 1) * P],
                                         act_in[:, q, :], start=(q == 0), stop=(q == 3))
                        if k == 4 and b == 0 and q == 0:
                            last.then_inc(chunk_done, 1)
                    if k % 4 == 3 and b == 0:
                        last.then_inc(chunk_done, 1)
                last.then_inc(br_mm, 1)
            pe.wait_ge(m_ready, KD)
            for tt in range(TT):
                for n in range(N_O1):
                    if tt == 0:
                        chunk(C_O1 + n)
                    for k in range(KD):
                        last = pe.matmul(psum[:, 2 + 2 * tt + n // 2, (n % 2) * CW:(n % 2 + 1) * CW],
                                         mT[:, k, tt * P:(tt + 1) * P], wide(C_O1 + n)[:, k, :],
                                         start=(k == 0), stop=(k == KD - 1))
                        if tt == 0 and n == 0 and k == 0:
                            last.then_inc(chunk_done, 1)
                    if tt:
                        last.then_inc(chunk_done, 1)
                    elif n % 2:
                        last.then_inc(part_mm, 1)
            turn_tile(1, h2[:, 0, :], 0, (0, 1))
            pe.wait_ge(hT_ready[1], KD)
            pe.wait_ge(x_mid, N_O1)
            def pair_scores(n):
                tt, m = n // 4, n % 4
                chunk(C_KEYS)
                pe.wait_ge(part_out, n + 1)
                if tt:
                    pe.wait_ge(s_out, m + 1)
                elif m == 2:
                    pe.wait_ge(hT_ready[1], 2 * KD)
                for i in range(4):
                    hp = 4 * m + i
                    last = pe.matmul(psum[:, S_BANK[m], i * NK:(i + 1) * NK], qT[:, m, i, :],
                                     slot(C_KEYS)[:, hp * NK:(hp + 1) * NK], start=True, stop=True)
                last.then_inc(s_mm, 1)

            for n in range(TT * HEADS // PAIR):
                tt, m = n // 4, n % 4
                if tt:
                    pe.wait_ge(part_out, m + 1)
                    pe.wait_ge(hT_ready[1], 2 * KD)
                for j in range(2):
                    if tt == 0:
                        chunk(C_Q + 2 * m + j)
                    for c in range(2):
                        at = (2 * j + c) * P
                        for k in range(KD):
                            last = pe.matmul(psum[:, 2 + m, at:at + P], wide(C_Q + 2 * m + j)[:, k, c * P:(c + 1) * P],
                                             h2T[:, k, tt * P:(tt + 1) * P], start=(k == 0), stop=(k == KD - 1))
                    if tt:
                        last.then_inc(chunk_done, 1)
                    elif j:
                        last.then_inc(part_mm, 1)
                if n == 0:
                    turn_tile(1, h2[:, 1, :], 1, (6, 7))
                    pair_scores(0)
                elif n > 1:
                    pair_scores(n - 1)
            pair_scores(TT * HEADS // PAIR - 1)
            pe.wait_ge(cb_ready, KD)
            pe.wait_ge(loaded_rows, 32)
            pe.wait_ge(s_out, TT * HP // 4)
            m = 0
            for n in range(N_ADA):
                chunk(C_ADA + n)
                if MOD_HEADS[n]:
                    pe.wait_ge(head_kept, MOD_HEADS[n])
                if n >= 2:
                    pe.wait_ge(ada_out, n - 1)
                for k in range(KD):
                    first = pe.matmul(psum[:, 4 + n % 2, 0:CW], cb[:, k, :], wide(C_ADA + n)[:, k, :],
                                      start=(k == 0), stop=False)
                    if n == 0 and k == 0:
                        first.then_inc(chunk_done, 1)
                r = 32 * (n // 6)
                last = pe.matmul(psum[:, 4 + n % 2, 0:CW], ones[r:r + 1, :], brow[r:r + 1, (n % 6) * CW:(n % 6 + 1) * CW],
                                 start=False, stop=True)
                last.then_inc(chunk_done, 1)
                if n // 4 not in (2, 5):
                    pe.wait_ge(ada_out, n + 1)
                    if m:
                        pe.wait_ge(mcol_out, m)
                    for i in range(2):
                        last = pe.matmul(psum[:, 6, i:i + 1], mrow[0:1, n % 2, i * P:(i + 1) * P], ones[0:1, 0:1],
                                         start=True, stop=True)
                    last.then_inc(mcol_mm, 1)
                    m += 1
            def project(n, tt=None):
                a, b = (0, T) if tt is None else (tt * P, (tt + 1) * P)
                bank, w = 2 + n % 4, wide(C_MB + n)
                if 4 <= n < N_MB:
                    for k in range(KD):
                        last = pe.matmul(psum[:, bank, 0:CW], hT3[:, k, a:b], w[:, k, :],
                                         start=(k == 0), stop=(k == KD - 1))
                elif n < N_PROJ - 1:
                    for c in range(2):
                        for k in range(KD):
                            last = pe.matmul(psum[:, bank, c * (b - a):(c + 1) * (b - a)], w[:, k, c * P:(c + 1) * P],
                                             hT3[:, k, a:b], start=(k == 0), stop=(k == KD - 1))
                else:
                    w = slot(C_MB + n)[:, 0:KD * LAST].rearrange("p (k c) -> p k c", k=KD)
                    for k in range(KD):
                        last = pe.matmul(psum[0:LAST, bank, 0:b - a], w[:, k, :], hT3[:, k, a:b],
                                         start=(k == 0), stop=(k == KD - 1))
                return last

            turn_tile(2, xn3[0], 0, (0, 1))
            pe.wait_ge(hT_ready[2], KD)
            for n in range(N_EARLY):
                chunk(C_MB + n)
                if n >= 4:
                    pe.wait_ge(part_out, TT * HP // 4 + n - 3)
                project(n, 0).then_inc(part_mm, 1)
            turn_tile(2, xn3[1], 1, (6, 7))
            pe.wait_ge(hT_ready[2], 2 * KD)
            pe.wait_ge(part_out, TT * HP // 4 + N_EARLY)

            def late(n):
                chunk(C_MB + n)
                if n >= 4:
                    pe.wait_ge(proj_out, n - 3)
                project(n, 1 if n < N_EARLY else None).then_inc(chunk_done, 1)

            def scores(j):
                tt = 0 if j < 2 else 1
                b = j - 2 * tt
                nk = (tt + 1) * P
                hb = 4 // (tt + 1)
                rows = slice(HD * (b // (tt + 1)), HD * (b // (tt + 1)) + HD)
                if j >= 4:
                    pe.wait_ge(sc_read, j - 3)
                for i in range(hb):
                    c = (hb * b + i) % 4
                    last = pe.matmul(psum[:, SC_BANK[j], i * nk:(i + 1) * nk], mqk[rows, c, tt * P:(tt + 1) * P],
                                     mqk[rows, 4 + c, 0:nk], start=True, stop=True)
                last.then_inc(sc_mm, 1)

            def turn_weights(j):
                tt, sc = (0, sc0) if j < 2 else (1, sc1)
                b = j - 2 * tt
                hb = 4 // (tt + 1)
                pe.wait_ge(prob_ready, tt + 1)
                pe.wait_ge(sc_read, 6)
                if j >= 3:
                    pe.wait_ge(prT_ready, j - 2)
                for i in range(hb):
                    for kt in range(tt + 1):
                        at = (i * (tt + 1) + kt) * P
                        last = pe.transpose(psum[:, PR_BANK[j], at:at + P], sc[:, hb * b + i, kt * P:(kt + 1) * P], ident[:])
                last.then_inc(pr_mm, 1)

            def attend(tt):
                pe.wait_ge(prT_ready, (2, 6)[tt])
                if tt:
                    pe.wait_ge(ym_ready, 1)
                for par in range(2):
                    for c in range(4):
                        for kt in range(tt + 1):
                            h = 2 * c + par
                            last = pe.matmul(psum[HD * par:HD * par + HD, 6, c * P:(c + 1) * P],
                                             mv[:, kt, h * HD:(h + 1) * HD], prT[:, 4 * par + c, kt, :],
                                             start=(kt == 0), stop=(kt == tt))
                last.then_inc(pv_mm, 1)

            for n in range(5):
                late(n)
            pe.wait_ge(msq_ready, 1)
            for b in range(4):
                pe.matmul(psum[:, (6, 7, 0, 1)[b], :], headblk[:], msq[:, 2 * b:2 * b + 2, :].rearrange("p a t -> p (a t)"),
                          start=True, stop=True).then_inc(msum_mm, 1)
            late(5)
            late(N_MB + 0)
            pe.wait_ge(mqk_ready, 2)
            pe.wait_ge(m_norm, 4)
            for j in range(4):
                scores(j)
            late(N_MB + 1)
            scores(4)
            scores(5)
            late(N_MB + 2)
            turn_weights(0)
            turn_weights(1)
            late(N_MB + 3)
            attend(0)
            for j in range(2, 5):
                turn_weights(j)
            late(N_MB + 4)
            turn_weights(5)
            late(N_MB + 5)
            attend(1)
            late(N_MB + 6)
            late(N_MB + 7)
            pe.wait_ge(lora_in, 3)
            pe.wait_ge(ym_ready, TT)
            for i, rows in ((0, slice(0, 64)), (1, slice(64, 128))):
                for c in range(4):
                    last = pe.matmul(psum[:, 2 * i + c // 2, (c % 2) * T:(c % 2) * T + T],
                                     mats[rows, M_LORA + c * P:M_LORA + (c + 1) * P], ps[rows, 12, :],
                                     start=True, stop=True)
                last.then_inc(lora_mm, 1)
            pe.wait_ge(ksq_ready, 1)
            for b in range(2):
                last = pe.matmul(psum[:, 6 + b, :], headblk[:], t1[:, 2 * b:2 * b + 2, :].rearrange("p a t -> p (a t)"),
                                 start=True, stop=True)
            last.then_inc(ksum_mm, 1)
            for c in range(4):
                o = psum[:, 4 + c // 2, (c % 2) * T:(c % 2) * T + T]
                pe.matmul(o, mats[:, M_GUP + c * P:M_GUP + (c + 1) * P], ps[:, 13, :], start=True, stop=False)
                last = pe.matmul(o, mats[0:LAST, M_GUP + W2 + c * P:M_GUP + W2 + (c + 1) * P], ps[0:LAST, 14, :],
                                 start=False, stop=True)
            last.then_inc(lora_mm, 1)
            pe.wait_ge(rkk_ready, 4)
            pe.wait_ge(sig_out, 4)
            for b in range(2):
                last = pe.matmul(psum[:, b, :], headblk[:], t2[:, 2 * b:2 * b + 2, :].rearrange("p a t -> p (a t)"),
                                 start=True, stop=True)
            last.then_inc(bon_mm, 1)
            pe.wait_ge(tilde, 2)
            pe.wait_ge(sig_out, 10)
            def turn_tokens(tt, i):
                src = (ar[:, :, 0, :], bt, kt_, v_)[i]
                for c in range(4):
                    last = pe.transpose(psum[:, i, c * P:(c + 1) * P], src[:, c, tt * P:(tt + 1) * P], ident[:])
                last.then_inc(tok_mm, 1)

            def grams(tt, c):
                ts = slice(tt * P, (tt + 1) * P)
                if c == 1:
                    pe.wait_ge(tok_ready, 4 * tt + 4)
                for par in range(2):
                    h = 2 * c + par
                    rows = slice(HD * par, HD * par + HD)
                    if c >= 2:
                        pe.wait_ge(gram_out, 8 * tt + h - 3)
                    for i, src in enumerate((bt, kt_)):
                        last = pe.matmul(psum[:, GRAM_BANK[c % 2][par], i * 2 * P:(i + 1) * 2 * P], src[rows, c, ts],
                                         ar[rows, c, :, ts], start=True, stop=True)
                    last.then_inc(gram_mm, 1)

            for i in range(4):
                turn_tokens(0, i)
            for c in range(4):
                grams(0, c)
            for tt in range(TT):
                ts = slice(tt * P, (tt + 1) * P)
                pe.wait_ge(tok_ready, 4 * tt + 4)
                for par in range(2):
                    rows = slice(HD * par, HD * par + HD)
                    for c in range(4):
                        last = pe.matmul(psum[:, 2 + par, c * P:(c + 1) * P], ar[rows, c, 0, ts], bt[rows, c, ts],
                                         start=True, stop=True)
                last.then_inc(nt_mm, 1)
                pe.wait_ge(nt_out, 3 * tt + 3)
                for lv in range(1, 5):
                    s_src = (lambda h: nak[:, h, 0, :]) if lv % 2 else (lambda h: pw_s[:, h, :])
                    t_src, t_dst = (nts, pw_t) if lv % 2 else (pw_t, nts)
                    if lv > 1:
                        pe.wait_ge(ps_out, 6 * tt + 2 * (lv - 1))
                        pe.wait_ge(pt_out, 8 * tt + 2 * (lv - 1))
                    for q in range(2):
                        hs = range(4 * q, 4 * q + 4)
                        for h in hs:
                            last = pe.matmul(psum[:, 2 + q, (h % 4) * P:(h % 4 + 1) * P], s_src(h), t_src[:, h, :],
                                             start=True, stop=True)
                        last.then_inc(pt_mm, 1)
                        if lv < 4:
                            for h in hs:
                                last = pe.matmul(psum[:, q, (h % 4) * P:(h % 4 + 1) * P], t_src[:, h, :], s_src(h),
                                                 start=True, stop=True)
                            last.then_inc(ps_mm, 1)
                    for q in range(2):
                        pe.wait_ge(pt_out, 8 * tt + 2 * (lv - 1) + q + 1)
                        if lv > 1:
                            pe.wait_ge(ix_out, 8 * tt + 2 * (lv - 2) + q + 1)
                        for h in range(4 * q, 4 * q + 4):
                            last = pe.matmul(psum[:, 4 + q, (h % 4) * P:(h % 4 + 1) * P], t_dst[:, h, :], inv[:, h, :],
                                             start=True, stop=True)
                        last.then_inc(ix_mm, 1)
                for h in range(NH):
                    last = pe.matmul(psum[:, 6, h * HD:(h + 1) * HD], nak[:, h, 1, :], tok[:, 3, h * HD:(h + 1) * HD],
                                     start=True, stop=True)
                last.then_inc(wu_mm, 1)
                pe.wait_ge(ix_out, 8 * tt + 8)
                pe.wait_ge(wu_out, 3 * tt + 1)
                for h in range(NH):
                    b = (7, 0)[h // 4]
                    at = (h % 4) * P
                    pe.matmul(psum[:, b, at:at + HD], inv[:, h, :], tok[:, 0, h * HD:(h + 1) * HD], start=True, stop=True)
                    last = pe.matmul(psum[:, b, at + HD:at + P], inv[:, h, :], z2[:, h, :], start=True, stop=True)
                    if h % 4 == 3:
                        last.then_inc(wu_mm, 1)
                pe.wait_ge(wu_out, 3 * tt + 3)
                for par in range(2):
                    for c in range(4):
                        h = 2 * c + par
                        last = pe.matmul(psum[HD * par:HD * par + HD, 0, c * P:(c + 1) * P], nak[:, h, 1, 0:HD],
                                         rbk[:, h, 0, :], start=True, stop=True)
                last.then_inc(q2_mm, 1)
                for par in range(2):
                    for c in range(4):
                        h = 2 * c + par
                        o = psum[HD * par:HD * par + HD, 1, c * P:(c + 1) * P]
                        pe.matmul(o, tok[:, 3, h * HD:(h + 1) * HD], rbk[:, h, 1, :], start=True, stop=False)
                        last = pe.matmul(o, nak[:, h, 1, HD:P], rbk[:, h, 0, :], start=False, stop=True)
                last.then_inc(yp_mm, 1)
                for ch in range(P // CL):
                    rows = slice(CL * ch, CL * ch + CL)
                    for par in range(2):
                        for c in range(4):
                            h = 2 * c + par
                            hs = slice(h * HD, (h + 1) * HD)
                            orow = slice(HD * par, HD * par + HD)
                            pe.matmul(psum[orow, 2 + ch, c * HD:(c + 1) * HD], nak[rows, h, 1, 0:HD], tok[rows, 1, hs],
                                      start=True, stop=True)
                            o = psum[orow, 2 + ch, T + c * HD:T + (c + 1) * HD]
                            pe.matmul(o, tok[rows, 1, hs], nak[rows, h, 1, HD:P], start=True, stop=False)
                            last = pe.matmul(o, tok[rows, 2, hs], tok[rows, 3, hs], start=False, stop=True)
                    last.then_inc(fg_mm, 1)
                for ch in range(P // CL):
                    g = tt * (P // CL) + ch
                    if g == NC - 1:
                        break
                    pe.wait_ge(fg_out, 4 * tt + ch + 1)
                    if g:
                        pe.wait_ge(st_out, g)
                    for c in range(4):
                        last = pe.matmul(psum[:, 6 + g % 2, c * HD:(c + 1) * HD], phi[:, ch, c, :], states[g % 5][:, c, :],
                                         start=True, stop=True)
                    last.then_inc(st_mm, 1)
                    if tt == 0:
                        if ch == 0:
                            pe.wait_ge(q2_out, 1)
                            pe.wait_ge(yp_out, 1)
                            pe.wait_ge(fg_out, 4)
                        if ch < 2:
                            turn_tokens(1, 2 * ch)
                            turn_tokens(1, 2 * ch + 1)
                        else:
                            grams(1, ch - 2)
                pe.wait_ge(q2_out, tt + 1)
                pe.wait_ge(fg_out, 4 * tt + 4)
                if tt:
                    pe.wait_ge(st_out, NC - 1)
                else:
                    pe.wait_ge(st_out, P // CL)
                for par in range(2):
                    rows = slice(HD * par, HD * par + HD)
                    for c in range(4):
                        for ch in range(P // CL):
                            g = tt * (P // CL) + ch
                            at = c * P + ch * CL
                            last = pe.matmul(psum[rows, 6 + par, at:at + CL], states[g % 5][rows, c, :],
                                             qt[rows, c, ch * CL:(ch + 1) * CL], start=True, stop=True)
                    last.then_inc(ys_mm, 1)
                if tt == 0:
                    grams(1, 2)
                    grams(1, 3)
            pe.wait_ge(ys_out, 4)
            for b in range(2):
                pe.matmul(psum[:, b, :], headblk[:], yT[:, 2 * b:2 * b + 2, :].rearrange("p a t -> p (a t)"),
                          start=True, stop=True).then_inc(ln_mm, 1)
            def out_half(tt, n, y, half):
                for k in range(4):
                    last = pe.matmul(psum[:, 4 + 2 * tt + n // 2, (n % 2) * CW:(n % 2 + 1) * CW],
                                     y[:, k, tt * P:(tt + 1) * P], wide(C_O2 + n)[:, 4 * half + k, :],
                                     start=(half == 1 and n % 2 == 0 and k == 0), stop=(half == 0 and k == 3),
                                     skip_group_check=True)
                return last

            for tt in range(TT):
                for n in range(N_O2):
                    chunk(C_O2 + n)
                    out_half(tt, n, ymT, 1)
                    if tt == 0 and n == 1:
                        pe.wait_ge(ln_sq, 1)
                        for b in range(2):
                            pe.matmul(psum[:, 2 + b, :], headblk[:],
                                      dsq[:, 2 * b:2 * b + 2, :].rearrange("p a t -> p (a t)"),
                                      start=True, stop=True).then_inc(ln_mm, 1)
            pe.wait_ge(y_done, 1)
            for n in range(N_O2):
                last = out_half(0, n, yT, 0)
                if n % 2:
                    last.then_inc(part_mm, 1)
            for n in range(N_O2):
                out_half(1, n, yT, 0).then_inc(chunk_done, 1)
            for tt in range(TT):
                turn_tile(3, xn4[:, tt, :], tt, (0, 1) if tt == 0 else (2, 3))
            pe.wait_ge(hT_ready[3], 2 * KD)
            for tt in range(TT):
                for k in range(KD):
                    last = pe.matmul(psum[:, 5, tt * NE:(tt + 1) * NE], hT4[:, k, tt * P:(tt + 1) * P],
                                     mats[:, M_ROUTER + k * NE:M_ROUTER + (k + 1) * NE],
                                     start=(k == 0), stop=(k == KD - 1))
            last.then_inc(router_mm, 1)
            pe.wait_ge(picks_ready, 1)
            pe.matmul(psum[:, 6, 0:NE], before[:], picks[:, 0, :], start=True, stop=True)
            pe.matmul(psum[:, 6, NE:2 * NE], ones[:], picks[:, 0, :], start=True, stop=False)
            pe.matmul(psum[:, 6, NE:2 * NE], before[:], picks[:, 1, :], start=False, stop=True)
            pe.matmul(psum[:, 6, 2 * NE:3 * NE], ones[:], picks[:, 0, :], start=True, stop=False)
            pe.matmul(psum[:, 6, 2 * NE:3 * NE], ones[:], picks[:, 1, :], start=False, stop=True).then_inc(router_mm, 1)
            pe.wait_ge(loaded_b, 16)
            pe.wait_ge(count_ready, 1)

            def front_gather(f):
                pe.wait_ge(oh_ready, f + 1)
                for tt in range(TT):
                    for h in range(2):
                        last = pe.matmul(psum[CAP * h:CAP * h + CAP, 2, :], oh[:, tt, :], xn4[:, tt, h * 512:(h + 1) * 512],
                                         start=(tt == 0), stop=(tt == TT - 1))
                last.then_inc(g_mm, 1)

            def front_turn(f):
                pe.wait_ge(xs_ready, f + 1)
                for j in range(4):
                    last = pe.transpose(psum[:, 3, j * P:(j + 1) * P], xs[:, j * P:(j + 1) * P], ident[:])
                last.then_inc(xt_mm, 1)

            def experts(p):
                f0 = p * (NE + 1)
                front_gather(f0)
                front_turn(f0)
                with pe.Fori(0, NE) as e:
                    it = p * NE + e
                    f = p * (NE + 1) + e

                    def moe_chunk(j):
                        n = C_MOE + j
                        pe.wait_ge(landed[n % SLOTS], it * 16 + uses(n))
                        return slot(n)

                    pe.wait_ge(xT_ready, f + 1)
                    pe.wait_ge(gu_read, it + 1)
                    for kt in range(GU_CHUNKS):
                        w = moe_chunk(kt)
                        x = xT[:, kt % 4, CAP * (kt // 4):CAP * (kt // 4) + CAP]
                        for gu in range(2):
                            for h in range(2):
                                at = gu * FF + h * 512
                                last = pe.matmul(psum[CAP * h:CAP * h + CAP, gu, :], x, w[:, at:at + 512],
                                                 start=(kt == 0), stop=False, skip_group_check=True)
                        last.then_inc(chunk_done, 1)
                    pe.wait_ge(sel_ready, f + 1)
                    for gu in range(2):
                        last = pe.matmul(psum[:, gu, :], sel_e[0:2 * NE], bmoe[0:2 * NE, gu, :], start=False, stop=True,
                                         skip_group_check=True)
                    pe.wait_ge(ye_ready, it + 1)
                    last = pe.matmul(psum[:, 5, :], sel_e[0:2 * NE], bmoe[0:2 * NE, 2, :], start=True, stop=False,
                                     skip_group_check=True)
                    last.then_inc(gu_mm, 1)
                    pe.wait_ge(sct_ready, it + 1)
                    front_gather(f + 1)
                    pe.wait_ge(act_ready, it + 1)
                    pe.wait_ge(acc_done, it * TT + 1)
                    for j in range(4):
                        last = pe.transpose(psum[:, 4, j * P:(j + 1) * P], ag[:, j * P:(j + 1) * P], ident[:])
                    last.then_inc(at_mm, 1)
                    front_turn(f + 1)
                    pe.wait_ge(ohw_ready, it + 1)
                    for tt in range(TT):
                        last = pe.transpose(psum[:, 2, tt * P:(tt + 1) * P], ohw[:, tt, :], ident[:])
                    last.then_inc(sct_mm, 1)
                    pe.wait_ge(actT_ready, it + 1)
                    for q in range(DN_CHUNKS):
                        w = moe_chunk(GU_CHUNKS + q)
                        for i in range(2):
                            kt = 2 * q + i
                            a_in = act_t[:, kt % 4, CAP * (kt // 4):CAP * (kt // 4) + CAP]
                            for h in range(2):
                                last = pe.matmul(psum[CAP * h:CAP * h + CAP, 5, :], a_in,
                                                 w[:, i * D + h * 512:i * D + h * 512 + 512],
                                                 start=False, stop=(kt == KD - 1), skip_group_check=True)
                        if q < DN_CHUNKS - 1:
                            last.then_inc(chunk_done, 1)
                    last.then_inc(y_mm, 1)
                    pe.wait_ge(sct_ready, it + 2)
                    pe.wait_ge(ye_ready, it + 2)
                    pe.wait_ge(xT_ready, f + 2)
                    for tt in range(TT):
                        for h in range(2):
                            rows = slice(CAP * h, CAP * h + CAP)
                            last = pe.matmul(psum[:, (6, 3)[tt] + h, :], sct[rows, tt, :], ye[rows, :],
                                             start=True, stop=True)
                            if tt == 0 and h == 0:
                                last.then_inc(chunk_done, 1)
                        last.then_inc(sum_mm, 1)

            experts(0)
            further_passes(pe, experts)


def kernel(**inputs):
    from concourse import bacc
    from concourse.bass_utils import run_bass_kernel_spmd

    a = {n: np.asarray(v) for n, v in inputs.items()}
    f = np.float32

    def chunks(w):
        n = w.shape[1] // CW
        return w.reshape(KD, P, n, CW).transpose(2, 1, 0, 3).reshape(n, P, CHUNK)

    def branch(w):
        return w.reshape(4, P, 2, 512).transpose(2, 1, 0, 3).reshape(2, P, CHUNK)

    pool_b, conv_b = branch(a["w_branch_pool"][0]), branch(a["w_branch_conv"][0])
    keys = a["sub_keys"][0].reshape(HP, NK, P).transpose(2, 0, 1).reshape(1, P, CHUNK)
    w2 = a["w_in_2"][0]
    whole = RW - LAST
    last = np.concatenate([w2[:, whole:RW].reshape(KD, P, LAST).transpose(1, 0, 2).reshape(P, KD * LAST),
                           np.zeros((P, CHUNK - KD * LAST), f)], axis=1)[None]
    w2 = np.concatenate([w2[:, RW:], w2[:, :whole]], axis=1)
    stream = np.concatenate([
        chunks(a["w_in"][0]), pool_b[0:1], conv_b[0:1], pool_b[1:2], conv_b[1:2], chunks(a["w_out"][0]),
        chunks(a["w_q"][0]), keys, chunks(a["w_ada_2"][0]), chunks(w2), last, chunks(a["w_out_2"][0])])

    def column(v, n):
        v = v.reshape(-1)
        return np.concatenate([v, np.zeros(n * P - v.size, f)]).reshape(n, P).T

    vectors = {
        "g_mix": a["g_mix"], "pool_scale": a["pool_scale"], "conv_w": a["conv_w"], "norm1_g": a["norm1_g_2"],
        "mu": a["rwkv_mu_2"], "w0": a["rwkv_w0_2"], "a0": a["rwkv_a0_2"], "k_k": a["rwkv_k_k_2"],
        "k_a": a["rwkv_k_a_2"], "r_k": a["rwkv_r_k_2"], "ln_g": a["rwkv_ln_g_2"], "ln_b": a["rwkv_ln_b_2"],
        "q_g": np.tile(a["q_norm_g_2"].reshape(-1), 2), "k_g": np.tile(a["k_norm_g_2"].reshape(-1), 2),
        "norm2_g": a["norm2_g_2"], "c": a["c_2"]}
    cols = np.concatenate([column(vectors[n], COLS[n][1]) for n in COLS], axis=1)
    group = a["pool_group_w"][0].transpose(1, 0, 2).reshape(P, 512)
    lora = np.concatenate([a["rwkv_w_up_2"][0], a["rwkv_a_up_2"][0]], axis=0)
    gup = np.concatenate([a["rwkv_g_up_2"][0], np.zeros((2 * P - 160, W2), f)]).reshape(2, P, W2)
    gup = gup.transpose(1, 0, 2).reshape(P, 2 * W2)
    router = a["w_router_2"][0].reshape(KD, P, NE).transpose(1, 0, 2).reshape(P, KD * NE)
    mats = np.concatenate([group, lora, gup, router], axis=1)
    rows = np.concatenate([a["g_ffn"].reshape(-1), a["g_final"].reshape(-1), a["b_router_2"].reshape(-1)])[None]
    bada = a["b_ada_2"].reshape(4, 6 * CW)
    bg = a["b_gate_up_2"][0].reshape(NE, 2, 2, 512).transpose(0, 2, 1, 3).reshape(2 * NE, D)
    bias_moe = np.concatenate([bg, a["b_down_2"][0].reshape(2 * NE, 512)], axis=1)
    arrays = {
        "x": a["x"][0], "stream": stream, "cols": cols, "mats": mats, "rows": rows, "bada": bada,
        "expert_u": a["expert_u"][0], "expert_v": a["expert_v"][0], "w_gate_up": a["w_gate_up_2"][0],
        "w_down": a["w_down_2"][0], "bias_moe": bias_moe}
    arrays = {n: np.ascontiguousarray(v) for n, v in arrays.items()}
    nc = bacc.Bacc("TRN2", target_bir_lowering=False, num_devices=1)
    args = [nc.dram_tensor("in_" + n, v.shape, mybir.dt.from_np(v.dtype), kind="ExternalInput").ap()
            for n, v in arrays.items()]
    out = nc.dram_tensor("out", (T, D), F32, kind="ExternalOutput").ap()
    build(nc, *args, out)
    r = run_bass_kernel_spmd(nc, [{"in_" + n: v for n, v in arrays.items()}], core_ids=[0])
    return r.results[0]["out"].reshape(1, T, D)
```
